# Optimizing a Trainium2 kernel written in Bass

```python
import math
import jax, jax.numpy as jnp
from jax import lax
import numpy as np

D_MODEL = 1024
BATCH = 1
SEQ = 1024
DEPTH = 2

GRID_W = 64
CTX_LEN = 256
Q_BLOCK = 128
ROPE_THETA = 10000.0
NORM_EPS = 1e-6

CONV_CH = 256
CONV_WIDTH = 3
MLA_HEADS = 4
MLA_Q_LORA = 256
MLA_KV_LORA = 128
MLA_NOPE = 64
MLA_ROPE = 32
MLA_V = 64
DIFF_HEADS = 4
DIFF_QK = 32
DIFF_V = 64
GQA_Q_HEADS = 4
GQA_KV_HEADS = 2
GQA_GROUP = GQA_Q_HEADS // GQA_KV_HEADS
GQA_HD = 64

IN_CONV = 3 * CONV_CH
IN_MLA = MLA_Q_LORA + MLA_KV_LORA + MLA_ROPE
DIFF_QW = DIFF_HEADS * 2 * DIFF_QK
IN_DIFF = 2 * DIFF_QW + DIFF_HEADS * DIFF_V
GQA_QW = GQA_Q_HEADS * GQA_HD
GQA_KW = GQA_KV_HEADS * GQA_HD
IN_GQA = GQA_QW + 2 * GQA_KW
D_IN = IN_CONV + IN_MLA + IN_DIFF + IN_GQA
IN_SPLITS = (IN_CONV, IN_CONV + IN_MLA, IN_CONV + IN_MLA + IN_DIFF)
D_MIX = CONV_CH + MLA_HEADS * MLA_V + DIFF_HEADS * DIFF_V + GQA_Q_HEADS * GQA_HD

MLA_SCALE = (MLA_NOPE + MLA_ROPE) ** -0.5
DIFF_SCALE = DIFF_QK ** -0.5
GQA_SCALE = GQA_HD ** -0.5

N_GROUPS = 4
EXPERTS_PER_GROUP = 8
N_EXPERTS = N_GROUPS * EXPERTS_PER_GROUP
TOP_K = 2
D_EXPERT = 256
EXPERT_BLOCK = 128

DEEPNORM_ALPHA = (2 * DEPTH) ** 0.25
DEEPNORM_BETA = (8 * DEPTH) ** -0.25
ADA_SCALE = 0.5

kernel_name = "hybrid_diffusion_trunk_mla_diff_gqa_conv_hmoe"

def rms_norm(z, gain):
    zf = z.astype(jnp.float32)
    zf = zf * lax.rsqrt(jnp.mean(zf * zf, axis=-1, keepdims=True) + NORM_EPS)
    return (zf * gain.astype(jnp.float32)).astype(z.dtype)

def layer_norm(z, gain, bias):
    zf = z.astype(jnp.float32)
    mu = jnp.mean(zf, axis=-1, keepdims=True)
    var = jnp.mean(jnp.square(zf - mu), axis=-1, keepdims=True)
    out = (zf - mu) * lax.rsqrt(var + NORM_EPS) * gain.astype(jnp.float32) + bias.astype(jnp.float32)
    return out.astype(z.dtype)

def rope_1d(z, pos):
    half = z.shape[-1] // 2
    freqs = ROPE_THETA ** (-jnp.arange(half, dtype=jnp.float32) / half)
    ang = pos.astype(jnp.float32)[:, None] * freqs
    shape = (ang.shape[0],) + (1,) * (z.ndim - 3) + (half,)
    cos = jnp.cos(ang).reshape(shape).astype(z.dtype)
    sin = jnp.sin(ang).reshape(shape).astype(z.dtype)
    z1, z2 = z[..., :half], z[..., half:]
    return jnp.concatenate([z1 * cos - z2 * sin, z2 * cos + z1 * sin], axis=-1)

def rope2d(z, row, col):
    h = z.shape[-1] // 2
    return jnp.concatenate([rope_1d(z[..., :h], row), rope_1d(z[..., h:], col)], axis=-1)

def softmax_f32(scores, scale):
    return jax.nn.softmax(scores.astype(jnp.float32) * scale, axis=-1)

def sweep_query_blocks(fn, q):
    b, s = q.shape[:2]
    nb = s // Q_BLOCK
    qb = jnp.moveaxis(q.reshape((b, nb, Q_BLOCK) + q.shape[2:]), 1, 0)
    out = lax.map(fn, qb)
    return jnp.moveaxis(out, 0, 1).reshape((b, s) + out.shape[3:])

def mha_core(q, k, v, scale):
    p = softmax_f32(jnp.einsum('bqhd,bthd->bhqt', q, k), scale)
    return jnp.einsum('bhqt,bthd->bqhd', p.astype(v.dtype), v)

def gqa_core(q, k, v, scale):
    p = softmax_f32(jnp.einsum('bqkgd,btkd->bkgqt', q, k), scale)
    return jnp.einsum('bkgqt,btkd->bqkgd', p.astype(v.dtype), v)

def diff_core(q, k, v, lam, scale):
    p = softmax_f32(jnp.einsum('bqhmd,bthmd->bhmqt', q, k), scale)
    a = p[:, :, 0] - lam * p[:, :, 1]
    return jnp.einsum('bhqt,bthd->bqhd', a.astype(v.dtype), v)

def conv_group(z, conv_w):
    gate_b, gate_c, val = jnp.split(z, 3, axis=-1)
    zc = gate_c * val
    conv = lax.conv_general_dilated(zc, conv_w[:, None, :], window_strides=(1,),
                                    padding=((CONV_WIDTH // 2, CONV_WIDTH // 2),),
                                    dimension_numbers=('NWC', 'WIO', 'NWC'),
                                    feature_group_count=CONV_CH)
    return gate_b * conv

def mla_queries(z, q_norm, w_uq, w_qr, pos):
    b, n = z.shape[:2]
    cq = rms_norm(z[..., :MLA_Q_LORA], q_norm)
    q_nope = (cq @ w_uq).reshape(b, n, MLA_HEADS, MLA_NOPE)
    q_rope = (cq @ w_qr).reshape(b, n, MLA_HEADS, MLA_ROPE)
    if pos is not None:
        q_rope = rope2d(q_rope, *pos)
    return jnp.concatenate([q_nope, q_rope], axis=-1)

def mla_keys_values(z, kv_norm, w_uk, w_uv, pos):
    b, n = z.shape[:2]
    ckv = rms_norm(z[..., MLA_Q_LORA:MLA_Q_LORA + MLA_KV_LORA], kv_norm)
    k_rope = z[..., MLA_Q_LORA + MLA_KV_LORA:][:, :, None, :]
    if pos is not None:
        k_rope = rope2d(k_rope, *pos)
    k_nope = (ckv @ w_uk).reshape(b, n, MLA_HEADS, MLA_NOPE)
    v = (ckv @ w_uv).reshape(b, n, MLA_HEADS, MLA_V)
    k = jnp.concatenate([k_nope, jnp.broadcast_to(k_rope, (b, n, MLA_HEADS, MLA_ROPE))], axis=-1)
    return k, v

def diff_queries(z, pos):
    b, n = z.shape[:2]
    q = z[..., :DIFF_QW].reshape(b, n, DIFF_HEADS, 2, DIFF_QK)
    return rope2d(q, *pos) if pos is not None else q

def diff_keys_values(z, pos):
    b, n = z.shape[:2]
    k = z[..., DIFF_QW:2 * DIFF_QW].reshape(b, n, DIFF_HEADS, 2, DIFF_QK)
    v = z[..., 2 * DIFF_QW:].reshape(b, n, DIFF_HEADS, DIFF_V)
    if pos is not None:
        k = rope2d(k, *pos)
    return k, v

def gqa_queries(z, q_gain, pos):
    b, n = z.shape[:2]
    q = rms_norm(z[..., :GQA_QW].reshape(b, n, GQA_KV_HEADS, GQA_GROUP, GQA_HD), q_gain)
    return rope2d(q, *pos) if pos is not None else q

def gqa_keys_values(z, k_gain, pos):
    b, n = z.shape[:2]
    k = rms_norm(z[..., GQA_QW:GQA_QW + GQA_KW].reshape(b, n, GQA_KV_HEADS, GQA_HD), k_gain)
    v = z[..., GQA_QW + GQA_KW:].reshape(b, n, GQA_KV_HEADS, GQA_HD)
    if pos is not None:
        k = rope2d(k, *pos)
    return k, v

def hybrid_mixer(u, uc, pos, conv_w, mla_q_norm, mla_kv_norm, mla_w_uq, mla_w_qr, mla_w_uk, mla_w_uv,
                 diff_lambda, diff_subln, gqa_q_norm, gqa_k_norm, layer_idx, need_ctx):
    b, s = u.shape[:2]
    za, zm, zd, zg = jnp.split(u, IN_SPLITS, axis=-1)
    zac, zmc, zdc, zgc = jnp.split(uc, IN_SPLITS, axis=-1)

    k_mc, v_mc = mla_keys_values(zmc, mla_kv_norm, mla_w_uk, mla_w_uv, None)
    k_ml, v_ml = mla_keys_values(zm, mla_kv_norm, mla_w_uk, mla_w_uv, pos)
    k_m = jnp.concatenate([k_mc, k_ml], axis=1)
    v_m = jnp.concatenate([v_mc, v_ml], axis=1)
    y_m = sweep_query_blocks(lambda qb: mha_core(qb, k_m, v_m, MLA_SCALE),
                             mla_queries(zm, mla_q_norm, mla_w_uq, mla_w_qr, pos))

    lam_init = 0.8 - 0.6 * math.exp(-0.3 * layer_idx)
    dl = diff_lambda.astype(jnp.float32)
    lam = jnp.exp(jnp.sum(dl[0] * dl[1])) - jnp.exp(jnp.sum(dl[2] * dl[3])) + lam_init
    k_dc, v_dc = diff_keys_values(zdc, None)
    k_dl, v_dl = diff_keys_values(zd, pos)
    k_d = jnp.concatenate([k_dc, k_dl], axis=1)
    v_d = jnp.concatenate([v_dc, v_dl], axis=1)
    y_d = sweep_query_blocks(lambda qb: diff_core(qb, k_d, v_d, lam, DIFF_SCALE), diff_queries(zd, pos))

    def diff_out(o):
        o = rms_norm(o, diff_subln) * (1.0 - lam_init)
        return o.reshape(o.shape[0], o.shape[1], DIFF_HEADS * DIFF_V)

    k_gc, v_gc = gqa_keys_values(zgc, gqa_k_norm, None)
    k_gl, v_gl = gqa_keys_values(zg, gqa_k_norm, pos)
    k_g = jnp.concatenate([k_gc, k_gl], axis=1)
    v_g = jnp.concatenate([v_gc, v_gl], axis=1)
    y_g = sweep_query_blocks(lambda qb: gqa_core(qb, k_g, v_g, GQA_SCALE), gqa_queries(zg, gqa_q_norm, pos))

    y = jnp.concatenate([conv_group(za, conv_w),
                         y_m.reshape(b, s, MLA_HEADS * MLA_V),
                         diff_out(y_d),
                         y_g.reshape(b, s, GQA_Q_HEADS * GQA_HD)], axis=-1)
    if not need_ctx:
        return y, None

    bc, nc = uc.shape[:2]
    yc_m = mha_core(mla_queries(zmc, mla_q_norm, mla_w_uq, mla_w_qr, None), k_mc, v_mc, MLA_SCALE)
    yc_d = diff_core(diff_queries(zdc, None), k_dc, v_dc, lam, DIFF_SCALE)
    yc_g = gqa_core(gqa_queries(zgc, gqa_q_norm, None), k_gc, v_gc, GQA_SCALE)
    yc = jnp.concatenate([conv_group(zac, conv_w),
                          yc_m.reshape(bc, nc, MLA_HEADS * MLA_V),
                          diff_out(yc_d),
                          yc_g.reshape(bc, nc, GQA_Q_HEADS * GQA_HD)], axis=-1)
    return y, yc

def grouped_expert_ffn(h, flat_e, flat_w, w1, w3, w2):
    n, d = h.shape
    a = flat_e.shape[0]
    k = a // n
    flat_tok = jnp.repeat(jnp.arange(n, dtype=jnp.int32), k)
    order = jnp.argsort(flat_e)
    se = flat_e[order]
    counts = jnp.bincount(flat_e, length=N_EXPERTS)
    starts = jnp.cumsum(counts) - counts
    padded = (counts + EXPERT_BLOCK - 1) // EXPERT_BLOCK * EXPERT_BLOCK
    pad_ends = jnp.cumsum(padded)
    pad_starts = pad_ends - padded
    dest = pad_starts[se] + (jnp.arange(a, dtype=jnp.int32) - starts[se])
    n_slots = (-(-a // EXPERT_BLOCK) + N_EXPERTS) * EXPERT_BLOCK
    slot_tok = jnp.full((n_slots,), n, jnp.int32).at[dest].set(flat_tok[order])
    slot_w = jnp.zeros((n_slots,), flat_w.dtype).at[dest].set(flat_w[order])
    xs = jnp.take(h, slot_tok, axis=0, mode='fill', fill_value=0)
    nb = n_slots // EXPERT_BLOCK
    block_e = jnp.minimum(jnp.searchsorted(pad_ends, jnp.arange(nb) * EXPERT_BLOCK, side='right'),
                          N_EXPERTS - 1)

    def expert_block(args):
        xb, e = args
        return (jax.nn.silu(xb @ w1[e]) * (xb @ w3[e])) @ w2[e]

    ys = lax.map(expert_block, (xs.reshape(nb, EXPERT_BLOCK, d), block_e)).reshape(n_slots, d)
    ys = ys * slot_w[:, None].astype(ys.dtype)
    return jax.ops.segment_sum(ys, slot_tok, num_segments=n)

def hier_moe(h, w_group, b_group, w_sub, b_sub, w1, w3, w2):
    n = h.shape[0]
    pg = jax.nn.softmax((h @ w_group + b_group).astype(jnp.float32), axis=-1)
    g_w, g_idx = lax.top_k(pg, 1)
    sub = (h @ w_sub + b_sub).reshape(n, N_GROUPS, EXPERTS_PER_GROUP)
    sub = sub[jnp.arange(n), g_idx[:, 0]]
    ps = jax.nn.softmax(sub.astype(jnp.float32), axis=-1)
    e_w, e_local = lax.top_k(ps, TOP_K)
    e_w = e_w / jnp.sum(e_w, axis=-1, keepdims=True)
    weights = g_w * e_w
    experts = g_idx * EXPERTS_PER_GROUP + e_local
    return grouped_expert_ffn(h, experts.reshape(-1), weights.reshape(-1), w1, w3, w2)

def setup_inputs(seed: int = 0) -> dict:
    key = jax.random.key(seed)
    ks = iter(jax.random.split(key, 40))
    L, D = DEPTH, D_MODEL

    def nrm(shape, scale):
        return jax.random.normal(next(ks), shape, jnp.float32) * scale

    return {
        "x": nrm((BATCH, SEQ, D), 1.0),
        "c": nrm((BATCH, D), 1.0),
        "ctx": nrm((BATCH, CTX_LEN, D), 1.0),
        "c_ctx": nrm((D,), 1.0),
        "w_ada": nrm((L, D, 6 * D), ADA_SCALE * D ** -0.5),
        "b_ada": nrm((L, 6 * D), 0.01),
        "w_in": nrm((L, D, D_IN), D ** -0.5),
        "w_out": nrm((L, D_MIX, D), DEEPNORM_BETA * D_MIX ** -0.5),
        "conv_w": nrm((L, CONV_WIDTH, CONV_CH), CONV_WIDTH ** -0.5),
        "mla_q_norm": 1.0 + nrm((L, MLA_Q_LORA), 0.02),
        "mla_kv_norm": 1.0 + nrm((L, MLA_KV_LORA), 0.02),
        "mla_w_uq": nrm((L, MLA_Q_LORA, MLA_HEADS * MLA_NOPE), MLA_Q_LORA ** -0.5),
        "mla_w_qr": nrm((L, MLA_Q_LORA, MLA_HEADS * MLA_ROPE), MLA_Q_LORA ** -0.5),
        "mla_w_uk": nrm((L, MLA_KV_LORA, MLA_HEADS * MLA_NOPE), MLA_KV_LORA ** -0.5),
        "mla_w_uv": nrm((L, MLA_KV_LORA, MLA_HEADS * MLA_V), MLA_KV_LORA ** -0.5),
        "diff_lambda": nrm((L, 4, DIFF_QK), 0.1),
        "diff_subln": 1.0 + nrm((L, DIFF_V), 0.02),
        "gqa_q_norm": 1.0 + nrm((L, GQA_HD), 0.02),
        "gqa_k_norm": 1.0 + nrm((L, GQA_HD), 0.02),
        "ln1_g": 1.0 + nrm((L, D), 0.02),
        "ln1_b": nrm((L, D), 0.02),
        "ln2_g": 1.0 + nrm((L, D), 0.02),
        "ln2_b": nrm((L, D), 0.02),
        "moe_w_group": nrm((L, D, N_GROUPS), D ** -0.5),
        "moe_b_group": nrm((L, N_GROUPS), 0.01),
        "moe_w_sub": nrm((L, D, N_EXPERTS), D ** -0.5),
        "moe_b_sub": nrm((L, N_EXPERTS), 0.01),
        "moe_w1": nrm((L, N_EXPERTS, D, D_EXPERT), D ** -0.5),
        "moe_w3": nrm((L, N_EXPERTS, D, D_EXPERT), D ** -0.5),
        "moe_w2": nrm((L, N_EXPERTS, D_EXPERT, D), DEEPNORM_BETA * D_EXPERT ** -0.5),
    }

def reference(x, c, ctx, c_ctx, w_ada, b_ada, w_in, w_out, conv_w, mla_q_norm, mla_kv_norm,
              mla_w_uq, mla_w_qr, mla_w_uk, mla_w_uv, diff_lambda, diff_subln, gqa_q_norm, gqa_k_norm,
              ln1_g, ln1_b, ln2_g, ln2_b, moe_w_group, moe_b_group, moe_w_sub, moe_b_sub,
              moe_w1, moe_w3, moe_w2):
    b, s, d = x.shape
    n_ctx = ctx.shape[1]
    rows = s // GRID_W
    row = jnp.repeat(jnp.arange(rows, dtype=jnp.int32), GRID_W)
    col = jnp.tile(jnp.arange(GRID_W, dtype=jnp.int32), rows)
    pos = (row, col)
    silu_c = jax.nn.silu(c)
    silu_cc = jax.nn.silu(c_ctx)
    cx = ctx
    for l in range(DEPTH):
        need_ctx = l < DEPTH - 1
        mod = (silu_c @ w_ada[l] + b_ada[l])[:, None, :]
        sh1, sc1, g1, sh2, sc2, g2 = jnp.split(mod, 6, axis=-1)
        modc = silu_cc @ w_ada[l] + b_ada[l]
        csh1, csc1, cg1, csh2, csc2, cg2 = jnp.split(modc, 6, axis=-1)

        u = (x * (1.0 + sc1) + sh1) @ w_in[l]
        uc = (cx * (1.0 + csc1) + csh1) @ w_in[l]
        y, yc = hybrid_mixer(u, uc, pos, conv_w[l], mla_q_norm[l], mla_kv_norm[l], mla_w_uq[l],
                             mla_w_qr[l], mla_w_uk[l], mla_w_uv[l], diff_lambda[l], diff_subln[l],
                             gqa_q_norm[l], gqa_k_norm[l], l, need_ctx)
        x = layer_norm(DEEPNORM_ALPHA * x + g1 * (y @ w_out[l]), ln1_g[l], ln1_b[l])
        tokens = (x * (1.0 + sc2) + sh2).reshape(b * s, d)
        if need_ctx:
            cx = layer_norm(DEEPNORM_ALPHA * cx + cg1 * (yc @ w_out[l]), ln1_g[l], ln1_b[l])
            tokens = jnp.concatenate([tokens, (cx * (1.0 + csc2) + csh2).reshape(b * n_ctx, d)], axis=0)

        f = hier_moe(tokens, moe_w_group[l], moe_b_group[l], moe_w_sub[l], moe_b_sub[l],
                     moe_w1[l], moe_w3[l], moe_w2[l])
        x = layer_norm(DEEPNORM_ALPHA * x + g2 * f[:b * s].reshape(b, s, d), ln2_g[l], ln2_b[l])
        if need_ctx:
            cx = layer_norm(DEEPNORM_ALPHA * cx + cg2 * f[b * s:].reshape(b, n_ctx, d), ln2_g[l], ln2_b[l])
    return x


_drawn_inputs = setup_inputs


def setup_inputs(seed=0):
    import zlib

    import numpy as np

    out = dict(_drawn_inputs(seed))
    spreads = {}
    factors = {'ctx': 7.155,
     'c_ctx': 3.373,
     'b_ada': 8.0,
     'mla_q_norm': 8.0,
     'mla_kv_norm': 8.0,
     'mla_w_uq': 8.0,
     'mla_w_qr': 8.0,
     'mla_w_uk': 8.0,
     'mla_w_uv': 3.048,
     'diff_lambda': 8.0,
     'diff_subln': 8.0,
     'gqa_q_norm': 8.0,
     'gqa_k_norm': 8.0,
     'moe_b_group': 8.0,
     'moe_b_sub': 8.0}
    for name, (base, spread) in spreads.items():
        noise = np.random.default_rng([zlib.crc32(name.encode()), seed]).standard_normal(out[name].shape)
        drawn = base * np.exp(spread * noise) if base else spread * noise
        out[name] = __import__('jax').numpy.asarray(drawn.astype(out[name].dtype))
    for name, factor in factors.items():
        out[name] = (out[name] * factor).astype(out[name].dtype)
    return out
```

```python
import math
from contextlib import ExitStack

import concourse.bass as bass
import numpy as np
from concourse import mybir

F32 = mybir.dt.float32
I32 = mybir.dt.int32
U32 = mybir.dt.uint32
ALU = mybir.AluOpType
ACT = mybir.ActivationFunctionType
AX_X = mybir.AxisListType.X

DEPTH, D, LAT, CTX, GRID_W = 2, 1024, 1024, 256, 64
P = 128
KD = D // P
NT_LAT, NT_CTX = LAT // P, CTX // P
NT = NT_LAT + NT_CTX
T = NT * P
EPS, THETA = 1e-6, 10000.0
CONV = 256
MLA_H, MLA_QK, MLA_NOPE = 4, 96, 64
DIFF_H, DIFF_QK = 4, 32
GQA_KV, GQA_G, HD = 2, 2, 64
MLA_SCALE, DIFF_SCALE, GQA_SCALE = MLA_QK ** -0.5, DIFF_QK ** -0.5, HD ** -0.5
NG, EPG, NE, DE = 4, 8, 32, 256
ALPHA = (2 * DEPTH) ** 0.25

GATE_C, VAL, GATE_B, CQ, DQ, DK, GQ, GK, CKV, DV, GV, KR = (
    0, 256, 512, 768, 1024, 1280, 1536, 1792, 1920, 2048, 2304, 2432)
D_IN = 2464
U_CHUNKS = [(0, 512), (512, 1024), (1024, 1536), (1536, 2048), (2048, 2464)]
QM, QD, QG, QB, Q_W = 0, 384, 640, 896, 1152
U_CQ, U_DQ, U_GQ, U_CKV, U_KR, U_W = 512, 768, 1280, 1664, 1792, 1824
U_OF = {GATE_C: 0, DQ: U_DQ, GQ: U_GQ}
A_STEPS, VAR_STEP = 10, 3
ZROWS = 1 + LAT + 1 + CTX + 1

CAP_BLOCKS = T // P
MAX_OVER = (2 * T - 1) // P
YROWS = (NE + MAX_OVER) * P


def conv_row(t):
    return t * P + 1 if not isinstance(t, int) or t < NT_LAT else t * P + 2


def phase_semaphores(nc, ctx, name):
    held = []

    def give_back():
        nc.clear_and_free_semaphores(held)
        nc.all_engine_barrier()

    ctx.callback(give_back)

    def sem(n):
        held.append(nc.alloc_semaphore(name(n)))
        return held[-1]

    return sem


def mod_weights(nc, l, io, c, keep):
    NCH, RING = 12, 3
    ctx = ExitStack()
    sb = lambda n, s, d=F32: ctx.enter_context(nc.sbuf_tensor(f"{n}_{l}", s, d))
    sem = phase_semaphores(nc, ctx, lambda n: f"{n}_{l}")
    with ctx:
        wa = sb("wa", [P, RING, KD, 512])
        mod = sb("mod", [2, 6 * D])
        bias = sb("ada_bias", [2, 6 * D])
        ct = sb("ct", [P, KD, 2])
        et = sb("et", [P, KD, 2])
        st = sb("silu_c", [P, KD, 2])
        ps = c["ps"]
        wa_in = [sem(f"wa_in{j}") for j in range(RING)]
        small_in, neg_exp, silu_step, silu_rdy = sem("mod_small_in"), sem("neg_exp"), sem("silu_step"), sem("silu_rdy")
        mm_done, mod_rdy, col_ps, stored = (
            sem("mod_mm"), sem("mod_rdy"), sem("col_ps"), sem("mod_stored"))

        with nc.Block() as block:
            @block.sync
            def _(sp):
                sp.dma_start(ct[:, :, :], io["c_cols"]).then_inc(small_in, 16)
                sp.dma_start(bias[:, :], io["b_ada"][l:l + 1, :].broadcast_to([2, 6 * D])).then_inc(small_in, 16)
                with sp.Fori(0, NCH // RING) as i:
                    for j in range(RING):
                        sp.wait_ge(mm_done, i * RING + j + 1)
                        sp.dma_start(wa[:, j, :, :], io["w_ada"][l, bass.ds(i * RING + j, 1), :, :, :].rearrange(
                            "a p k n -> p (a k) n")).then_inc(wa_in[j], 16)
                sp.wait_ge(mod_rdy, RING + NCH)
                sp.dma_start(io["mod"][:, :], mod[:, :]).then_inc(stored, 16)
                sp.wait_ge(stored, 16)

            @block.scalar
            def _(act):
                act.wait_ge(small_in, 32)
                act.activation(et[:, :, :], ct[:, :, :], ACT.Exp, scale=-1.0).then_inc(neg_exp, 1)

            @block.vector
            def _(dve):
                dve.sem_inc(mod_rdy, RING)
                dve.wait_ge(neg_exp, 1)
                dve.tensor_scalar(et[:, :, :], et[:, :, :], 1.0, None, ALU.add).then_inc(silu_step, 1)
                dve.wait_ge(silu_step, 1)
                dve.reciprocal(et[:, :, :], et[:, :, :]).then_inc(silu_step, 1)
                dve.wait_ge(silu_step, 2)
                dve.tensor_tensor(st[:, :, :], et[:, :, :], ct[:, :, :], ALU.mult).then_inc(silu_rdy, 1)
                with dve.Fori(0, NCH // RING) as i:
                    for j in range(RING):
                        dve.wait_ge(mm_done, RING + i * RING + j + 1)
                        at = bass.ds(i * (RING * 512) + j * 512, 512)
                        dve.tensor_tensor(mod[:, at], ps[0:2, j * 512:(j + 1) * 512], bias[:, at],
                                          ALU.add).then_inc(mod_rdy, 1)
                dve.wait_ge(col_ps, 1)
                dve.tensor_copy(keep["shift1"][:, :, :],
                                ps[:, 2048:2048 + 2 * KD].rearrange("p (k s) -> p k s", s=2))
                dve.tensor_scalar(keep["scale1"][:, :, :],
                                  ps[:, 2048 + 2 * KD:2048 + 4 * KD].rearrange("p (k s) -> p k s", s=2),
                                  1.0, None, ALU.add)

            @block.tensor
            def _(pe):
                pe.sem_inc(mm_done, RING)
                pe.wait_ge(silu_rdy, 1)
                with pe.Fori(0, NCH // RING) as i:
                    for j in range(RING):
                        pe.wait_ge(wa_in[j], i * 16 + 16)
                        pe.wait_ge(mod_rdy, i * RING + j + 1)
                        for k in range(KD):
                            mm = pe.matmul(ps[0:2, j * 512:(j + 1) * 512], st[:, k, :], wa[:, j, k, :],
                                           start=(k == 0), stop=(k == KD - 1))
                        mm.then_inc(mm_done, 1)
                pe.wait_ge(mod_rdy, RING + NCH)
                for v in range(2):
                    for k in range(KD):
                        at = v * D + k * P
                        o = 2048 + (v * KD + k) * 2
                        mm = pe.matmul(ps[:, o:o + 2], mod[0:2, at:at + P], c["ident"][0:2, 0:2], start=True, stop=True)
                mm.then_inc(col_ps, 1)


class Steps:

    def __init__(self, eng, sem, per_tile):
        self.eng, self.sem, self.per_tile = eng, sem, per_tile

    def begin(self, t):
        self.base, self.k = t * self.per_tile, 0

    def after(self, ins):
        self.k += 1
        ins.then_inc(self.sem, 1)
        self.eng.wait_ge(self.sem, self.base + self.k)

    def end(self):
        assert self.k == self.per_tile, (self.k, self.per_tile)


def in_pairs(eng, n, body):
    if n > 2:
        with eng.Fori(0, n // 2) as r:
            for s in range(2):
                body(r * 2 + s, s, r)
    else:
        for t in range(n):
            body(t, t % 2, t // 2)


def skewed(eng, head, tail):
    head(0, 0, 0, 0)
    with eng.Fori(0, NT_LAT // 2 - 1) as r:
        head(r * 2 + 1, 1, r, 0)
        tail(r * 2, 0, r)
        head(r * 2 + 2, 0, r + 1, 0)
        tail(r * 2 + 1, 1, r)
    for t in range(NT_LAT - 1, NT):
        head(t, t % 2, t // 2, 0 if t < NT_LAT else 1)
        tail(t - 1, (t - 1) % 2, (t - 1) // 2)
    tail(NT - 1, (NT - 1) % 2, (NT - 1) // 2)


def project(nc, l, io, c, keep, kv):
    ctx = ExitStack()
    sb = lambda n, s, d=F32: ctx.enter_context(nc.sbuf_tensor(f"{n}_{l}", s, d))
    sem = phase_semaphores(nc, ctx, lambda n: f"p1_{n}_{l}")
    x_src = io["x_in"] if l == 0 else io["x_mid"]
    with ctx:
        w_in = sb("w_in", [P, KD, D_IN])
        w_q = sb("w_q", [P, 2, 4 * MLA_QK])
        w_kv = sb("w_kv", [P, 512])
        lat_gain = sb("lat_gain", [P, 3])
        qk_gain = sb("qk_gain", [P, 384])
        rope = sb("rope", [P, NT, 192])
        neg_half = sb("neg_half", [P, 8])
        xt = [sb(f"xt{j}", [P, D]) for j in range(2)]
        hT = sb("hT", [P, KD, P])
        u = [sb(f"u{j}", [P, U_W]) for j in range(2)]
        qrow = [sb(f"qrow{j}", [P, Q_W]) for j in range(2)]
        zc = [sb(f"zc{j}", [P, CONV]) for j in range(2)]
        ka = [sb(f"ka{j}", [P, MLA_H, MLA_QK]) for j in range(2)]
        lat = [sb(f"lat{j}", [P, 384]) for j in range(2)]
        kdg = [sb(f"kdg{j}", [P, 384]) for j in range(2)]
        latT = sb("latT", [P, 3, P])
        t1 = sb("rt1", [P, 512])
        t2 = sb("rt2", [P, 512])
        ss = sb("ss", [P, 8])
        rs = sb("rs", [P, 8])
        junk = sb("junk", [P, 256])
        zero_row = sb("zero_row", [P, CONV])
        ps = c["ps"]
        ident = c["ident"]
        w_sem = sem("weights_in")
        x_in = [sem(f"x_in{j}") for j in range(2)]
        xT_ps, hT_rdy, u_ps, u_rdy = sem("xT_ps"), sem("hT_rdy"), sem("u_ps"), sem("u_rdy")
        sq_rdy, rs_rdy = sem("sq_rdy"), sem("rs_rdy")
        a_step, b_step, b_done = sem("a_step"), sem("b_step"), sem("b_done")
        latT_ps, latT_rdy, q_ps, kv_ps, q_rdy, kv_rdy = (
            sem("latT_ps"), sem("latT_rdy"), sem("q_ps"), sem("kv_ps"), sem("q_rdy"), sem("kv_rdy"))
        kT_ps, kT_rdy, kmT_ps, kmT_rdy = sem("kT_ps"), sem("kT_rdy"), sem("kmT_ps"), sem("kmT_rdy")
        zc_rdy, half_rdy, zero_out = sem("zc_rdy"), sem("half_rdy"), sem("zero_out")
        ys_zeroed = sem("ys_zeroed")
        q_out = [sem(f"q_out{j}") for j in range(2)]

        with nc.Block() as block:
            @block.sync
            def _(sp):
                sp.dma_start(w_q[:, :, :], io["w_q"][l]).then_inc(w_sem, 16)
                sp.dma_start(w_kv[:, :], io["w_kv"][l]).then_inc(w_sem, 16)
                sp.dma_start(lat_gain[:, :], io["lat_gain"][l]).then_inc(w_sem, 16)
                sp.dma_start(qk_gain[:, :], io["qk_gain"][l:l + 1, :].broadcast_to([P, 384])).then_inc(w_sem, 16)
                sp.dma_start(rope[:, :, :], io["rope"]).then_inc(w_sem, 16)
                for k in range(KD):
                    sp.dma_start(w_in[:, k, :], io["w_in"][l, :, k, :]).then_inc(w_sem, 16)

                def load(t, s):
                    sp.dma_start(xt[s][:, :], x_src[bass.ds(t * P, P), :]).then_inc(x_in[s], 16)

                def store(t, s):
                    sp.wait_ge(b_done, t + 3)
                    sp.dma_start(io["qrow"][bass.ds(t * P, P), :], qrow[s][:, :]).then_inc(q_out[s], 16)
                    sp.wait_ge(zc_rdy, t + 1)
                    sp.dma_start(io["zc"][bass.ds(conv_row(t), P), :], zc[s][:, :]).then_inc(q_out[s], 16)

                sp.wait_ge(half_rdy, 2)
                for row in (0, LAT + 1, ZROWS - 1):
                    sp.dma_start(io["zc"][row:row + 1, :], zero_row[0:1, :]).then_inc(zero_out, 16)
                for s in range(2):
                    sp.sem_inc(q_out[s], 32)
                    load(s, s)
                with sp.Fori(0, NT_LAT // 2) as r:
                    for s in range(2):
                        sp.wait_ge(xT_ps, r * 2 + s + 1)
                        load(r * 2 + s + 2, s)
                        store(r * 2 + s, s)
                for t in range(NT_LAT, NT):
                    store(t, t % 2)
                sp.wait_ge(zero_out, 48)
                for s in range(2):
                    sp.wait_ge(q_out[s], 32 + 32 * (NT // 2))

            @block.tensor
            def _(pe):
                pe.wait_ge(w_sem, 16 * (5 + KD))

                def head(t, s, r, ctxt):
                    pe.wait_ge(x_in[s], r * 16 + 16)
                    pe.wait_ge(kmT_rdy, t + 1)
                    for k in range(KD):
                        tr = pe.transpose(ps[:, 2560 + k * P:2560 + (k + 1) * P], xt[s][:, k * P:(k + 1) * P],
                                          ident[:, :])
                    tr.then_inc(xT_ps, 1)
                    pe.wait_ge(hT_rdy, t * 2 + 2)
                    for n, (a, b) in enumerate(U_CHUNKS):
                        pe.wait_ge(u_rdy, t * 5 + n + 1)
                        for k in range(KD):
                            mm = pe.matmul(ps[:, n * 512:n * 512 + b - a], hT[:, k, :], w_in[:, k, a:b],
                                           start=(k == 0), stop=(k == KD - 1))
                        mm.then_inc(u_ps, 1)

                def tail(t, s, r):
                    pe.wait_ge(kmT_rdy, t + 2)
                    pe.wait_ge(a_step, t * A_STEPS + A_STEPS)
                    for j in range(3):
                        tr = pe.transpose(ps[:, 3584 + j * P:3584 + (j + 1) * P], lat[s][:, j * P:(j + 1) * P],
                                          ident[:, :])
                    tr.then_inc(latT_ps, 1)
                    for j in range(3):
                        tr = pe.transpose(ps[:, 2560 + j * P:2560 + (j + 1) * P], kdg[s][:, j * P:(j + 1) * P],
                                          ident[:, :])
                    tr.then_inc(kT_ps, 1)
                    pe.wait_ge(latT_rdy, t + 1)
                    for j in range(2):
                        mm = pe.matmul(ps[:, 3072:3072 + 384], latT[:, j, :], w_q[:, j, :], start=(j == 0),
                                       stop=(j == 1))
                    mm.then_inc(q_ps, 1)
                    pe.matmul(ps[:, 3584:4096], latT[:, 2, :], w_kv[:, :], start=True, stop=True).then_inc(kv_ps, 1)
                    pe.wait_ge(kT_rdy, t + 1)
                    pe.wait_ge(kv_rdy, t + 1)
                    for h in range(MLA_H):
                        tr = pe.transpose(ps[0:MLA_QK, 2560 + h * P:2560 + (h + 1) * P], ka[s][:, h, :], ident[:, :])
                    tr.then_inc(kmT_ps, 1)

                skewed(pe, head, tail)

            @block.scalar
            def _(act):
                act.sem_inc(u_rdy, 5)
                act.sem_inc(kmT_rdy, 2)
                act.wait_ge(w_sem, 16 * (5 + KD))

                def head(t, s, r, ctxt):
                    act.wait_ge(xT_ps, t + 1)
                    for k in range(KD // 2):
                        op = act.activation(hT[:, k, :], ps[:, 2560 + k * P:2560 + (k + 1) * P], ACT.Identity,
                                            bias=keep["shift1"][:, k, ctxt:ctxt + 1],
                                            scale=keep["scale1"][:, k, ctxt:ctxt + 1])
                    op.then_inc(hT_rdy, 1)
                    act.wait_ge(b_done, t + 1)
                    act.wait_ge(q_out[s], r * 32 + 32)
                    for n, (a, b) in enumerate(U_CHUNKS):
                        act.wait_ge(u_ps, t * 5 + n + 1)
                        b0 = n * 512
                        if a == GATE_B:
                            act.copy(qrow[s][:, QB:QB + CONV], ps[:, b0:b0 + CONV])
                            op = act.copy(u[s][:, U_CQ:U_CQ + 256], ps[:, b0 + 256:b0 + 512])
                        elif a == DV:
                            act.copy(kv["vd"][:, bass.ds(t, 1), :], ps[:, b0:b0 + 256].unsqueeze(1))
                            act.copy(kv["vg"][:, bass.ds(t, 1), :], ps[:, b0 + 256:b0 + 384].unsqueeze(1))
                            op = act.copy(u[s][:, U_KR:U_KR + 32], ps[:, b0 + 384:b0 + 416])
                        else:
                            ua = U_OF[a]
                            op = act.copy(u[s][:, ua:ua + b - a], ps[:, b0:b0 + b - a])
                        op.then_inc(u_rdy, 1)
                    act.wait_ge(u_rdy, t * 5 + 10)
                    act.wait_ge(rs_rdy, t + 1)
                    act.activation(junk[:, :], u[s][:, U_CQ:U_CQ + 256], ACT.Square, scale=256 ** -0.5,
                                   accum_out=ss[:, 0:1]).then_inc(sq_rdy, 1)
                    act.wait_ge(sq_rdy, t * 2 + 1)
                    act.activation(junk[:, 0:128], u[s][:, U_CKV:U_CKV + 128], ACT.Square, scale=128 ** -0.5,
                                   accum_out=ss[:, 1:2]).then_inc(sq_rdy, 1)

                def tail(t, s, r):
                    act.wait_ge(latT_ps, t + 1)
                    for j in range(3):
                        op = act.activation(latT[:, j, :], ps[:, 3584 + j * P:3584 + (j + 1) * P], ACT.Copy,
                                            scale=lat_gain[:, j:j + 1])
                    op.then_inc(latT_rdy, 1)
                    act.wait_ge(kT_ps, t + 1)
                    act.copy(kv["kd"][:, :, bass.ds(t * P, P)],
                             ps[:, 2560:2560 + 2 * P].rearrange("p (j n) -> p j n", j=2))
                    act.copy(kv["kg"][:, bass.ds(t * P, P)], ps[:, 2560 + 2 * P:2560 + 3 * P]).then_inc(kT_rdy, 1)
                    act.wait_ge(kv_ps, t + 1)
                    act.copy(ka[s][:, :, 0:MLA_NOPE],
                             ps[:, 3584:3584 + 256].rearrange("p (h n) -> p h n", h=MLA_H)).then_inc(kv_rdy, 1)
                    act.copy(kv["vm"][:, bass.ds(t, 1), :], ps[:, 3840:4096].unsqueeze(1))
                    act.wait_ge(q_ps, t + 1)
                    act.copy(qrow[s][:, 0:384], ps[:, 3072:3072 + 384]).then_inc(q_rdy, 1)
                    act.wait_ge(kmT_ps, t + 1)
                    act.copy(kv["km"][:, :, bass.ds(t * P, P)],
                             ps[0:MLA_QK, 2560:3072].rearrange("p (h n) -> p h n", h=MLA_H)).then_inc(kmT_rdy, 1)

                skewed(act, head, tail)

            @block.gpsimd
            def _(pool):
                pool.memset(neg_half[:, :], -0.5).then_inc(half_rdy, 1)
                pool.memset(zero_row[:, :], 0.0).then_inc(half_rdy, 1)
                pool.wait_ge(half_rdy, 2)
                pool.sem_inc(rs_rdy, 1)
                if l == 0:
                    for b in range(MAX_OVER):
                        pool.dma_start(
                            io["ys"][(NE + b) * P:(NE + b + 1) * P, :].rearrange("p (a n) -> p a n", n=CONV),
                            zero_row[:, :].unsqueeze(1).broadcast_to([P, D // CONV, CONV])).then_inc(ys_zeroed, 16)

                def head(t, s, r, ctxt):
                    pool.wait_ge(u_rdy, t * 5 + 10)
                    pool.wait_ge(q_out[s], r * 32 + 32)
                    pool.tensor_tensor(zc[s][:, :], u[s][:, 0:CONV], u[s][:, CONV:2 * CONV],
                                       ALU.mult).then_inc(zc_rdy, 1)
                    pool.wait_ge(a_step, t * A_STEPS + VAR_STEP)
                    pool.tensor_tensor(rs[:, :], ss[:, :], neg_half[:, :], ALU.pow).then_inc(rs_rdy, 1)

                skewed(pool, head, lambda t, s, r: None)
                if l == 0:
                    pool.wait_ge(ys_zeroed, 16 * MAX_OVER)

            @block.vector
            def _(dve):
                dve.sem_inc(b_done, 2)
                sa, sbb = Steps(dve, a_step, A_STEPS), Steps(dve, b_step, 1)
                dve.wait_ge(w_sem, 16 * (5 + KD))

                def rotate(z, n, w, t, steps):
                    q = w // 4
                    at = 0 if w == 32 else 64
                    cos = rope[:, bass.ds(t, 1), at:at + w].broadcast_to([P, n, w])
                    sin = rope[:, bass.ds(t, 1), at + w:at + 2 * w]
                    dve.tensor_tensor(t1[:, 0:n * w].rearrange("p (h w) -> p h w", h=n), z, cos, ALU.mult)
                    sin4 = sin.rearrange("p h (a b q) -> p h a b q", a=2, b=2)
                    out5 = t2[:, 0:n * w].rearrange("p (h a b q) -> p h a b q", a=2, b=2, q=q)
                    z5 = z.rearrange("p h (a b q) -> p h a b q", a=2, b=2)
                    for b in range(2):
                        last = dve.tensor_tensor(out5[:, :, :, b, :], z5[:, :, :, 1 - b, :],
                                                 sin4[:, :, :, b, :].broadcast_to([P, n, 2, q]), ALU.mult)
                    steps.after(last)

                def head(t, s, r, ctxt):
                    sa.begin(t)
                    dve.wait_ge(xT_ps, t + 1)
                    for k in range(KD // 2, KD):
                        op = dve.tensor_scalar(hT[:, k, :], ps[:, 2560 + k * P:2560 + (k + 1) * P],
                                               keep["scale1"][:, k, ctxt:ctxt + 1],
                                               keep["shift1"][:, k, ctxt:ctxt + 1], ALU.mult, ALU.add)
                    op.then_inc(hT_rdy, 1)
                    dve.wait_ge(u_rdy, t * 5 + 10)
                    gqk = u[s][:, U_GQ:U_GQ + 384]
                    sa.after(dve.scalar_tensor_tensor(t1[:, 0:384], gqk, 1.0 / HD, gqk, ALU.mult, ALU.mult))
                    sa.after(dve.tensor_reduce(ss[:, 2:8], t1[:, 0:384].rearrange("p (h n) -> p h n", n=HD), AX_X,
                                               ALU.add))
                    dve.wait_ge(sq_rdy, t * 2 + 2)
                    sa.after(dve.tensor_scalar(ss[:, :], ss[:, :], EPS, None, ALU.add))
                    dve.tensor_tensor(gqk, gqk, qk_gain[:, :], ALU.mult)
                    z = u[s][:, U_DQ:U_DQ + 512].rearrange("p (h w) -> p h w", w=32)
                    rotate(z, 16, 32, t, sa)
                    dve.wait_ge(q_out[s], r * 32 + 32)
                    dve.tensor_tensor(qrow[s][:, QD:QD + 256], t1[:, 0:256], t2[:, 0:256], ALU.add)
                    sa.after(dve.tensor_tensor(kdg[s][:, 0:256], t1[:, 256:512], t2[:, 256:512], ALU.add))
                    z = u[s][:, U_KR:U_KR + 32].rearrange("p (h w) -> p h w", w=32)
                    rotate(z, 1, 32, t, sa)
                    dve.wait_ge(kmT_rdy, t + 1)
                    sa.after(dve.tensor_tensor(ka[s][:, :, MLA_NOPE:MLA_QK],
                                               t1[:, 0:32].unsqueeze(1).broadcast_to([P, MLA_H, 32]),
                                               t2[:, 0:32].unsqueeze(1).broadcast_to([P, MLA_H, 32]), ALU.add))
                    dve.wait_ge(rs_rdy, t + 2)
                    dve.tensor_scalar(lat[s][:, 0:256], u[s][:, U_CQ:U_CQ + 256], rs[:, 0:1], None, ALU.mult)
                    dve.tensor_scalar(lat[s][:, 256:384], u[s][:, U_CKV:U_CKV + 128], rs[:, 1:2], None, ALU.mult)
                    g3 = gqk.rearrange("p (h n) -> p h n", n=HD)
                    sa.after(dve.tensor_tensor(g3, g3, rs[:, 2:8].unsqueeze(2).broadcast_to([P, 6, HD]), ALU.mult))
                    rotate(g3, 6, 64, t, sa)
                    dve.tensor_tensor(qrow[s][:, QG:QG + 256].rearrange("p (g k n) -> p k g n", g=2, k=2),
                                      t1[:, 0:256].rearrange("p (k g n) -> p k g n", g=2, k=2),
                                      t2[:, 0:256].rearrange("p (k g n) -> p k g n", g=2, k=2), ALU.add)
                    sa.after(dve.tensor_tensor(kdg[s][:, 256:384], t1[:, 256:384], t2[:, 256:384], ALU.add))
                    sa.end()

                def tail(t, s, r):
                    sbb.begin(t)
                    dve.wait_ge(q_rdy, t + 1)
                    dve.wait_ge(b_done, t + 2)
                    z = qrow[s][:, 0:384].rearrange("p (h w) -> p h w", w=MLA_QK)[:, :, MLA_NOPE:MLA_QK]
                    rotate(z, 4, 32, t, sbb)
                    dve.tensor_tensor(z, t1[:, 0:128].rearrange("p (h w) -> p h w", w=32),
                                      t2[:, 0:128].rearrange("p (h w) -> p h w", w=32), ALU.add).then_inc(b_done, 1)
                    sbb.end()

                skewed(dve, head, tail)


def layer_norm_steps(dve, st, z, stats, mv, tick, eps_step):
    for j in range(2):
        op = dve.bn_stats(stats[:, j, :], z[:, j * 512:(j + 1) * 512])
    st.after(op)
    dve.memset(tick[:, :], 0.0)
    st.after(dve.bn_aggr(mv[:, :], stats[:, :, :]))
    eps_step(dve.tensor_scalar(mv[:, 1:2], mv[:, 1:2], EPS, None, ALU.add))


def attend(nc, l, io, c, kv, stream):
    t0 = 0 if stream == 0 else NT_LAT
    n_tiles = NT_LAT if stream == 0 else NT_CTX
    key_tiles = list(range(NT)) if stream == 0 else list(range(NT_LAT, NT))
    k0, nk = key_tiles[0] * P, len(key_tiles) * P
    chunks = [key_tiles[a:a + 4] for a in range(0, len(key_tiles), 4)]
    nch = len(chunks)
    items = ([("diff", h, [2 * h, 2 * h + 1]) for h in range(DIFF_H)] +
             [("mla", h, [8 + h]) for h in range(MLA_H)] +
             [("gqa", h, [12 + h]) for h in range(GQA_KV * GQA_G)])
    NI, NU, NCHT = len(items), 16, len(items) * nch
    item_of = {u: n for n, (_, _, us) in enumerate(items) for u in us}
    S_AT = [1536, 0]
    T_AT, O_AT, QT_AT, WO_AT = 3072, 3584, 1536, 0
    SCALE = {"mla": MLA_SCALE, "diff": DIFF_SCALE, "gqa": GQA_SCALE}
    lam_init = 0.8 - 0.6 * math.exp(-0.3 * l)
    STEPS = NU + 2 * DIFF_H + (NI - DIFF_H) + 4 + 5
    x_src = io["x_in"] if l == 0 else io["x_mid"]

    ctx = ExitStack()
    sb = lambda n, s, d=F32: ctx.enter_context(nc.sbuf_tensor(f"at_{n}_{l}{stream}", s, d))
    sem = phase_semaphores(nc, ctx, lambda n: f"at_{n}_{l}{stream}")
    with ctx:
        w_out = sb("w_out", [P, KD, D])
        gate1, scale2, shift2 = sb("gate1", [P, D]), sb("scale2", [P, D]), sb("shift2", [P, D])
        ln_g, ln_b = sb("ln_g", [P, D]), sb("ln_b", [P, D])
        conv_w = sb("conv_w", [P, 3, CONV])
        dl = sb("dl", [P, 4, 32])
        dlp = sb("dlp", [P, 2, 32])
        dle = sb("dle", [P, 2])
        neg_lam = sb("neg_lam", [P, 1])
        subln = sb("subln", [P, HD])
        neg_half = sb("neg_half", [P, 4])
        qin = [sb(f"qin{j}", [P, Q_W]) for j in range(2)]
        zin = [sb(f"zin{j}", [P, 3, CONV]) for j in range(2)]
        xin = [sb(f"xin{j}", [P, D]) for j in range(2)]
        qT = sb("qT", [P, 8, P])
        prob = [sb(f"prob{j}", [P, nk]) for j in range(4)]
        pT = [sb(f"pT{j}", [P, nk]) for j in range(2)]
        y = [sb(f"y{j}", [P, D]) for j in range(2)]
        yT = sb("yT", [P, KD, P])
        z = sb("z", [P, D])
        x1 = [sb(f"x1{j}", [P, D]) for j in range(2)]
        h2 = [sb(f"h2{j}", [P, D]) for j in range(2)]
        mx, nm, rs, ri = sb("mx", [P, NU]), sb("nm", [P, NU]), sb("rs", [P, NU]), sb("ri", [P, NU])
        coef = sb("coef", [P, DIFF_H])
        dsq = sb("dsq", [P, 256])
        dss, drs = sb("dss", [P, 4]), sb("drs", [P, 4])
        stats, mv, rstd = sb("stats", [P, 2, 6]), sb("mv", [P, 2]), sb("rstd", [P, 1])
        tick = sb("tick", [P, 1])
        ps, ident = c["ps"], c["ident"]
        w_sem = sem("weights_in")
        q_in = [sem(f"q_in{j}") for j in range(2)]
        o_out = [sem(f"o_out{j}") for j in range(2)]
        setup, lam_exp, lam_rdy, half_rdy = sem("setup"), sem("lam_exp"), sem("lam_rdy"), sem("half_rdy")
        qT_ps, qT_rdy, s_rdy, m_rdy, exp_done, comb_done = (
            sem("qT_ps"), sem("qT_rdy"), sem("s_rdy"), sem("m_rdy"), sem("exp_done"), sem("comb_done"))
        t_ps, pt_ev, pv_done, o_ev = sem("t_ps"), sem("pt_ev"), sem("pv_done"), sem("o_ev")
        step, dvar_rdy, drs_rdy, y_rdy, conv_rdy, conv_step = (
            sem("step"), sem("dvar_rdy"), sem("drs_rdy"), sem("y_rdy"), sem("conv_rdy"), sem("conv_step"))
        yT_ps, yT_rdy, wo_ps, z_read, var_rdy, rstd_rdy, x1_rdy, h_step, h_rdy = (
            sem("yT_ps"), sem("yT_rdy"), sem("wo_ps"), sem("z_read"), sem("var_rdy"), sem("rstd_rdy"),
            sem("x1_rdy"), sem("h_step"), sem("h_rdy"))

        def tiles(eng, body):
            in_pairs(eng, n_tiles, body)

        def row(t):
            return bass.ds(t * P + t0 * P, P)

        with nc.Block() as block:
            @block.sync
            def _(sp):
                def load(t, s):
                    z0 = t * P + (t0 * P + 1 + stream)
                    sp.dma_start(qin[s][:, :], io["qrow"][row(t), :]).then_inc(q_in[s], 16)
                    for j in range(3):
                        sp.dma_start(zin[s][:, j, :], io["zc"][bass.ds(z0 + j - 1, P), :]).then_inc(q_in[s], 16)
                    sp.dma_start(xin[s][:, :], x_src[row(t), :]).then_inc(q_in[s], 16)

                def store(t, s):
                    sp.wait_ge(x1_rdy, t + 1)
                    sp.dma_start(io["x_post"][row(t), :], x1[s][:, :]).then_inc(o_out[s], 16)
                    sp.wait_ge(h_rdy, t + 1)
                    sp.dma_start(io["h2"][row(t), :], h2[s][:, :]).then_inc(o_out[s], 16)

                for s in range(2):
                    sp.sem_inc(o_out[s], 32)
                load(0, 0)
                mod = lambda v: io["mod"][stream:stream + 1, v * D:(v + 1) * D].broadcast_to([P, D])
                for dst, src in ((gate1, mod(2)), (shift2, mod(3)), (scale2, mod(4)),
                                 (ln_g, io["ln"][l, 0:1, :].broadcast_to([P, D])),
                                 (ln_b, io["ln"][l, 1:2, :].broadcast_to([P, D])),
                                 (subln, io["subln"][l:l + 1, :].broadcast_to([P, HD]))):
                    sp.dma_start(dst[:, :], src).then_inc(w_sem, 16)
                sp.dma_start(conv_w[:, :, :].rearrange("p j n -> p (j n)"),
                             io["conv_w"][l:l + 1, :].broadcast_to([P, 3 * CONV])).then_inc(w_sem, 16)
                sp.dma_start(dl[:, :, :].rearrange("p j n -> p (j n)"),
                             io["lambda"][l:l + 1, :].broadcast_to([P, P])).then_inc(w_sem, 16)
                sp.dma_start(w_out[:, :, :], io["w_out"][l]).then_inc(w_sem, 16)
                load(1, 1)
                if n_tiles > 2:
                    with sp.Fori(0, n_tiles // 2 - 1) as r:
                        for s in range(2):
                            store(r * 2 + s, s)
                            load(r * 2 + s + 2, s)
                for s in range(2):
                    store(n_tiles - 2 + s, s)
                for s in range(2):
                    sp.wait_ge(o_out[s], 32 + 32 * (n_tiles // 2))

            @block.tensor
            def _(pe):
                def scores(t, u, first):
                    kind, h, us = items[item_of[u]]
                    if u == 1:
                        pe.wait_ge(z_read, t + 1)
                    if u >= 2:
                        pe.wait_ge(exp_done, t * NU + u - 1)
                    if kind == "mla":
                        q, kk = qT[0:MLA_QK, h, :], kv["km"][0:MLA_QK, h, :]
                    elif kind == "diff":
                        b = 32 * (u % 4)
                        q, kk = qT[b:b + 32, 4 + u // 4, :], kv["kd"][b:b + 32, u // 4, :]
                    else:
                        b = 64 * (h // 2)
                        q, kk = qT[b:b + 64, 6 + h % 2, :], kv["kg"][b:b + 64, :]
                    at = S_AT[u % 2]
                    for a in range(0, nk, 512):
                        e = min(a + 512, nk)
                        mm = pe.matmul(ps[:, at + a:at + e], q, kk[:, k0 + a:k0 + e], start=True, stop=True)
                    mm.then_inc(s_rdy, 1)

                def transposes(t, n, ci):
                    kind, h, us = items[n]
                    if ci == 0 and kind == "diff":
                        pe.wait_ge(comb_done, t * DIFF_H + h + 1)
                    elif ci == 0:
                        pe.wait_ge(exp_done, t * NU + us[0] + 1)
                    pe.wait_ge(pt_ev, t * NCHT + n * nch + ci + 1)
                    for j in range(len(chunks[ci])):
                        a = (ci * 4 + j) * P
                        tr = pe.transpose(ps[:, T_AT + j * P:T_AT + (j + 1) * P], prob[us[0] % 4][:, a:a + P],
                                          ident[:, :])
                    tr.then_inc(t_ps, 1)

                def values(t, n, ci):
                    kind, h, us = items[n]
                    if ci == 0:
                        pe.wait_ge(o_ev, t * NI + n + 1)
                    pe.wait_ge(pt_ev, t * NCHT + n * nch + ci + 2)
                    for j, kt in enumerate(chunks[ci]):
                        v = {"mla": lambda: kv["vm"][:, kt, h * 64:h * 64 + 64],
                             "diff": lambda: kv["vd"][:, kt, h * 64:h * 64 + 64],
                             "gqa": lambda: kv["vg"][:, kt, (h // 2) * 64:(h // 2) * 64 + 64]}[kind]()
                        k = ci * 4 + j
                        o = O_AT + (n % 4) * 64
                        mm = pe.matmul(ps[:, o:o + 64], pT[n % 2][:, k * P:(k + 1) * P], v, start=(k == 0),
                                       stop=(k == len(key_tiles) - 1))
                    if ci == nch - 1:
                        mm.then_inc(pv_done, 1)

                def body(t, s, r):
                    pe.wait_ge(q_in[s], r * 80 + 80)
                    for j in range(8):
                        w = MLA_QK if j < 4 else P
                        a = j * MLA_QK if j < 4 else QD + (j - 4) * P
                        tr = pe.transpose(ps[0:w, QT_AT + j * P:QT_AT + (j + 1) * P], qin[s][:, a:a + w], ident[:, :])
                    tr.then_inc(qT_ps, 1)
                    pe.wait_ge(qT_rdy, t + 1)
                    for u in items[0][2]:
                        scores(t, u, True)
                    for n in range(NI + 1):
                        if n + 1 < NI:
                            for u in items[n + 1][2]:
                                scores(t, u, False)
                        for ci in range(nch):
                            if n < NI:
                                transposes(t, n, ci)
                            if n > 0:
                                values(t, n - 1, ci)
                    pe.wait_ge(conv_rdy, t + 1)
                    pe.wait_ge(y_rdy, t + 1)
                    for k in range(KD):
                        tr = pe.transpose(ps[:, QT_AT + k * P:QT_AT + (k + 1) * P], y[s][:, k * P:(k + 1) * P],
                                          ident[:, :])
                    tr.then_inc(yT_ps, 1)
                    pe.wait_ge(yT_rdy, t + 1)
                    for n in range(2):
                        for k in range(KD):
                            mm = pe.matmul(ps[:, WO_AT + n * 512:WO_AT + (n + 1) * 512], yT[:, k, :],
                                           w_out[:, k, n * 512:(n + 1) * 512], start=(k == 0), stop=(k == KD - 1))
                    mm.then_inc(wo_ps, 1)

                pe.wait_ge(w_sem, 16 * 9)
                tiles(pe, body)

            @block.scalar
            def _(act):
                act.sem_inc(pt_ev, 1)
                act.wait_ge(setup, 2)
                act.activation(dle[:, :], dle[:, :], ACT.Exp).then_inc(lam_exp, 1)

                def exps(t, n):
                    kind, h, us = items[n]
                    for u in us:
                        act.wait_ge(m_rdy, t * NU + u + 1)
                        if u >= 4:
                            act.wait_ge(t_ps, t * NCHT + (item_of[u - 4] + 1) * nch)
                        at = S_AT[u % 2]
                        act.activation(prob[u % 4][:, :], ps[:, at:at + nk], ACT.Exp, bias=nm[:, u:u + 1],
                                       scale=SCALE[kind], accum_out=rs[:, u:u + 1]).then_inc(exp_done, 1)

                def body(t, s, r):
                    act.wait_ge(qT_ps, t + 1)
                    act.copy(qT[0:MLA_QK, 0:4, :], ps[0:MLA_QK, QT_AT:QT_AT + 512].rearrange("p (j n) -> p j n", j=4))
                    act.copy(qT[:, 4:8, :], ps[:, QT_AT + 512:QT_AT + 1024].rearrange(
                        "p (j n) -> p j n", j=4)).then_inc(qT_rdy, 1)
                    exps(t, 0)
                    for n in range(NI):
                        for ci in range(nch):
                            act.wait_ge(t_ps, t * NCHT + n * nch + ci + 1)
                            if ci == 0 and n >= 2:
                                act.wait_ge(pv_done, t * NI + n - 1)
                            w = len(chunks[ci]) * P
                            act.copy(pT[n % 2][:, ci * 512:ci * 512 + w], ps[:, T_AT:T_AT + w]).then_inc(pt_ev, 1)
                        if n + 1 < NI:
                            exps(t, n + 1)
                    act.wait_ge(yT_ps, t + 1)
                    for b in range(2):
                        op = act.copy(yT[:, b * 4:b * 4 + 4, :],
                                      ps[:, QT_AT + b * 512:QT_AT + (b + 1) * 512].rearrange("p (j n) -> p j n", j=4))
                    op.then_inc(yT_rdy, 1)

                tiles(act, body)

            @block.vector
            def _(dve):
                dve.sem_inc(z_read, 1)
                dve.sem_inc(o_ev, 1)
                dve.wait_ge(w_sem, 16 * 9)
                dve.tensor_tensor(dlp[:, 0, :], dl[:, 0, :], dl[:, 1, :], ALU.mult)
                dve.tensor_tensor(dlp[:, 1, :], dl[:, 2, :], dl[:, 3, :], ALU.mult).then_inc(setup, 1)
                dve.wait_ge(setup, 1)
                dve.tensor_reduce(dle[:, :], dlp[:, :, :], AX_X, ALU.add).then_inc(setup, 1)
                dve.tensor_scalar(subln[:, :], subln[:, :], 1.0 - lam_init, None, ALU.mult)
                dve.tensor_scalar(scale2[:, :], scale2[:, :], 1.0, None, ALU.add).then_inc(lam_rdy, 1)
                dve.wait_ge(lam_exp, 1)
                dve.tensor_tensor(neg_lam[:, :], dle[:, 1:2], dle[:, 0:1], ALU.subtract).then_inc(lam_rdy, 1)
                dve.wait_ge(lam_rdy, 2)
                dve.tensor_scalar(neg_lam[:, :], neg_lam[:, :], -lam_init, None, ALU.add).then_inc(lam_rdy, 1)
                dve.wait_ge(lam_rdy, 3)
                st = Steps(dve, step, STEPS)

                def maxima(t, n):
                    kind, h, us = items[n]
                    for u in us:
                        dve.wait_ge(s_rdy, t * NU + u + 1)
                        at = S_AT[u % 2]
                        st.after(dve.tensor_reduce(mx[:, u:u + 1], ps[:, at:at + nk], AX_X, ALU.max))
                        dve.tensor_scalar(nm[:, u:u + 1], mx[:, u:u + 1], -SCALE[kind], None,
                                          ALU.mult).then_inc(m_rdy, 1)
                    if kind == "diff":
                        dve.wait_ge(exp_done, t * NU + us[1] + 1)
                        u = us[0]
                        st.after(dve.reciprocal(ri[:, u:u + 2], rs[:, u:u + 2]))
                        st.after(dve.tensor_scalar(coef[:, h:h + 1], ri[:, u + 1:u + 2], rs[:, u:u + 1], neg_lam[:, :],
                                                   ALU.mult, ALU.mult))
                        p0, p1 = prob[u % 4], prob[(u + 1) % 4]
                        dve.scalar_tensor_tensor(p0[:, :], p1[:, :], coef[:, h:h + 1], p0[:, :], ALU.mult,
                                                 ALU.add).then_inc(comb_done, 1)

                def output(t, s, n):
                    kind, h, us = items[n]
                    u = us[0]
                    if kind != "diff":
                        dve.wait_ge(exp_done, t * NU + u + 1)
                        st.after(dve.reciprocal(ri[:, u:u + 1], rs[:, u:u + 1]))
                    dve.wait_ge(pv_done, t * NI + n + 1)
                    col = {"mla": 256, "diff": 512, "gqa": 768}[kind] + h * 64
                    o = O_AT + (n % 4) * 64
                    dve.tensor_scalar(y[s][:, col:col + 64], ps[:, o:o + 64], ri[:, u:u + 1], None,
                                      ALU.mult).then_inc(o_ev, 1)

                def body(t, s, r):
                    st.begin(t)
                    yd = y[s][:, 512:768].rearrange("p (h n) -> p h n", n=HD)
                    maxima(t, 0)
                    for n in range(NI):
                        if n >= 2:
                            output(t, s, n - 2)
                        if n == 6:
                            dve.wait_ge(o_ev, t * NI + 4 + 1)
                            st.after(dve.scalar_tensor_tensor(dsq[:, :], y[s][:, 512:768], 1.0 / HD, y[s][:, 512:768],
                                                              ALU.mult, ALU.mult))
                            st.after(dve.tensor_reduce(dss[:, :], dsq[:, :].rearrange("p (h n) -> p h n", n=HD), AX_X,
                                                       ALU.add))
                            dve.tensor_scalar(dss[:, :], dss[:, :], EPS, None, ALU.add).then_inc(dvar_rdy, 1)
                        if n == 8:
                            dve.wait_ge(drs_rdy, t + 1)
                            st.after(dve.tensor_tensor(yd, yd, drs[:, :].unsqueeze(2).broadcast_to([P, 4, HD]),
                                                       ALU.mult))
                            st.after(dve.tensor_tensor(yd, yd, subln[:, :].unsqueeze(1).broadcast_to([P, 4, HD]),
                                                       ALU.mult))
                        if n + 1 < NI:
                            maxima(t, n + 1)
                    output(t, s, NI - 2)
                    output(t, s, NI - 1)
                    dve.wait_ge(o_ev, t * NI + NI + 1)
                    dve.sem_inc(y_rdy, 1)
                    dve.wait_ge(wo_ps, t + 1)
                    dve.tensor_tensor(z[:, :], ps[:, WO_AT:WO_AT + D], gate1[:, :], ALU.mult).then_inc(z_read, 1)
                    dve.wait_ge(z_read, t + 2)
                    st.after(dve.scalar_tensor_tensor(z[:, :], xin[s][:, :], ALPHA, z[:, :], ALU.mult, ALU.add))
                    layer_norm_steps(dve, st, z, stats, mv, tick, lambda op: op.then_inc(var_rdy, 1))
                    dve.wait_ge(rstd_rdy, t + 1)
                    st.after(dve.tensor_scalar(z[:, :], z[:, :], mv[:, 0:1], rstd[:, :], ALU.subtract, ALU.mult))
                    st.after(dve.tensor_tensor(z[:, :], z[:, :], ln_g[:, :], ALU.mult))
                    dve.wait_ge(o_out[s], r * 32 + 32)
                    dve.tensor_tensor(x1[s][:, :], z[:, :], ln_b[:, :], ALU.add).then_inc(x1_rdy, 1)
                    dve.wait_ge(x1_rdy, t + 1)
                    st.end()

                tiles(dve, body)

            @block.gpsimd
            def _(pool):
                pool.memset(neg_half[:, :], -0.5).then_inc(half_rdy, 1)
                pool.wait_ge(half_rdy, 1)
                pool.wait_ge(w_sem, 16 * 9)
                pool.wait_ge(lam_rdy, 1)

                def body(t, s, r):
                    pool.wait_ge(q_in[s], r * 80 + 80)
                    cv = zin[s]
                    pool.tensor_tensor(cv[:, :, :], zin[s][:, :, :], conv_w[:, :, :], ALU.mult).then_inc(conv_step, 1)
                    pool.wait_ge(conv_step, t * 3 + 1)
                    pool.tensor_tensor(cv[:, 0, :], cv[:, 0, :], cv[:, 1, :], ALU.add).then_inc(conv_step, 1)
                    pool.wait_ge(conv_step, t * 3 + 2)
                    pool.tensor_tensor(cv[:, 0, :], cv[:, 0, :], cv[:, 2, :], ALU.add).then_inc(conv_step, 1)
                    pool.wait_ge(conv_step, t * 3 + 3)
                    pool.tensor_tensor(y[s][:, 0:CONV], cv[:, 0, :], qin[s][:, QB:QB + CONV],
                                       ALU.mult).then_inc(conv_rdy, 1)
                    pool.wait_ge(dvar_rdy, t + 1)
                    pool.tensor_tensor(drs[:, :], dss[:, :], neg_half[:, :], ALU.pow).then_inc(drs_rdy, 1)
                    pool.wait_ge(var_rdy, t + 1)
                    pool.tensor_tensor(rstd[:, :], mv[:, 1:2], neg_half[:, 0:1], ALU.pow).then_inc(rstd_rdy, 1)
                    pool.wait_ge(x1_rdy, t + 1)
                    pool.tensor_tensor(h2[s][:, :], x1[s][:, :], scale2[:, :], ALU.mult).then_inc(h_step, 1)
                    pool.wait_ge(h_step, t + 1)
                    pool.tensor_tensor(h2[s][:, :], h2[s][:, :], shift2[:, :], ALU.add).then_inc(h_rdy, 1)

                tiles(pool, body)


def experts(nc, l, io, c):
    nt = NT if l < DEPTH - 1 else NT_LAT
    n_over = (2 * nt * P - 1) // P
    NBLK = NE + n_over
    HT_AT, LG_AT, RK_AT, CNT_AT, IX_AT = 0, 1024, 1536, 1536 + 384, 2048
    UP_AT, GT_AT, HM_AT, DN_AT = [0, 512], 1024, 2048, 2560
    W_RING = 3
    BIG = 3.0e38

    ctx = ExitStack()
    sb = lambda n, s, d=F32: ctx.enter_context(nc.sbuf_tensor(f"ex_{n}_{l}", s, d))
    sem = phase_semaphores(nc, ctx, lambda n: f"ex_{n}_{l}")
    with ctx:
        w13 = [sb(f"w13{j}", [P, KD, 2 * DE]) for j in range(W_RING)]
        w2 = [sb(f"w2{j}", [P, 2, D]) for j in range(W_RING)]
        w_route, b_route = sb("w_route", [P, KD, 36]), sb("b_route", [P, 36])
        before, ones = sb("before", [P, P]), sb("ones", [P, P])
        iota, token = sb("iota", [P, P]), sb("token", [P, NT])
        hx = [sb(f"hx{j}", [P, D]) for j in range(2)]
        hT = sb("hT", [P, KD, P])
        lg = sb("lg", [P, nt, 36])
        small = lambda n, w=nt: sb(n, [P, w])
        gmax, gsum, gi, m0, m1, i0, i1, e1 = [small(n) for n in ("gmax", "gsum", "gi", "m0", "m1", "i0", "i1", "e1")]
        g4, og = sb("g4", [P, nt, 4]), sb("og", [P, nt, 4])
        s84 = sb("s84", [P, nt, EPG, NG])
        s8, o8 = sb("s8", [P, nt, EPG]), sb("o8", [P, nt, EPG])
        ek, rk, blk, over, rmod = [small(n, 2 * nt) for n in ("ek", "rk", "blk", "over", "rmod")]
        rki = sb("rki", [P, 2 * nt], I32)
        member, mprod = sb("member", [P, 2 * nt, NE]), sb("mprod", [P, 2 * nt, NE])
        msum, cum, rank = sb("msum", [P, nt, NE]), sb("cum", [P, nt + 1, NE]), sb("rank", [P, nt, NE])
        cnt, ov, oe0, oe1 = small("cnt", NE), small("ov", NE), small("oe0", NE), small("oe1", NE)
        cnti = sb("cnti", [P, NE], I32)
        a_oh = [sb(f"a_oh{j}", [P, P]) for j in range(2)]
        b_oh = [sb(f"b_oh{j}", [P, NBLK]) for j in range(2)]
        idx = sb("idx", [P, NBLK], I32)
        ovc = sb("ovc", [1, n_over, NE])
        ovf = sb("ovf", [1, n_over + 1])
        ovi = sb("ovi", [1, n_over + 1], I32)
        xg = [sb(f"xg{j}", [P, D]) for j in range(2)]
        xgT = [sb(f"xgT{j}", [P, KD, P]) for j in range(2)]
        act1 = [sb(f"act1{j}", [P, DE]) for j in range(2)]
        hm = [sb(f"hm{j}", [P, DE]) for j in range(2)]
        hmT = [sb(f"hmT{j}", [P, 2, P]) for j in range(2)]
        yo = [sb(f"yo{j}", [P, D]) for j in range(2)]
        ps, ident = c["ps"], c["ident"]
        dest, wgt = c["dest"], c["wgt"]

        w_sem = sem("weights_in")
        h_in = [sem(f"h_in{j}") for j in range(2)]
        hT_ps, hT_rdy, lg_ps, lg_rdy = sem("hT_ps"), sem("hT_rdy"), sem("lg_ps"), sem("lg_rdy")
        step, exp_in, exp_out, ms_rdy, rank_ps, oh_rdy, ix_ps, idx_rdy = (
            sem("step"), sem("exp_in"), sem("exp_out"), sem("ms_rdy"), sem("rank_ps"), sem("oh_rdy"), sem("ix_ps"),
            sem("idx_rdy"))
        w_in = [sem(f"w_in{j}") for j in range(W_RING)]
        g_in = [sem(f"g_in{j}") for j in range(2)]
        gT_ps, gT_rdy, up_ps, silu_rdy, hm_rdy, hmT_ps, hmT_rdy, dn_ps, y_ev = (
            sem("gT_ps"), sem("gT_rdy"), sem("up_ps"), sem("silu_rdy"), sem("hm_rdy"), sem("hmT_ps"),
            sem("hmT_rdy"), sem("dn_ps"), sem("y_ev"))
        y_out = [sem(f"y_out{j}") for j in range(2)]
        o_w, o_g, o_gT_ps, o_gT, o_up, o_silu, o_hm, o_hmT_ps, o_hmT, o_dn, o_ev, o_out = (
            sem("o_w"), sem("o_g"), sem("o_gT_ps"), sem("o_gT"), sem("o_up"), sem("o_silu"), sem("o_hm"),
            sem("o_hmT_ps"), sem("o_hmT"), sem("o_dn"), sem("o_ev"), sem("o_out"))
        main_done, over_stored = sem("main_done"), sem("over_stored")

        def expert_steps(eng, body, before_all, after_all):
            before_all()
            with eng.Fori(0, (NE - 2) // 6) as r:
                for j in range(6):
                    e = 1 + j
                    body(r * 6 + e, e % 2, e % W_RING, r * 2 + e // W_RING)
            after_all()

        with nc.Block() as block:
            @block.sync
            def _(sp):
                def weights(e, wr):
                    if isinstance(e, int):
                        e_ = slice(e, e + 1)
                    else:
                        e_ = bass.ds(e, 1)
                    sp.dma_start(w13[wr][:, :, :], io["w13"][l, e_].rearrange("a p k n -> p (a k) n")).then_inc(
                        w_in[wr], 16)
                    sp.dma_start(w2[wr][:, :, :], io["w2"][l, e_].rearrange("a p k n -> p (a k) n")).then_inc(
                        w_in[wr], 16)

                for dst, src in ((w_route[:, :, :], io["w_route"][l]),
                                 (b_route[:, :], io["b_route"][l:l + 1, :].broadcast_to([P, 36])),
                                 (before[:, :], io["before"]), (ones[:, :], io["ones"]),
                                 (iota[:, :], io["iota"]), (token[:, :], io["token"])):
                    sp.dma_start(dst, src).then_inc(w_sem, 16)
                for s in range(2):
                    sp.dma_start(hx[s][:, :], io["h2"][s * P:(s + 1) * P, :]).then_inc(h_in[s], 16)
                with sp.Fori(0, nt // 2 - 1) as r:
                    for s in range(2):
                        sp.wait_ge(hT_ps, r * 2 + s + 1)
                        sp.dma_start(hx[s][:, :], io["h2"][bass.ds(r * 256 + (s + 2) * P, P), :]).then_inc(h_in[s], 16)
                for e in range(W_RING):
                    weights(e, e)
                with sp.Fori(0, 4) as r:
                    for j in range(6):
                        e = j + W_RING
                        sp.wait_ge(dn_ps, r * 6 + e - W_RING + 1)
                        weights(r * 6 + e, e % W_RING)
                for e in range(W_RING + 24, NE):
                    sp.wait_ge(dn_ps, e - W_RING + 1)
                    weights(e, e % W_RING)

                sp.wait_ge(main_done, 1)
                sp.sem_inc(o_out, 16)
                n_ov = sp.value_load(ovi[0:1, n_over:n_over + 1], min_val=0, max_val=n_over)
                with sp.Fori(0, n_over) as j:
                    with sp.If(n_ov > j):
                        e = sp.value_load(ovi[0:1, bass.ds(j, 1)], min_val=0, max_val=NE - 1)
                        sp.dma_start(w13[0][:, :, :], io["w13"][l, bass.ds(e, 1)].rearrange(
                            "a p k n -> p (a k) n")).then_inc(o_w, 16)
                        sp.dma_start(w2[0][:, :, :], io["w2"][l, bass.ds(e, 1)].rearrange(
                            "a p k n -> p (a k) n")).then_inc(o_w, 16)
                        sp.wait_ge(o_ev, j * 2 + 2)
                        sp.dma_start(io["ys"][bass.ds(j * P + NE * P, P), :], yo[0][:, :]).then_inc(o_out, 16)
                sp.wait_ge(o_out, n_ov * 16 + 16)
                sp.sem_inc(over_stored, 1)
                sp.wait_ge(over_stored, 1)

            @block.gpsimd
            def _(pool):
                def gather(b, slot, signal):
                    pool.indirect_dma_start(out=slot[:, :], out_offset=None, in_=io["h2"][:, :],
                                            in_offset=bass.IndirectOffsetOnAxis(ap=idx[:, b:b + 1], axis=0)
                                            ).then_inc(signal, 16)

                pool.wait_ge(idx_rdy, 1)
                for e in range(NE):
                    if e >= 2:
                        pool.wait_ge(gT_ps, e - 1)
                    gather(e, xg[e % 2], g_in[e % 2])
                pool.wait_ge(gT_ps, NE)
                n_ov = pool.value_load(ovi[0:1, n_over:n_over + 1], min_val=0, max_val=n_over)
                for j in range(n_over):
                    with pool.If(n_ov > j):
                        if j:
                            pool.wait_ge(o_gT_ps, j)
                        gather(NE + j, xg[0], o_g)

            @block.tensor
            def _(pe):
                pe.wait_ge(w_sem, 16 * 6)

                def route(t, s, r):
                    pe.wait_ge(h_in[s], r * 16 + 16)
                    for k in range(KD):
                        tr = pe.transpose(ps[:, HT_AT + k * P:HT_AT + (k + 1) * P], hx[s][:, k * P:(k + 1) * P],
                                          ident[:, :])
                    tr.then_inc(hT_ps, 1)
                    pe.wait_ge(hT_rdy, t * 2 + 2)
                    pe.wait_ge(lg_rdy, t + 1)
                    for k in range(KD):
                        mm = pe.matmul(ps[:, LG_AT:LG_AT + 36], hT[:, k, :], w_route[:, k, :], start=(k == 0),
                                       stop=(k == KD - 1))
                    mm.then_inc(lg_ps, 1)

                in_pairs(pe, nt, route)
                pe.wait_ge(ms_rdy, 1)
                rk_ps = ps[:, RK_AT:RK_AT + nt * NE]
                pe.matmul(rk_ps, before[:, :], msum[:, :, :].rearrange("p t e -> p (t e)"), start=True, stop=False)
                pe.matmul(rk_ps, ones[:, :], cum[:, 0:nt, :].rearrange("p t e -> p (t e)"), start=False, stop=True)
                pe.matmul(ps[:, CNT_AT:CNT_AT + NE], ones[:, :], cum[:, nt, :], start=True,
                          stop=True).then_inc(rank_ps, 1)
                for n in range(2 * nt):
                    pe.wait_ge(oh_rdy, n + 1)
                    pe.matmul(ps[:, IX_AT:IX_AT + NBLK], a_oh[n % 2][:, :], b_oh[n % 2][:, :], start=(n == 0),
                              stop=(n == 2 * nt - 1)).then_inc(ix_ps, 1)

                def gathered(xs, xTs, sig_in, value, sig_out):
                    pe.wait_ge(sig_in, value)
                    for k in range(KD):
                        tr = pe.transpose(ps[:, GT_AT + k * P:GT_AT + (k + 1) * P], xs[:, k * P:(k + 1) * P],
                                          ident[:, :])
                    tr.then_inc(sig_out, 1)

                def up(at, xTs, w, sig):
                    for k in range(KD):
                        mm = pe.matmul(ps[:, at:at + 512], xTs[:, k, :], w[:, k, :], start=(k == 0),
                                       stop=(k == KD - 1))
                    mm.then_inc(sig, 1)

                def hidden(h, sig):
                    for k in range(2):
                        tr = pe.transpose(ps[:, HM_AT + k * P:HM_AT + (k + 1) * P], h[:, k * P:(k + 1) * P],
                                          ident[:, :])
                    tr.then_inc(sig, 1)

                def down(hT_, w, sig):
                    for n in range(2):
                        for k in range(2):
                            mm = pe.matmul(ps[:, DN_AT + n * 512:DN_AT + (n + 1) * 512], hT_[:, k, :],
                                           w[:, k, n * 512:(n + 1) * 512], start=(k == 0), stop=(k == 1))
                    mm.then_inc(sig, 1)

                def step_up(e, s, wr, wn):
                    pe.wait_ge(w_in[wr], wn * 32 + 32)
                    pe.wait_ge(gT_rdy, e * 2 + 2)
                    pe.wait_ge(hm_rdy, e + 1)
                    up(UP_AT[s], xgT[s], w13[wr], up_ps)

                def step_down(e, s, wr):
                    pe.wait_ge(hmT_rdy, e + 1)
                    pe.wait_ge(y_ev, e * 2 + 2)
                    down(hmT[s], w2[wr], dn_ps)

                def step_hidden(e, s):
                    pe.wait_ge(hm_rdy, e + 3)
                    hidden(hm[s], hmT_ps)

                def first():
                    gathered(xg[0], xgT[0], g_in[0], 16, gT_ps)
                    step_up(0, 0, 0, 0)
                    gathered(xg[1], xgT[1], g_in[1], 16, gT_ps)
                    step_hidden(0, 0)

                def body(e, s, wr, wn):
                    step_up(e, s, wr, wn)
                    gathered(xg[1 - s], xgT[1 - s], g_in[1 - s],
                             (e - s) * 8 + (32 if s else 16), gT_ps)
                    step_down(e - 1, 1 - s, (wr - 1) % W_RING)
                    step_hidden(e, s)

                def last():
                    e = NE - 1
                    step_up(e, 1, e % W_RING, e // W_RING)
                    step_down(e - 1, 0, (e - 1) % W_RING)
                    step_hidden(e, 1)
                    step_down(e, 1, e % W_RING)

                expert_steps(pe, body, first, last)

                pe.wait_ge(main_done, 1)
                n_ov = pe.value_load(ovi[0:1, n_over:n_over + 1], min_val=0, max_val=n_over)
                with pe.Fori(0, n_over) as j:
                    with pe.If(n_ov > j):
                        gathered(xg[0], xgT[0], o_g, j * 16 + 16, o_gT_ps)
                        pe.wait_ge(o_w, j * 32 + 32)
                        pe.wait_ge(o_gT, j * 2 + 2)
                        up(UP_AT[0], xgT[0], w13[0], o_up)
                        pe.wait_ge(o_hm, j + 1)
                        hidden(hm[0], o_hmT_ps)
                        pe.wait_ge(o_hmT, j + 1)
                        down(hmT[0], w2[0], o_dn)

            @block.scalar
            def _(act):
                def route(t, s, r):
                    act.wait_ge(hT_ps, t + 1)
                    act.copy(hT[:, 0:4, :], ps[:, HT_AT:HT_AT + 512].rearrange(
                        "p (k n) -> p k n", k=4)).then_inc(hT_rdy, 1)

                in_pairs(act, nt, route)
                act.wait_ge(exp_in, 1)
                act.activation(g4[:, :, :], g4[:, :, :], ACT.Exp).then_inc(exp_out, 1)
                act.wait_ge(exp_in, 2)
                act.activation(e1[:, :], e1[:, :], ACT.Exp).then_inc(exp_out, 1)

                def rows(xTs, sig_in, value, sig_out):
                    act.wait_ge(sig_in, value)
                    act.copy(xTs[:, 0:4, :], ps[:, GT_AT:GT_AT + 512].rearrange(
                        "p (k n) -> p k n", k=4)).then_inc(sig_out, 1)

                def silu(e, s):
                    act.wait_ge(up_ps, e + 1)
                    act.activation(act1[s][:, :], ps[:, UP_AT[s]:UP_AT[s] + DE], ACT.Silu).then_inc(silu_rdy, 1)

                def output(e, s, n):
                    act.wait_ge(dn_ps, e + 1)
                    act.wait_ge(y_out[s], n * 16 + 16)
                    act.copy(yo[s][:, 0:512], ps[:, DN_AT:DN_AT + 512]).then_inc(y_ev, 1)
                    act.wait_ge(y_ev, e * 2 + 4)
                    rows_out = io["ys"][e * P:(e + 1) * P, :] if isinstance(e, int) else io["ys"][bass.ds(e * P, P), :]
                    act.dma_start(rows_out, yo[s][:, :]).then_inc(y_out[s], 16)

                def first():
                    for s in range(2):
                        act.sem_inc(y_out[s], 16)
                    rows(xgT[0], gT_ps, 1, gT_rdy)
                    silu(0, 0)
                    rows(xgT[1], gT_ps, 2, gT_rdy)

                def body(e, s, wr, wn):
                    silu(e, s)
                    rows(xgT[1 - s], gT_ps, e + 2, gT_rdy)
                    act.wait_ge(dn_ps, e)
                    p = 1 - s
                    act.wait_ge(y_out[p], (e - 1 - p) * 8 + 16)
                    act.copy(yo[p][:, 0:512], ps[:, DN_AT:DN_AT + 512]).then_inc(y_ev, 1)
                    act.wait_ge(y_ev, e * 2 + 2)
                    act.dma_start(io["ys"][bass.ds(e * P - P, P), :], yo[p][:, :]).then_inc(y_out[p], 16)

                def last():
                    e = NE - 1
                    silu(e, 1)
                    output(e - 1, 0, (e - 1) // 2)
                    output(e, 1, e // 2)
                    for s in range(2):
                        act.wait_ge(y_out[s], 16 + 16 * (NE // 2))
                    act.sem_inc(main_done, 1)

                expert_steps(act, body, first, last)
                n_ov = act.value_load(ovi[0:1, n_over:n_over + 1], min_val=0, max_val=n_over)
                with act.Fori(0, n_over) as j:
                    with act.If(n_ov > j):
                        rows(xgT[0], o_gT_ps, j + 1, o_gT)
                        act.wait_ge(o_up, j + 1)
                        act.activation(act1[0][:, :], ps[:, UP_AT[0]:UP_AT[0] + DE], ACT.Silu).then_inc(o_silu, 1)
                        act.wait_ge(o_dn, j + 1)
                        act.wait_ge(o_out, j * 16 + 16)
                        act.copy(yo[0][:, 0:512], ps[:, DN_AT:DN_AT + 512]).then_inc(o_ev, 1)

            @block.vector
            def _(dve):
                dve.sem_inc(lg_rdy, 1)
                dve.wait_ge(w_sem, 16 * 6)

                def route(t, s, r):
                    dve.wait_ge(hT_ps, t + 1)
                    dve.tensor_copy(hT[:, 4:8, :], ps[:, HT_AT + 512:HT_AT + 1024].rearrange(
                        "p (k n) -> p k n", k=4)).then_inc(hT_rdy, 1)
                    dve.wait_ge(lg_ps, t + 1)
                    dve.tensor_tensor(lg[:, bass.ds(t, 1), :], ps[:, LG_AT:LG_AT + 36].unsqueeze(1),
                                      b_route[:, :].unsqueeze(1), ALU.add).then_inc(lg_rdy, 1)

                in_pairs(dve, nt, route)
                dve.wait_ge(lg_rdy, nt + 1)
                st = Steps(dve, step, 0)
                st.begin(0)
                V = dve

                def tt(out, a, b, op):
                    st.after(V.tensor_tensor(out, a, b, op))

                def ts(out, a, x, op, x2=None, op2=None):
                    st.after(V.tensor_scalar(out, a, x, x2, op, op2) if op2 is not None
                             else V.tensor_scalar(out, a, x, None, op))

                def red(out, a, op):
                    st.after(V.tensor_reduce(out, a, AX_X, op))

                def over_last(v, shape):
                    return v.unsqueeze(len(shape) - 1).broadcast_to(shape)

                def count_up(n, w):
                    return iota[:, 0:w].unsqueeze(1).broadcast_to([P, n, w])

                def first_index(out, values, top, tmp, w):
                    tt(tmp, values, over_last(top, [P, nt, w]), ALU.is_equal)
                    st.after(V.scalar_tensor_tensor(tmp, tmp, -64.0, count_up(nt, w), ALU.mult, ALU.add))
                    red(out, tmp, ALU.min)
                    ts(out, out, 64.0, ALU.add)

                lgg = lg[:, :, 0:NG]
                red(gmax[:, :], lgg, ALU.max)
                first_index(gi[:, :], lgg, gmax[:, :], og[:, :, :], NG)
                V.tensor_tensor(g4[:, :, :], lgg, over_last(gmax[:, :], [P, nt, NG]), ALU.subtract).then_inc(exp_in, 1)
                tt(og[:, :, :], count_up(nt, NG), over_last(gi[:, :], [P, nt, NG]), ALU.is_equal)
                V.wait_ge(exp_out, 1)
                red(gsum[:, :], g4[:, :, :], ALU.add)
                st.after(V.reciprocal(gsum[:, :], gsum[:, :]))
                tt(s84[:, :, :, :], lg[:, :, NG:36].rearrange("p t (g e) -> p t e g", g=NG),
                   og[:, :, :].unsqueeze(2).broadcast_to([P, nt, EPG, NG]), ALU.mult)
                red(s8[:, :, :], s84[:, :, :, :], ALU.add)
                red(m0[:, :], s8[:, :, :], ALU.max)
                first_index(i0[:, :], s8[:, :, :], m0[:, :], o8[:, :, :], EPG)
                tt(o8[:, :, :], count_up(nt, EPG), over_last(i0[:, :], [P, nt, EPG]), ALU.is_equal)
                st.after(V.scalar_tensor_tensor(s8[:, :, :], o8[:, :, :], -BIG, s8[:, :, :], ALU.mult, ALU.add))
                red(m1[:, :], s8[:, :, :], ALU.max)
                first_index(i1[:, :], s8[:, :, :], m1[:, :], o8[:, :, :], EPG)
                V.tensor_tensor(e1[:, :], m1[:, :], m0[:, :], ALU.subtract).then_inc(exp_in, 1)
                V.wait_ge(exp_out, 2)
                ts(m0[:, :], e1[:, :], 1.0, ALU.add)
                st.after(V.reciprocal(m0[:, :], m0[:, :]))
                tt(wgt[:, 0:nt, 0], m0[:, :], gsum[:, :], ALU.mult)
                tt(wgt[:, 0:nt, 1], wgt[:, 0:nt, 0], e1[:, :], ALU.mult)
                ek2 = ek[:, :].rearrange("p (t k) -> p t k", k=2)
                for k, ik in enumerate((i0, i1)):
                    st.after(V.scalar_tensor_tensor(ek2[:, :, k], gi[:, :], float(EPG), ik[:, :], ALU.mult, ALU.add))
                tt(member[:, :, :], count_up(2 * nt, NE), over_last(ek[:, :], [P, 2 * nt, NE]), ALU.is_equal)
                mem4 = member[:, :, :].rearrange("p (t k) e -> p t k e", k=2)
                tt(msum[:, :, :], mem4[:, :, 0, :], mem4[:, :, 1, :], ALU.add)
                st.after(V.memset(cum[:, 0, :], 0.0))
                for t in range(nt):
                    tt(cum[:, t + 1, :], cum[:, t, :], msum[:, t, :], ALU.add)
                V.sem_inc(ms_rdy, 1)
                V.wait_ge(rank_ps, 1)
                st.after(V.tensor_copy(rank[:, :, :], ps[:, RK_AT:RK_AT + nt * NE].rearrange("p (t e) -> p t e", e=NE)))
                ts(cnt[:, :], ps[:, CNT_AT:CNT_AT + NE], float(P - 1), ALU.add)
                mp4 = mprod[:, :, :].rearrange("p (t k) e -> p t k e", k=2)
                tt(mp4, mem4, rank[:, :, :].unsqueeze(2).broadcast_to([P, nt, 2, NE]), ALU.mult)
                red(rk[:, :], mprod[:, :, :], ALU.add)
                st.after(V.tensor_copy(rki[:, :], rk[:, :]))
                ts(rki[:, :], rki[:, :], 7, ALU.arith_shift_right)
                st.after(V.tensor_copy(over[:, :], rki[:, :]))
                st.after(V.scalar_tensor_tensor(rmod[:, :], over[:, :], -float(P), rk[:, :], ALU.mult, ALU.add))
                st.after(V.tensor_copy(cnti[:, :], cnt[:, :]))
                ts(cnti[:, :], cnti[:, :], 7, ALU.arith_shift_right)
                st.after(V.tensor_copy(ov[:, :], cnti[:, :]))
                ts(ov[:, :], ov[:, :], -1.0, ALU.add, 0.0, ALU.max)
                src, dst = ov, oe0
                for sh in (1, 2, 4, 8, 16):
                    st.after(V.tensor_copy(dst[:, 0:sh], src[:, 0:sh]))
                    tt(dst[:, sh:NE], src[:, sh:NE], src[:, 0:NE - sh], ALU.add)
                    src, dst = dst, (oe1 if dst is oe0 else oe0)
                ovend, ovbase = src, dst
                tt(ovbase[:, :], ovend[:, :], ov[:, :], ALU.subtract)
                tt(mprod[:, :, :], member[:, :, :], ovbase[:, :].unsqueeze(1).broadcast_to([P, 2 * nt, NE]), ALU.mult)
                red(blk[:, :], mprod[:, :, :], ALU.add)
                tt(blk[:, :], blk[:, :], over[:, :], ALU.add)
                st.after(V.scalar_tensor_tensor(blk[:, :], blk[:, :], float(NE - 1), ek[:, :], ALU.add, ALU.subtract))
                ts(over[:, :], over[:, :], 1.0, ALU.min)
                tt(blk[:, :], blk[:, :], over[:, :], ALU.mult)
                tt(blk[:, :], blk[:, :], ek[:, :], ALU.add)
                st.after(V.scalar_tensor_tensor(dest[:, 0:2 * nt], blk[:, :], float(P), rmod[:, :], ALU.mult, ALU.add))
                oc = ovc[:, :, :]
                tt(oc, iota[0:1, 0:n_over].unsqueeze(2).broadcast_to([1, n_over, NE]),
                   ovend[0:1, :].unsqueeze(1).broadcast_to([1, n_over, NE]), ALU.is_ge)
                red(ovf[:, 0:n_over], oc, ALU.add)
                ts(ovf[:, 0:n_over], ovf[:, 0:n_over], float(NE - 1), ALU.min)
                st.after(V.tensor_copy(ovf[:, n_over:n_over + 1], ovend[0:1, NE - 1:NE]))
                st.after(V.tensor_copy(ovi[:, :], ovf[:, :]))
                for n in range(2 * nt):
                    if n >= 2:
                        V.wait_ge(ix_ps, n - 1)
                    V.tensor_scalar(a_oh[n % 2][:, :], iota[:, :], rmod[:, n:n + 1], None, ALU.is_equal)
                    V.tensor_scalar(b_oh[n % 2][:, :], iota[:, 0:NBLK], blk[:, n:n + 1], token[:, n // 2:n // 2 + 1],
                                    ALU.is_equal, ALU.mult).then_inc(oh_rdy, 1)
                V.wait_ge(ix_ps, 2 * nt)
                V.tensor_copy(idx[:, :], ps[:, IX_AT:IX_AT + NBLK]).then_inc(idx_rdy, 1)
                V.wait_ge(idx_rdy, 1)

                def rows(xTs, sig_in, value, sig_out):
                    dve.wait_ge(sig_in, value)
                    dve.tensor_copy(xTs[:, 4:8, :], ps[:, GT_AT + 512:GT_AT + 1024].rearrange(
                        "p (k n) -> p k n", k=4)).then_inc(sig_out, 1)

                def gated(e, s):
                    dve.wait_ge(silu_rdy, e + 1)
                    dve.tensor_tensor(hm[s][:, :], act1[s][:, :], ps[:, UP_AT[s] + DE:UP_AT[s] + 2 * DE],
                                      ALU.mult).then_inc(hm_rdy, 1)

                def hidden(e, s):
                    dve.wait_ge(hmT_ps, e + 1)
                    dve.tensor_copy(hmT[s][:, :, :], ps[:, HM_AT:HM_AT + 256].rearrange(
                        "p (k n) -> p k n", k=2)).then_inc(hmT_rdy, 1)

                def output(e, p):
                    dve.wait_ge(dn_ps, e + 1)
                    dve.wait_ge(y_out[p], (e - p) * 8 + 16)
                    dve.tensor_copy(yo[p][:, 512:1024], ps[:, DN_AT + 512:DN_AT + 1024]).then_inc(y_ev, 1)

                def first():
                    dve.sem_inc(hm_rdy, 2)
                    dve.sem_inc(y_ev, 2)
                    rows(xgT[0], gT_ps, 1, gT_rdy)
                    gated(0, 0)
                    rows(xgT[1], gT_ps, 2, gT_rdy)
                    hidden(0, 0)

                def body(e, s, wr, wn):
                    gated(e, s)
                    rows(xgT[1 - s], gT_ps, e + 2, gT_rdy)
                    output(e - 1, 1 - s)
                    hidden(e, s)

                def last():
                    e = NE - 1
                    gated(e, 1)
                    output(e - 1, 0)
                    hidden(e, 1)
                    output(e, 1)

                expert_steps(dve, body, first, last)
                dve.wait_ge(main_done, 1)
                n_ov = dve.value_load(ovi[0:1, n_over:n_over + 1], min_val=0, max_val=n_over)
                with dve.Fori(0, n_over) as j:
                    with dve.If(n_ov > j):
                        rows(xgT[0], o_gT_ps, j + 1, o_gT)
                        dve.wait_ge(o_silu, j + 1)
                        dve.tensor_tensor(hm[0][:, :], act1[0][:, :], ps[:, UP_AT[0] + DE:UP_AT[0] + 2 * DE],
                                          ALU.mult).then_inc(o_hm, 1)
                        dve.wait_ge(o_hmT_ps, j + 1)
                        dve.tensor_copy(hmT[0][:, :, :], ps[:, HM_AT:HM_AT + 256].rearrange(
                            "p (k n) -> p k n", k=2)).then_inc(o_hmT, 1)
                        dve.wait_ge(o_dn, j + 1)
                        dve.wait_ge(o_out, j * 16 + 16)
                        dve.tensor_copy(yo[0][:, 512:1024], ps[:, DN_AT + 512:DN_AT + 1024]).then_inc(o_ev, 1)


def combine(nc, l, io, c, out):
    nt = NT if l < DEPTH - 1 else NT_LAT
    STEPS = 6
    ctx = ExitStack()
    sb = lambda n, s, d=F32: ctx.enter_context(nc.sbuf_tensor(f"cb_{n}_{l}", s, d))
    sem = phase_semaphores(nc, ctx, lambda n: f"cb_{n}_{l}")
    RING = nt
    with ctx:
        yy = sb("yy", [P, RING, 2, D])
        xin = [sb(f"x{j}", [P, D]) for j in range(2)]
        gate2 = sb("gate2", [P, 2, D])
        ln_g, ln_b = sb("ln_g", [P, D]), sb("ln_b", [P, D])
        f = [sb(f"f{j}", [P, D]) for j in range(2)]
        z = sb("z", [P, D])
        xo = [sb(f"xo{j}", [P, D]) for j in range(2)]
        stats, mv, rstd, tick = sb("stats", [P, 2, 6]), sb("mv", [P, 2]), sb("rstd", [P, 1]), sb("tick", [P, 1])
        neg_half = sb("neg_half", [P, 1])
        dest, wgt = c["dest"], c["wgt"]
        w_sem, half_rdy = sem("w_in"), sem("half_rdy")
        x_in = [sem(f"x_in{j}") for j in range(2)]
        y_in = [sem(f"y_in{t}") for t in range(nt)]
        o_out = [sem(f"o_out{j}") for j in range(2)]
        first_rdy, step, var_rdy, rstd_rdy, xo_rdy, y_all = (
            sem("first"), sem("step"), sem("var_rdy"), sem("rstd_rdy"), sem("xo_rdy"), sem("y_all"))

        def store_at(t):
            return out[0, bass.ds(t * P, P), :] if l == DEPTH - 1 else io["x_mid"][bass.ds(t * P, P), :]

        with nc.Block() as block:
            @block.sync
            def _(sp):
                def load(t, s):
                    sp.dma_start(xin[s][:, :], io["x_post"][bass.ds(t * P, P), :]).then_inc(x_in[s], 16)

                def store(t, s):
                    sp.wait_ge(xo_rdy, t + 1)
                    sp.dma_start(store_at(t), xo[s][:, :]).then_inc(o_out[s], 16)

                for s in range(2):
                    sp.sem_inc(o_out[s], 16)
                    load(s, s)
                for s in range(2):
                    sp.dma_start(gate2[:, s, :], io["mod"][s:s + 1, 5 * D:6 * D].broadcast_to([P, D])).then_inc(w_sem, 16)
                sp.dma_start(ln_g[:, :], io["ln"][l, 2:3, :].broadcast_to([P, D])).then_inc(w_sem, 16)
                sp.dma_start(ln_b[:, :], io["ln"][l, 3:4, :].broadcast_to([P, D])).then_inc(w_sem, 16)
                with sp.Fori(0, nt // 2 - 1) as r:
                    for s in range(2):
                        store(r * 2 + s, s)
                        load(r * 2 + s + 2, s)
                for s in range(2):
                    store(nt - 2 + s, s)
                for s in range(2):
                    sp.wait_ge(o_out[s], 16 + 16 * (nt // 2))

            @block.gpsimd
            def _(pool):
                pool.memset(neg_half[:, :], -0.5).then_inc(half_rdy, 1)
                pool.wait_ge(half_rdy, 1)
                for t in range(nt):
                    for k in range(2):
                        pool.indirect_dma_start(
                            out=yy[:, t, k, :], out_offset=None, in_=io["ys"][:, :],
                            in_offset=bass.IndirectOffsetOnAxis(ap=dest[:, 2 * t + k:2 * t + k + 1], axis=0)
                        ).then_inc(y_in[t], 16)
                for t in range(nt):
                    pool.wait_ge(var_rdy, t + 1)
                    pool.tensor_tensor(rstd[:, :], mv[:, 1:2], neg_half[:, :], ALU.pow).then_inc(rstd_rdy, 1)

            @block.scalar
            def _(act):
                for t in range(nt):
                    act.wait_ge(y_in[t], 32)
                    if t >= 2:
                        act.wait_ge(step, (t - 2) * STEPS + 2)
                    act.activation(f[t % 2][:, :], yy[:, t, 0, :], ACT.Copy,
                                   scale=wgt[:, t, 0:1]).then_inc(first_rdy, 1)

            @block.vector
            def _(dve):
                dve.wait_ge(w_sem, 64)
                st = Steps(dve, step, STEPS)

                def body(t, s, stream):
                    st.begin(t)
                    dve.wait_ge(first_rdy, t + 1)
                    at = bass.ds(t, 1)
                    st.after(dve.scalar_tensor_tensor(f[s][:, :].unsqueeze(1), yy[:, at, 1, :], wgt[:, at, 1],
                                                      f[s][:, :].unsqueeze(1), ALU.mult, ALU.add))
                    st.after(dve.tensor_tensor(z[:, :], f[s][:, :], gate2[:, stream, :], ALU.mult))
                    dve.wait_ge(x_in[s], 16 * (t // 2) + 16)
                    st.after(dve.scalar_tensor_tensor(z[:, :], xin[s][:, :], ALPHA, z[:, :], ALU.mult, ALU.add))
                    for j in range(2):
                        op = dve.bn_stats(stats[:, j, :], z[:, j * 512:(j + 1) * 512])
                    st.after(op)
                    st.after(dve.bn_aggr(mv[:, :], stats[:, :, :]))
                    dve.tensor_scalar(mv[:, 1:2], mv[:, 1:2], EPS, None, ALU.add).then_inc(var_rdy, 1)
                    dve.wait_ge(rstd_rdy, t + 1)
                    st.after(dve.tensor_scalar(z[:, :], z[:, :], mv[:, 0:1], rstd[:, :], ALU.subtract, ALU.mult))
                    dve.wait_ge(o_out[s], 16 * (t // 2) + 16)
                    dve.tensor_tensor(xo[s][:, :], z[:, :], ln_g[:, :], ALU.mult).then_inc(y_all, 1)
                    dve.wait_ge(y_all, t + 1)
                    dve.tensor_tensor(xo[s][:, :], xo[s][:, :], ln_b[:, :], ALU.add).then_inc(xo_rdy, 1)
                    st.end()

                for t in range(nt):
                    body(t, t % 2, 0 if t < NT_LAT else 1)


def build(nc, io, out):
    ctx = ExitStack()
    with ctx:
        sb = lambda n, s, d=F32: ctx.enter_context(nc.sbuf_tensor(n, s, d))
        c = {"ps": ctx.enter_context(nc.psum_tensor("ps", [P, 4096], F32)),
             "ident": sb("ident", [P, P]),
             "dest": sb("dest", [P, 2 * NT], I32), "wgt": sb("wgt", [P, NT, 2])}
        keep = {"shift1": sb("shift1", [P, KD, 2]), "scale1": sb("scale1", [P, KD, 2])}
        const_in = ctx.enter_context(nc.semaphore("const_in"))
        with nc.Block() as block:
            @block.sync
            def _(sp):
                sp.dma_start(c["ident"][:, :], io["ident"]).then_inc(const_in, 16)
                sp.wait_ge(const_in, 16)
        for l in range(DEPTH):
            mod_weights(nc, l, io, c, keep)
            with ExitStack() as layer:
                kvt = lambda n, s: layer.enter_context(nc.sbuf_tensor(f"{n}_{l}", s, F32))
                kv = {"km": kvt("km", [MLA_QK, MLA_H, T]), "kd": kvt("kd", [P, 2, T]), "kg": kvt("kg", [P, T]),
                      "vm": kvt("vm", [P, NT, 256]), "vd": kvt("vd", [P, NT, 256]), "vg": kvt("vg", [P, NT, 128])}
                project(nc, l, io, c, keep, kv)
                attend(nc, l, io, c, kv, 0)
                if l < DEPTH - 1:
                    attend(nc, l, io, c, kv, 1)
            experts(nc, l, io, c)
            combine(nc, l, io, c, out)


def host_arrays(g):
    L, K = DEPTH, KD
    arr = {}
    arr["x_in"] = np.concatenate([g["x"][0], g["ctx"][0]], axis=0)
    arr["c_cols"] = np.stack([g["c"][0], g["c_ctx"]]).reshape(2, K, P).transpose(2, 1, 0)
    arr["w_ada"] = g["w_ada"].reshape(L, K, P, 12, 512).transpose(0, 3, 2, 1, 4)
    arr["b_ada"] = g["b_ada"]
    conv, mla, dif, gqa = 0, 768, 1184, 1952
    cols = [(conv + 256, 256), (conv + 512, 256), (conv, 256), (mla, 256), (dif, 512), (gqa, 384), (mla + 256, 128),
            (dif + 512, 256), (gqa + 384, 128), (mla + 384, 32)]
    order = np.concatenate([np.arange(a, a + n) for a, n in cols])
    arr["w_in"] = g["w_in"][:, :, order].reshape(L, K, P, D_IN).transpose(0, 2, 1, 3)
    uq = g["mla_w_uq"].reshape(L, 2, P, MLA_H, 64)
    qr = g["mla_w_qr"].reshape(L, 2, P, MLA_H, 32)
    arr["w_q"] = np.concatenate([uq, qr], axis=4).reshape(L, 2, P, 384).transpose(0, 2, 1, 3)
    arr["w_kv"] = np.concatenate([g["mla_w_uk"], g["mla_w_uv"]], axis=2)
    arr["lat_gain"] = np.concatenate([g["mla_q_norm"].reshape(L, 2, P), g["mla_kv_norm"].reshape(L, 1, P)],
                                     axis=1).transpose(0, 2, 1)
    arr["qk_gain"] = np.concatenate([g["gqa_q_norm"]] * 4 + [g["gqa_k_norm"]] * 2, axis=1)
    arr["w_out"] = g["w_out"].reshape(L, K, P, D).transpose(0, 2, 1, 3)
    arr["conv_w"] = g["conv_w"].reshape(L, 3 * CONV)
    arr["lambda"] = g["diff_lambda"].reshape(L, 128)
    arr["subln"] = g["diff_subln"]
    arr["ln"] = np.stack([g["ln1_g"], g["ln1_b"], g["ln2_g"], g["ln2_b"]], axis=1)
    arr["w_route"] = np.concatenate([g["moe_w_group"], g["moe_w_sub"]], axis=2).reshape(L, K, P, 36).transpose(0, 2, 1, 3)
    arr["b_route"] = np.concatenate([g["moe_b_group"], g["moe_b_sub"]], axis=1)
    w13 = np.concatenate([g["moe_w1"], g["moe_w3"]], axis=3)
    arr["w13"] = w13.reshape(L, NE, K, P, 2 * DE).transpose(0, 1, 3, 2, 4)
    arr["w2"] = g["moe_w2"].reshape(L, NE, 2, P, D).transpose(0, 1, 3, 2, 4)
    arr["ident"] = np.eye(P, dtype=np.float32)
    arr["before"] = np.triu(np.ones((P, P), np.float32), 1)
    arr["ones"] = np.ones((P, P), np.float32)
    arr["iota"] = np.broadcast_to(np.arange(P, dtype=np.float32), (P, P))
    arr["token"] = (np.arange(NT)[None, :] * P + np.arange(P)[:, None]).astype(np.float32)
    tok = np.arange(LAT)
    rope = np.zeros((T, 192), np.float32)
    rope[:, 0:32] = 1.0
    rope[:, 64:128] = 1.0
    for width, at in ((32, 0), (64, 64)):
        q = width // 4
        freqs = np.float32(THETA) ** (-np.arange(q, dtype=np.float32) / np.float32(q))
        for axis, pos in enumerate((tok // GRID_W, tok % GRID_W)):
            ang = pos.astype(np.float32)[:, None] * freqs.astype(np.float32)
            for half in range(2):
                o = at + axis * 2 * q + half * q
                rope[:LAT, o:o + q] = np.cos(ang)
                rope[:LAT, o + width:o + width + q] = np.sin(ang) * (1.0 if half else -1.0)
    arr["rope"] = rope.reshape(NT, P, 192).transpose(1, 0, 2)
    return arr


def kernel(**inputs):
    import concourse.bacc as bacc
    from concourse.bass_utils import run_bass_kernel_spmd as run

    nc = bacc.Bacc("TRN2", target_bir_lowering=False, num_devices=1)
    io, arrays = {}, {}
    for name, a in host_arrays({k: np.asarray(v) for k, v in inputs.items()}).items():
        a = np.ascontiguousarray(a)
        arrays[f"in_{name}"] = a
        io[name] = nc.dram_tensor(f"in_{name}", a.shape, mybir.dt.from_np(a.dtype), kind="ExternalInput").ap()
    for name, shape in (("mod", (2, 6 * D)), ("qrow", (T, Q_W)), ("zc", (ZROWS, CONV)), ("x_mid", (T, D)),
                        ("x_post", (T, D)), ("h2", (T, D)), ("ys", (YROWS, D))):
        io[name] = nc.dram_tensor(f"{name}_scratch", shape, F32, kind="Internal").ap()
    out = nc.dram_tensor("out_x", (1, LAT, D), F32, kind="ExternalOutput").ap()
    build(nc, io, out)
    r = run(nc, [arrays], core_ids=[0])
    return r.results[0]["out_x"]
```

```python
import math
from contextlib import ExitStack

import concourse.bass as bass
import numpy as np
from concourse import mybir

F32 = mybir.dt.float32
I32 = mybir.dt.int32
U32 = mybir.dt.uint32
ALU = mybir.AluOpType
ACT = mybir.ActivationFunctionType
AX_X = mybir.AxisListType.X

DEPTH, D, LAT, CTX, GRID_W = 2, 1024, 1024, 256, 64
P = 128
KD = D // P
NT_LAT, NT_CTX = LAT // P, CTX // P
NT = NT_LAT + NT_CTX
T = NT * P
EPS, THETA = 1e-6, 10000.0
CONV = 256
MLA_H, MLA_QK, MLA_NOPE = 4, 96, 64
DIFF_H, DIFF_QK = 4, 32
GQA_KV, GQA_G, HD = 2, 2, 64
MLA_SCALE, DIFF_SCALE, GQA_SCALE = MLA_QK ** -0.5, DIFF_QK ** -0.5, HD ** -0.5
NG, EPG, NE, DE = 4, 8, 32, 256
ALPHA = (2 * DEPTH) ** 0.25

GATE_C, VAL, GATE_B, CQ, DQ, DK, GQ, GK, CKV, DV, GV, KR = (
    0, 256, 512, 768, 1024, 1280, 1536, 1792, 1920, 2048, 2304, 2432)
D_IN = 2464
U_CHUNKS = [(0, 512), (512, 1024), (1024, 1536), (1536, 2048), (2048, 2464)]
QM, QD, QG, QB, Q_W = 0, 384, 640, 896, 1152
U_CQ, U_DQ, U_GQ, U_CKV, U_KR, U_W = 512, 768, 1280, 1664, 1792, 1824
U_OF = {GATE_C: 0, DQ: U_DQ, GQ: U_GQ}
A_STEPS, VAR_STEP = 10, 3
ZROWS = 1 + LAT + 1 + CTX + 1

CAP_BLOCKS = T // P
MAX_OVER = (2 * T - 1) // P
YROWS = (NE + MAX_OVER) * P


def conv_row(t):
    return t * P + 1 if not isinstance(t, int) or t < NT_LAT else t * P + 2


def phase_semaphores(nc, ctx, name):
    held = []

    def give_back():
        nc.clear_and_free_semaphores(held)
        nc.all_engine_barrier()

    ctx.callback(give_back)

    def sem(n):
        held.append(nc.alloc_semaphore(name(n)))
        return held[-1]

    return sem


def mod_weights(nc, l, io, c, keep):
    NCH, RING = 12, 3
    ctx = ExitStack()
    sb = lambda n, s, d=F32: ctx.enter_context(nc.sbuf_tensor(f"{n}_{l}", s, d))
    sem = phase_semaphores(nc, ctx, lambda n: f"{n}_{l}")
    with ctx:
        wa = sb("wa", [P, RING, KD, 512])
        mod = sb("mod", [2, 6 * D])
        bias = sb("ada_bias", [2, 6 * D])
        ct = sb("ct", [P, KD, 2])
        et = sb("et", [P, KD, 2])
        st = sb("silu_c", [P, KD, 2])
        ps = c["ps"]
        wa_in = [sem(f"wa_in{j}") for j in range(RING)]
        small_in, neg_exp, silu_step, silu_rdy = sem("mod_small_in"), sem("neg_exp"), sem("silu_step"), sem("silu_rdy")
        mm_done, mod_rdy, col_ps, stored = (
            sem("mod_mm"), sem("mod_rdy"), sem("col_ps"), sem("mod_stored"))

        with nc.Block() as block:
            @block.sync
            def _(sp):
                sp.dma_start(ct[:, :, :], io["c_cols"]).then_inc(small_in, 16)
                sp.dma_start(bias[:, :], io["b_ada"][l:l + 1, :].broadcast_to([2, 6 * D])).then_inc(small_in, 16)
                with sp.Fori(0, NCH // RING) as i:
                    for j in range(RING):
                        sp.wait_ge(mm_done, i * RING + j + 1)
                        sp.dma_start(wa[:, j, :, :], io["w_ada"][l, bass.ds(i * RING + j, 1), :, :, :].rearrange(
                            "a p k n -> p (a k) n")).then_inc(wa_in[j], 16)
                sp.wait_ge(mod_rdy, RING + NCH)
                sp.dma_start(io["mod"][l], mod[:, :]).then_inc(stored, 16)
                sp.wait_ge(stored, 16)

            @block.scalar
            def _(act):
                act.wait_ge(small_in, 32)
                act.activation(et[:, :, :], ct[:, :, :], ACT.Exp, scale=-1.0).then_inc(neg_exp, 1)

            @block.vector
            def _(dve):
                dve.sem_inc(mod_rdy, RING)
                dve.wait_ge(neg_exp, 1)
                dve.tensor_scalar(et[:, :, :], et[:, :, :], 1.0, None, ALU.add).then_inc(silu_step, 1)
                dve.wait_ge(silu_step, 1)
                dve.reciprocal(et[:, :, :], et[:, :, :]).then_inc(silu_step, 1)
                dve.wait_ge(silu_step, 2)
                dve.tensor_tensor(st[:, :, :], et[:, :, :], ct[:, :, :], ALU.mult).then_inc(silu_rdy, 1)
                with dve.Fori(0, NCH // RING) as i:
                    for j in range(RING):
                        dve.wait_ge(mm_done, RING + i * RING + j + 1)
                        at = bass.ds(i * (RING * 512) + j * 512, 512)
                        dve.tensor_tensor(mod[:, at], ps[0:2, j * 512:(j + 1) * 512], bias[:, at],
                                          ALU.add).then_inc(mod_rdy, 1)
                dve.wait_ge(col_ps, 1)
                dve.tensor_copy(keep["shift1"][:, :, :],
                                ps[:, 2048:2048 + 2 * KD].rearrange("p (k s) -> p k s", s=2))
                dve.tensor_scalar(keep["scale1"][:, :, :],
                                  ps[:, 2048 + 2 * KD:2048 + 4 * KD].rearrange("p (k s) -> p k s", s=2),
                                  1.0, None, ALU.add)

            @block.tensor
            def _(pe):
                pe.sem_inc(mm_done, RING)
                pe.wait_ge(silu_rdy, 1)
                with pe.Fori(0, NCH // RING) as i:
                    for j in range(RING):
                        pe.wait_ge(wa_in[j], i * 16 + 16)
                        pe.wait_ge(mod_rdy, i * RING + j + 1)
                        for k in range(KD):
                            mm = pe.matmul(ps[0:2, j * 512:(j + 1) * 512], st[:, k, :], wa[:, j, k, :],
                                           start=(k == 0), stop=(k == KD - 1))
                        mm.then_inc(mm_done, 1)
                pe.wait_ge(mod_rdy, RING + NCH)
                for v in range(2):
                    for k in range(KD):
                        at = v * D + k * P
                        o = 2048 + (v * KD + k) * 2
                        mm = pe.matmul(ps[:, o:o + 2], mod[0:2, at:at + P], c["ident"][0:2, 0:2], start=True, stop=True)
                mm.then_inc(col_ps, 1)


class Steps:

    def __init__(self, eng, sem, per_tile):
        self.eng, self.sem, self.per_tile = eng, sem, per_tile

    def begin(self, t):
        self.base, self.k = t * self.per_tile, 0

    def after(self, ins):
        self.k += 1
        ins.then_inc(self.sem, 1)
        self.eng.wait_ge(self.sem, self.base + self.k)

    def end(self):
        assert self.k == self.per_tile, (self.k, self.per_tile)


def in_pairs(eng, n, body):
    if n > 2:
        with eng.Fori(0, n // 2) as r:
            for s in range(2):
                body(r * 2 + s, s, r)
    else:
        for t in range(n):
            body(t, t % 2, t // 2)


def pipelined(eng, body):
    body(0, 0, 0, False, True, 0)
    with eng.Fori(0, NT_LAT // 2 - 1) as r:
        body(r * 2 + 1, 1, r, True, True, 0)
        body(r * 2 + 2, 0, r + 1, True, True, 0)
    for t in range(NT_LAT - 1, NT):
        body(t, t % 2, t // 2, True, t + 1 < NT, 1)


def project(nc, l, io, c, keep, kv):
    ctx = ExitStack()
    sb = lambda n, s, d=F32: ctx.enter_context(nc.sbuf_tensor(f"{n}_{l}", s, d))
    sem = phase_semaphores(nc, ctx, lambda n: f"p1_{n}_{l}")
    x_src = io["x_in"] if l == 0 else io["x_mid"]
    with ctx:
        w_in = sb("w_in", [P, KD, D_IN])
        w_q = sb("w_q", [P, 2, 4 * MLA_QK])
        w_kv = sb("w_kv", [P, 512])
        lat_gain = sb("lat_gain", [P, 3])
        qk_gain = sb("qk_gain", [P, 384])
        rope = sb("rope", [P, NT, 192])
        neg_half = sb("neg_half", [P, 8])
        xt = [sb(f"xt{j}", [P, D]) for j in range(2)]
        hT = [sb(f"hT{j}", [P, KD, P]) for j in range(2)]
        u = [sb(f"u{j}", [P, U_W]) for j in range(2)]
        qrow = [sb(f"qrow{j}", [P, Q_W]) for j in range(2)]
        zc = [sb(f"zc{j}", [P, CONV]) for j in range(2)]
        ka = [sb(f"ka{j}", [P, MLA_H, MLA_QK]) for j in range(2)]
        kdg = [sb(f"kdg{j}", [P, 384]) for j in range(2)]
        latT = sb("latT", [P, 3, P])
        t1 = sb("rt1", [P, 512])
        t2 = sb("rt2", [P, 512])
        ss = sb("ss", [P, 8])
        rs = sb("rs", [P, 8])
        junk = sb("junk", [P, 256])
        zero_row = sb("zero_row", [P, CONV])
        ps = c["ps"]
        ident = c["ident"]
        w_sem = sem("weights_in")
        w_in_in = [sem(f"w_in_in{n}") for n in range(len(U_CHUNKS))]
        x_in = [sem(f"x_in{j}") for j in range(2)]
        xT_ps, hT_rdy, u_ps, u_rdy = sem("xT_ps"), sem("hT_rdy"), sem("u_ps"), sem("u_rdy")
        sq_rdy, rs_rdy = sem("sq_rdy"), sem("rs_rdy")
        a_step, b_step, b_done = sem("a_step"), sem("b_step"), sem("b_done")
        latT_ps, latT_rdy, q_ps, kv_ps, q_rdy, kv_rdy = (
            sem("latT_ps"), sem("latT_rdy"), sem("q_ps"), sem("kv_ps"), sem("q_rdy"), sem("kv_rdy"))
        kT_ps, kT_rdy, kmT_ps, kmT_rdy = sem("kT_ps"), sem("kT_rdy"), sem("kmT_ps"), sem("kmT_rdy")
        zc_rdy, half_rdy, zero_out = sem("zc_rdy"), sem("half_rdy"), sem("zero_out")
        ys_zeroed = sem("ys_zeroed")
        q_out = [sem(f"q_out{j}") for j in range(2)]

        with nc.Block() as block:
            @block.sync
            def _(sp):
                def load(t, s):
                    sp.dma_start(xt[s][:, :], x_src[bass.ds(t * P, P), :]).then_inc(x_in[s], 16)

                for s in range(2):
                    load(s, s)
                sp.dma_start(w_in[:, :, 0:512], io["w_in"][l, :, :, 0:512]).then_inc(w_in_in[0], 16)
                sp.dma_start(w_q[:, :, :], io["w_q"][l]).then_inc(w_sem, 16)
                sp.dma_start(w_kv[:, :], io["w_kv"][l]).then_inc(w_sem, 16)
                sp.dma_start(lat_gain[:, :], io["lat_gain"][l]).then_inc(w_sem, 16)
                sp.dma_start(qk_gain[:, :], io["qk_gain"][l:l + 1, :].broadcast_to([P, 384])).then_inc(w_sem, 16)
                sp.dma_start(rope[:, :, :], io["rope"]).then_inc(w_sem, 16)

                def store(t, s):
                    sp.wait_ge(b_done, t + 3)
                    sp.dma_start(io["qrow"][bass.ds(t * P, P), :], qrow[s][:, :]).then_inc(q_out[s], 16)
                    sp.wait_ge(zc_rdy, t + 1)
                    sp.dma_start(io["zc"][bass.ds(conv_row(t), P), :], zc[s][:, :]).then_inc(q_out[s], 16)

                for n, (a, b) in list(enumerate(U_CHUNKS))[1:]:
                    sp.dma_start(w_in[:, :, a:b], io["w_in"][l, :, :, a:b]).then_inc(w_in_in[n], 16)
                sp.wait_ge(half_rdy, 2)
                for row in (0, LAT + 1, ZROWS - 1):
                    sp.dma_start(io["zc"][row:row + 1, :], zero_row[0:1, :]).then_inc(zero_out, 16)
                for s in range(2):
                    sp.sem_inc(q_out[s], 32)
                with sp.Fori(0, NT_LAT // 2) as r:
                    for s in range(2):
                        sp.wait_ge(xT_ps, r * 2 + s + 1)
                        load(r * 2 + s + 2, s)
                        store(r * 2 + s, s)
                for t in range(NT_LAT, NT):
                    store(t, t % 2)
                sp.wait_ge(zero_out, 48)
                for s in range(2):
                    sp.wait_ge(q_out[s], 32 + 32 * (NT // 2))

            @block.tensor
            def _(pe):
                def transpose_x(t, s, r):
                    pe.wait_ge(x_in[s], r * 16 + 16)
                    for k in range(KD):
                        tr = pe.transpose(ps[:, 2560 + k * P:2560 + (k + 1) * P], xt[s][:, k * P:(k + 1) * P],
                                          ident[:, :])
                    tr.then_inc(xT_ps, 1)

                def product(t, s, n, first):
                    if first:
                        pe.wait_ge(w_in_in[n], 16)
                    pe.wait_ge(u_rdy, t * 5 + n + 1)
                    a, b = U_CHUNKS[n]
                    for k in range(KD):
                        mm = pe.matmul(ps[:, n * 512:n * 512 + b - a], hT[s][:, k, :], w_in[:, k, a:b],
                                       start=(k == 0), stop=(k == KD - 1))
                    mm.then_inc(u_ps, 1)

                def rest(t, s, part):
                    if part == 1:
                        pe.wait_ge(kmT_rdy, t + 2)
                        pe.wait_ge(a_step, t * A_STEPS + A_STEPS)
                        for j, a in enumerate((U_CQ, U_CQ + P, U_CKV)):
                            tr = pe.transpose(ps[:, 3584 + j * P:3584 + (j + 1) * P], u[s][:, a:a + P], ident[:, :])
                        tr.then_inc(latT_ps, 1)
                        for j in range(3):
                            tr = pe.transpose(ps[:, 2560 + j * P:2560 + (j + 1) * P], kdg[s][:, j * P:(j + 1) * P],
                                              ident[:, :])
                        tr.then_inc(kT_ps, 1)
                    elif part == 2:
                        pe.wait_ge(latT_rdy, t + 1)
                        for j in range(2):
                            mm = pe.matmul(ps[:, 3072:3072 + 384], latT[:, j, :], w_q[:, j, :], start=(j == 0),
                                           stop=(j == 1))
                        mm.then_inc(q_ps, 1)
                        pe.matmul(ps[:, 3584:4096], latT[:, 2, :], w_kv[:, :], start=True,
                                  stop=True).then_inc(kv_ps, 1)
                    elif part == 3:
                        pe.wait_ge(kT_rdy, t + 1)
                        pe.wait_ge(kv_rdy, t + 1)
                        for h in range(MLA_H):
                            tr = pe.transpose(ps[0:MLA_QK, 2560 + h * P:2560 + (h + 1) * P], ka[s][:, h, :],
                                              ident[:, :])
                        tr.then_inc(kmT_ps, 1)

                def body(t, s, r, prev, nxt, ctxt):
                    pe.wait_ge(hT_rdy, t * 2 + 2)
                    for n in range(len(U_CHUNKS)):
                        product(t, s, n, not prev)
                        if n == 0 and nxt:
                            pe.wait_ge(kmT_rdy, t + 1)
                            transpose_x(t + 1, 1 - s, r + s)
                        if n == 1 and nxt:
                            pe.wait_ge(hT_rdy, t * 2 + 4)
                        if prev:
                            rest(t - 1, 1 - s, n)

                transpose_x(0, 0, 0)
                pe.wait_ge(w_sem, 16 * 5)
                pipelined(pe, body)
                for part in range(1, 4):
                    rest(NT - 1, (NT - 1) % 2, part)

            @block.scalar
            def _(act):
                act.sem_inc(u_rdy, 5)
                act.sem_inc(kmT_rdy, 2)

                def modulate(t, s, ctxt):
                    act.wait_ge(xT_ps, t + 1)
                    for k in range(KD // 2):
                        op = act.activation(hT[s][:, k, :], ps[:, 2560 + k * P:2560 + (k + 1) * P], ACT.Identity,
                                            bias=keep["shift1"][:, k, ctxt:ctxt + 1],
                                            scale=keep["scale1"][:, k, ctxt:ctxt + 1])
                    op.then_inc(hT_rdy, 1)

                def read_product(t, s, n):
                    a, b = U_CHUNKS[n]
                    act.wait_ge(u_ps, t * 5 + n + 1)
                    b0 = n * 512
                    if a == GATE_B:
                        act.copy(qrow[s][:, QB:QB + CONV], ps[:, b0:b0 + CONV])
                        op = act.copy(u[s][:, U_CQ:U_CQ + 256], ps[:, b0 + 256:b0 + 512])
                    elif a == DV:
                        act.copy(kv["vd"][:, bass.ds(t, 1), :], ps[:, b0:b0 + 256].unsqueeze(1))
                        act.copy(kv["vg"][:, bass.ds(t, 1), :], ps[:, b0 + 256:b0 + 384].unsqueeze(1))
                        op = act.copy(u[s][:, U_KR:U_KR + 32], ps[:, b0 + 384:b0 + 416])
                    else:
                        ua = U_OF[a]
                        op = act.copy(u[s][:, ua:ua + b - a], ps[:, b0:b0 + b - a])
                    op.then_inc(u_rdy, 1)

                def squares(t, s):
                    act.wait_ge(u_rdy, t * 5 + 10)
                    act.wait_ge(rs_rdy, t + 1)
                    act.activation(junk[:, :], u[s][:, U_CQ:U_CQ + 256], ACT.Square, scale=256 ** -0.5,
                                   accum_out=ss[:, 0:1]).then_inc(sq_rdy, 1)
                    act.wait_ge(sq_rdy, t * 2 + 1)
                    act.activation(junk[:, 0:128], u[s][:, U_CKV:U_CKV + 128], ACT.Square, scale=128 ** -0.5,
                                   accum_out=ss[:, 1:2]).then_inc(sq_rdy, 1)

                def rest(t, s, part):
                    if part == 1:
                        act.wait_ge(latT_ps, t + 1)
                        for j in range(3):
                            op = act.activation(latT[:, j, :], ps[:, 3584 + j * P:3584 + (j + 1) * P], ACT.Copy,
                                                scale=lat_gain[:, j:j + 1])
                        op.then_inc(latT_rdy, 1)
                        act.wait_ge(kT_ps, t + 1)
                        act.copy(kv["kd"][:, :, bass.ds(t * P, P)],
                                 ps[:, 2560:2560 + 2 * P].rearrange("p (j n) -> p j n", j=2))
                        act.copy(kv["kg"][:, bass.ds(t * P, P)], ps[:, 2560 + 2 * P:2560 + 3 * P]).then_inc(kT_rdy, 1)
                    elif part == 2:
                        act.wait_ge(kv_ps, t + 1)
                        act.copy(ka[s][:, :, 0:MLA_NOPE],
                                 ps[:, 3584:3584 + 256].rearrange("p (h n) -> p h n", h=MLA_H)).then_inc(kv_rdy, 1)
                        act.copy(kv["vm"][:, bass.ds(t, 1), :], ps[:, 3840:4096].unsqueeze(1))
                        act.wait_ge(q_ps, t + 1)
                        act.copy(qrow[s][:, 0:384], ps[:, 3072:3072 + 384]).then_inc(q_rdy, 1)
                    elif part == 3:
                        act.wait_ge(kmT_ps, t + 1)
                        act.copy(kv["km"][:, :, bass.ds(t * P, P)],
                                 ps[0:MLA_QK, 2560:3072].rearrange("p (h n) -> p h n", h=MLA_H)).then_inc(kmT_rdy, 1)

                def body(t, s, r, prev, nxt, ctxt):
                    act.wait_ge(b_done, t + 1)
                    act.wait_ge(q_out[s], r * 32 + 32)
                    for n in range(len(U_CHUNKS)):
                        read_product(t, s, n)
                        if n == 0 and nxt:
                            modulate(t + 1, 1 - s, ctxt)
                        if prev:
                            rest(t - 1, 1 - s, n)
                    squares(t, s)

                modulate(0, 0, 0)
                act.wait_ge(w_sem, 16 * 5)
                pipelined(act, body)
                for part in range(1, 4):
                    rest(NT - 1, (NT - 1) % 2, part)

            @block.gpsimd
            def _(pool):
                pool.memset(neg_half[:, :], -0.5).then_inc(half_rdy, 1)
                pool.memset(zero_row[:, :], 0.0).then_inc(half_rdy, 1)
                pool.wait_ge(half_rdy, 2)
                pool.sem_inc(rs_rdy, 1)
                if l == 0:
                    for b in range(MAX_OVER):
                        pool.dma_start(
                            io["ys"][(NE + b) * P:(NE + b + 1) * P, :].rearrange("p (a n) -> p a n", n=CONV),
                            zero_row[:, :].unsqueeze(1).broadcast_to([P, D // CONV, CONV])).then_inc(ys_zeroed, 16)

                def head(t, s, r):
                    pool.wait_ge(u_rdy, t * 5 + 10)
                    pool.wait_ge(q_out[s], r * 32 + 32)
                    pool.tensor_tensor(zc[s][:, :], u[s][:, 0:CONV], u[s][:, CONV:2 * CONV],
                                       ALU.mult).then_inc(zc_rdy, 1)
                    pool.wait_ge(a_step, t * A_STEPS + VAR_STEP)
                    pool.tensor_tensor(rs[:, :], ss[:, :], neg_half[:, :], ALU.pow).then_inc(rs_rdy, 1)

                in_pairs(pool, NT, head)
                if l == 0:
                    pool.wait_ge(ys_zeroed, 16 * MAX_OVER)

            @block.vector
            def _(dve):
                dve.sem_inc(b_done, 2)
                sa, sbb = Steps(dve, a_step, A_STEPS), Steps(dve, b_step, 1)

                def rotate(z, n, w, t, steps):
                    q = w // 4
                    at = 0 if w == 32 else 64
                    cos = rope[:, bass.ds(t, 1), at:at + w].broadcast_to([P, n, w])
                    sin = rope[:, bass.ds(t, 1), at + w:at + 2 * w]
                    dve.tensor_tensor(t1[:, 0:n * w].rearrange("p (h w) -> p h w", h=n), z, cos, ALU.mult)
                    sin4 = sin.rearrange("p h (a b q) -> p h a b q", a=2, b=2)
                    out5 = t2[:, 0:n * w].rearrange("p (h a b q) -> p h a b q", a=2, b=2, q=q)
                    z5 = z.rearrange("p h (a b q) -> p h a b q", a=2, b=2)
                    for b in range(2):
                        last = dve.tensor_tensor(out5[:, :, :, b, :], z5[:, :, :, 1 - b, :],
                                                 sin4[:, :, :, b, :].broadcast_to([P, n, 2, q]), ALU.mult)
                    steps.after(last)

                def modulate(t, s, ctxt):
                    dve.wait_ge(xT_ps, t + 1)
                    for k in range(KD // 2, KD):
                        op = dve.tensor_scalar(hT[s][:, k, :], ps[:, 2560 + k * P:2560 + (k + 1) * P],
                                               keep["scale1"][:, k, ctxt:ctxt + 1],
                                               keep["shift1"][:, k, ctxt:ctxt + 1], ALU.mult, ALU.add)
                    op.then_inc(hT_rdy, 1)

                def head(t, s, r):
                    sa.begin(t)
                    dve.wait_ge(b_done, t + 2)
                    dve.wait_ge(u_rdy, t * 5 + 10)
                    gqk = u[s][:, U_GQ:U_GQ + 384]
                    sa.after(dve.scalar_tensor_tensor(t1[:, 0:384], gqk, 1.0 / HD, gqk, ALU.mult, ALU.mult))
                    sa.after(dve.tensor_reduce(ss[:, 2:8], t1[:, 0:384].rearrange("p (h n) -> p h n", n=HD), AX_X,
                                               ALU.add))
                    dve.wait_ge(sq_rdy, t * 2 + 2)
                    sa.after(dve.tensor_scalar(ss[:, :], ss[:, :], EPS, None, ALU.add))
                    dve.tensor_tensor(gqk, gqk, qk_gain[:, :], ALU.mult)
                    z = u[s][:, U_DQ:U_DQ + 512].rearrange("p (h w) -> p h w", w=32)
                    rotate(z, 16, 32, t, sa)
                    dve.wait_ge(q_out[s], r * 32 + 32)
                    dve.tensor_tensor(qrow[s][:, QD:QD + 256], t1[:, 0:256], t2[:, 0:256], ALU.add)
                    sa.after(dve.tensor_tensor(kdg[s][:, 0:256], t1[:, 256:512], t2[:, 256:512], ALU.add))
                    z = u[s][:, U_KR:U_KR + 32].rearrange("p (h w) -> p h w", w=32)
                    rotate(z, 1, 32, t, sa)
                    dve.wait_ge(kmT_rdy, t + 1)
                    sa.after(dve.tensor_tensor(ka[s][:, :, MLA_NOPE:MLA_QK],
                                               t1[:, 0:32].unsqueeze(1).broadcast_to([P, MLA_H, 32]),
                                               t2[:, 0:32].unsqueeze(1).broadcast_to([P, MLA_H, 32]), ALU.add))
                    dve.wait_ge(rs_rdy, t + 2)
                    for a, b, j in ((U_CQ, U_CQ + 256, 0), (U_CKV, U_CKV + 128, 1)):
                        dve.tensor_scalar(u[s][:, a:b], u[s][:, a:b], rs[:, j:j + 1], None, ALU.mult)
                    g3 = gqk.rearrange("p (h n) -> p h n", n=HD)
                    sa.after(dve.tensor_tensor(g3, g3, rs[:, 2:8].unsqueeze(2).broadcast_to([P, 6, HD]), ALU.mult))
                    rotate(g3, 6, 64, t, sa)
                    dve.tensor_tensor(qrow[s][:, QG:QG + 256].rearrange("p (g k n) -> p k g n", g=2, k=2),
                                      t1[:, 0:256].rearrange("p (k g n) -> p k g n", g=2, k=2),
                                      t2[:, 0:256].rearrange("p (k g n) -> p k g n", g=2, k=2), ALU.add)
                    sa.after(dve.tensor_tensor(kdg[s][:, 256:384], t1[:, 256:384], t2[:, 256:384], ALU.add))
                    sa.end()

                def tail(t, s):
                    sbb.begin(t)
                    dve.wait_ge(q_rdy, t + 1)
                    z = qrow[s][:, 0:384].rearrange("p (h w) -> p h w", w=MLA_QK)[:, :, MLA_NOPE:MLA_QK]
                    rotate(z, 4, 32, t, sbb)
                    dve.tensor_tensor(z, t1[:, 0:128].rearrange("p (h w) -> p h w", w=32),
                                      t2[:, 0:128].rearrange("p (h w) -> p h w", w=32), ALU.add).then_inc(b_done, 1)
                    sbb.end()

                def body(t, s, r, prev, nxt, ctxt):
                    if prev:
                        head(t - 1, 1 - s, r - 1 + s)
                    if nxt:
                        modulate(t + 1, 1 - s, ctxt)
                    if prev:
                        tail(t - 1, 1 - s)

                modulate(0, 0, 0)
                dve.wait_ge(w_sem, 16 * 5)
                pipelined(dve, body)
                head(NT - 1, (NT - 1) % 2, NT // 2 - 1)
                tail(NT - 1, (NT - 1) % 2)


def layer_norm_steps(dve, st, z, stats, mv, tick, eps_step):
    for j in range(2):
        op = dve.bn_stats(stats[:, j, :], z[:, j * 512:(j + 1) * 512])
    st.after(op)
    dve.memset(tick[:, :], 0.0)
    st.after(dve.bn_aggr(mv[:, :], stats[:, :, :]))
    eps_step(dve.tensor_scalar(mv[:, 1:2], mv[:, 1:2], EPS, None, ALU.add))


ITEMS = []
for _h in range(4):
    ITEMS += [("diff", _h, [3 * _h, 3 * _h + 1]), ("mla", _h, [3 * _h + 2])]
ITEMS += [("gqa", _h, [12 + _h]) for _h in range(4)]
ITEM_OF = {u: n for n, (_, _, us) in enumerate(ITEMS) for u in us}
NI, NU = len(ITEMS), 16
TRANSPOSE_IN = {3: 0, 5: 1, 7: 2, 8: 3, 10: 4, 11: 5, 13: 6, 14: 7, 15: 8}
TRANSPOSE_LATE = {0: 9, 1: 10, 2: 11}
VALUES_IN = {6: 0, 7: 1, 8: 2, 9: 3, 11: 4, 12: 5, 14: 6, 15: 7}
VALUES_LATE = {0: 8, 1: 9, 2: 10, 3: 11}
BACK_IN = {u + 1: n for u, n in VALUES_IN.items() if u + 1 < NU}
BACK_LATE = {0: 7, 1: 8, 2: 9, 3: 10, 4: 11}
Y_SLOT, WO_SLOTS, Q_SLOTS = 4, (4, 5), (6, 9)
LN_SLOTS = (6, 7, 8, 9, 10)


def tile_bodies(eng, n, body):
    body(0, 0, 0, True, False, True)
    if n > 2:
        with eng.Fori(0, n // 2 - 1) as r:
            body(r * 2 + 1, 1, r, True, True, True)
            body(r * 2 + 2, 0, r + 1, True, True, True)
    body(n - 1, 1, n // 2 - 1, True, True, False)
    body(n, 0, n // 2, False, True, False)


def attend(nc, l, io, c, kv, stream):
    t0 = 0 if stream == 0 else NT_LAT
    n_tiles = NT_LAT if stream == 0 else NT_CTX
    key_tiles = list(range(NT)) if stream == 0 else list(range(NT_LAT, NT))
    k0, nk = key_tiles[0] * P, len(key_tiles) * P
    chunks = [key_tiles[a:a + 4] for a in range(0, len(key_tiles), 4)]
    nch = len(chunks)
    NCHT = NI * nch
    S_AT, T_AT, O_AT = [0, 1536], 3072, 3584
    SCALE = {"mla": MLA_SCALE, "diff": DIFF_SCALE, "gqa": GQA_SCALE}
    lam_init = 0.8 - 0.6 * math.exp(-0.3 * l)
    OWN = NU + 2 * DIFF_H + 3 + 2
    LATE = 5 + 2 + 1 + 2 + 2
    x_src = io["x_in"] if l == 0 else io["x_mid"]

    ctx = ExitStack()
    sb = lambda n, s, d=F32: ctx.enter_context(nc.sbuf_tensor(f"at_{n}_{l}{stream}", s, d))
    sem = phase_semaphores(nc, ctx, lambda n: f"at_{n}_{l}{stream}")
    with ctx:
        w_out = sb("w_out", [P, KD, D])
        gate1, scale2, shift2 = sb("gate1", [P, D]), sb("scale2", [P, D]), sb("shift2", [P, D])
        ln_g, ln_b = sb("ln_g", [P, D]), sb("ln_b", [P, D])
        conv_w = sb("conv_w", [P, 3, CONV])
        dl = sb("dl", [P, 4, 32])
        dlp = sb("dlp", [P, 2, 32])
        dle = sb("dle", [P, 2])
        neg_lam = sb("neg_lam", [P, 1])
        subln = sb("subln", [P, HD])
        neg_half = sb("neg_half", [P, 4])
        qin = [sb(f"qin{j}", [P, Q_W]) for j in range(2)]
        zin = [sb(f"zin{j}", [P, 3, CONV]) for j in range(2)]
        xin = [sb(f"xin{j}", [P, D]) for j in range(2)]
        qT = [sb(f"qT{j}", [P, 8, P]) for j in range(2)]
        prob = [sb(f"prob{j}", [P, nk]) for j in range(4)]
        pT = [sb(f"pT{j}", [P, nk]) for j in range(2)]
        y = [sb(f"y{j}", [P, D]) for j in range(2)]
        oT = sb("oT", [HD, P])
        yT = sb("yT", [P, KD, P])
        z = sb("z", [P, D])
        x1 = [sb(f"x1{j}", [P, D]) for j in range(2)]
        h2 = sb("h2", [P, D])
        mx, nm, rs, ri = sb("mx", [P, NU]), sb("nm", [P, NU]), sb("rs", [P, NU]), sb("ri", [P, NU])
        coef = sb("coef", [P, DIFF_H])
        dsq = z[:, 0:DIFF_H * HD]
        dss, drs = sb("dss", [P, 4]), sb("drs", [P, 4])
        stats, mv, rstd = sb("stats", [P, 2, 6]), sb("mv", [P, 2]), sb("rstd", [P, 1])
        tick = sb("tick", [P, 1])
        ps, ident = c["ps"], c["ident"]
        w_sem, w_out_in = sem("weights_in"), sem("w_out_in")
        q_in = [sem(f"q_in{j}") for j in range(2)]
        x_in = [sem(f"x_in{j}") for j in range(2)]
        x1_out = [sem(f"x1_out{j}") for j in range(2)]
        h_out = sem("h_out")
        setup, lam_exp, lam_rdy, half_rdy = sem("setup"), sem("lam_exp"), sem("lam_rdy"), sem("half_rdy")
        qT_ps, qT_rdy, s_rdy, m_rdy, exp_done, comb_done = (
            sem("qT_ps"), sem("qT_rdy"), sem("s_rdy"), sem("m_rdy"), sem("exp_done"), sem("comb_done"))
        t_ps, t_ev, pv_done, oT_rdy, back_ps, o_ev = (
            sem("t_ps"), sem("t_ev"), sem("pv_done"), sem("oT_rdy"), sem("back_ps"), sem("o_ev"))
        own, late, dvar_rdy, drs_rdy, y_rdy, conv_rdy, conv_step = (
            sem("own"), sem("late"), sem("dvar_rdy"), sem("drs_rdy"), sem("y_rdy"), sem("conv_rdy"), sem("conv_step"))
        yT_ps, yT_rdy, wo_ps, z_read, var_rdy, rstd_rdy, x1_rdy, h_step, h_rdy = (
            sem("yT_ps"), sem("yT_rdy"), sem("wo_ps"), sem("z_read"), sem("var_rdy"), sem("rstd_rdy"),
            sem("x1_rdy"), sem("h_step"), sem("h_rdy"))

        def row(t):
            return bass.ds(t * P + t0 * P, P)

        with nc.Block() as block:
            @block.sync
            def _(sp):
                def load_q(t, s):
                    z0 = t * P + (t0 * P + 1 + stream)
                    sp.dma_start(qin[s][:, :], io["qrow"][row(t), :]).then_inc(q_in[s], 16)
                    for j in range(3):
                        sp.dma_start(zin[s][:, j, :], io["zc"][bass.ds(z0 + j - 1, P), :]).then_inc(q_in[s], 16)

                def load_x(t, s):
                    sp.dma_start(xin[s][:, :], x_src[row(t), :]).then_inc(x_in[s], 16)

                def body(t, s, more_q, more_x):
                    if more_q:
                        sp.wait_ge(conv_rdy, t + 1)
                        sp.wait_ge(qT_ps, t * 2 + 2)
                        load_q(t + 2, s)
                    if not isinstance(t, int) or t > 0:
                        sp.wait_ge(x1_rdy, t)
                        sp.dma_start(io["x_post"][row(t - 1), :], x1[1 - s][:, :]).then_inc(x1_out[1 - s], 16)
                        sp.wait_ge(h_rdy, t)
                        sp.dma_start(io["h2"][row(t - 1), :], h2[:, :]).then_inc(h_out, 16)
                    if more_x:
                        load_x(t + 1, 1 - s)

                for s in range(2):
                    sp.sem_inc(x1_out[s], 16)
                sp.sem_inc(h_out, 16)
                load_q(0, 0)
                mod = lambda v: io["mod"][l, stream:stream + 1, v * D:(v + 1) * D].broadcast_to([P, D])
                for dst, src in ((gate1, mod(2)), (shift2, mod(3)), (scale2, mod(4)),
                                 (ln_g, io["ln"][l, 0:1, :].broadcast_to([P, D])),
                                 (ln_b, io["ln"][l, 1:2, :].broadcast_to([P, D])),
                                 (subln, io["subln"][l:l + 1, :].broadcast_to([P, HD]))):
                    sp.dma_start(dst[:, :], src).then_inc(w_sem, 16)
                sp.dma_start(conv_w[:, :, :].rearrange("p j n -> p (j n)"),
                             io["conv_w"][l:l + 1, :].broadcast_to([P, 3 * CONV])).then_inc(w_sem, 16)
                sp.dma_start(dl[:, :, :].rearrange("p j n -> p (j n)"),
                             io["lambda"][l:l + 1, :].broadcast_to([P, P])).then_inc(w_sem, 16)
                load_q(1, 1)
                load_x(0, 0)
                load_x(1, 1)
                sp.dma_start(w_out[:, :, :], io["w_out"][l]).then_inc(w_out_in, 16)
                body(0, 0, n_tiles > 2, False)
                if n_tiles > 2:
                    with sp.Fori(0, n_tiles // 2 - 2) as r:
                        body(r * 2 + 1, 1, True, True)
                        body(r * 2 + 2, 0, True, True)
                    for t in range(n_tiles - 3, n_tiles - 1):
                        body(t, t % 2, t + 2 < n_tiles, True)
                body(n_tiles - 1, 1, False, False)
                body(n_tiles, 0, False, False)
                for s in range(2):
                    sp.wait_ge(x1_out[s], 16 + 16 * (n_tiles // 2))
                sp.wait_ge(h_out, 16 + 16 * n_tiles)

            @block.tensor
            def _(pe):
                def scores(u, s):
                    kind, h, us = ITEMS[ITEM_OF[u]]
                    if kind == "mla":
                        q, kk = qT[s][0:MLA_QK, h, :], kv["km"][0:MLA_QK, h, :]
                    elif kind == "diff":
                        m = 2 * h + us.index(u)
                        b = 32 * (m % 4)
                        q, kk = qT[s][b:b + 32, 4 + m // 4, :], kv["kd"][b:b + 32, m // 4, :]
                    else:
                        b = 64 * (h // 2)
                        q, kk = qT[s][b:b + 64, 6 + h % 2, :], kv["kg"][b:b + 64, :]
                    at = S_AT[u % 2]

                    def bank(a):
                        e = min(a + 512, nk)
                        mm = pe.matmul(ps[:, at + a:at + e], q, kk[:, k0 + a:k0 + e], start=True, stop=True)
                        if e == nk:
                            mm.then_inc(s_rdy, 1)

                    return [lambda a=a: bank(a) for a in range(0, nk, 512)]

                def transposes(t, n, after):
                    kind, h, us = ITEMS[n]

                    def chunk(ci):
                        if ci == 0:
                            if kind == "diff":
                                pe.wait_ge(comb_done, t * DIFF_H + h + 1)
                            else:
                                pe.wait_ge(exp_done, t * NU + us[0] + 1)
                            after()
                        pe.wait_ge(t_ev, t * NCHT + n * nch + ci + 1)
                        for j in range(len(chunks[ci])):
                            a = (ci * 4 + j) * P
                            tr = pe.transpose(ps[:, T_AT + j * P:T_AT + (j + 1) * P], prob[us[0] % 4][:, a:a + P],
                                              ident[:, :])
                        tr.then_inc(t_ps, 1)

                    return [lambda ci=ci: chunk(ci) for ci in range(nch)]

                def values(t, n):
                    kind, h, us = ITEMS[n]
                    vt, vc = {"mla": (kv["vm"], h * 64), "diff": (kv["vd"], h * 64), "gqa": (kv["vg"], (h // 2) * 64)}[kind]
                    pe.wait_ge(o_ev, t * NI + n + 1)
                    for ci in range(nch):
                        pe.wait_ge(t_ev, t * NCHT + n * nch + ci + 2)
                        for j, kt in enumerate(chunks[ci]):
                            k = ci * 4 + j
                            mm = pe.matmul(ps[0:HD, O_AT:O_AT + P], vt[:, kt, vc:vc + HD],
                                           pT[n % 2][:, k * P:(k + 1) * P], start=(k == 0),
                                           stop=(k == len(key_tiles) - 1))
                    mm.then_inc(pv_done, 1)

                def turn_back(t, n):
                    pe.wait_ge(oT_rdy, t * NI + n + 1)
                    pe.matmul(ps[:, O_AT + P:O_AT + P + HD], oT[:, :], ident[0:HD, 0:HD], start=True,
                              stop=True).then_inc(back_ps, 1)

                def y_part(t, s, part, own):
                    if part == 0:
                        pe.wait_ge(conv_rdy, t + 1)
                        pe.wait_ge(y_rdy, t + 1)
                        pe.wait_ge(t_ev, (t + 1) * NCHT + (nch if own else 0) + 1)
                    else:
                        pe.wait_ge(yT_rdy, t * 2 + 1)
                    for j in range(4):
                        k = part * 4 + j
                        tr = pe.transpose(ps[:, T_AT + j * P:T_AT + (j + 1) * P], y[s][:, k * P:(k + 1) * P],
                                          ident[:, :])
                    tr.then_inc(yT_ps, 1)

                def q_part(t, s, r, part):
                    pe.wait_ge(q_in[s], r * 64 + 64)
                    for j in range(4):
                        w = P if part else MLA_QK
                        a = QD + j * P if part else j * MLA_QK
                        tr = pe.transpose(ps[0:w, T_AT + j * P:T_AT + (j + 1) * P], qin[s][:, a:a + w], ident[:, :])
                    tr.then_inc(qT_ps, 1)

                def project_out(t, half):
                    if half == 0:
                        pe.wait_ge(o_ev, (t + 1) * NI + 1)
                        pe.wait_ge(yT_rdy, t * 2 + 2)
                    else:
                        pe.wait_ge(z_read, t * 2 + 1)
                    for k in range(KD):
                        mm = pe.matmul(ps[:, O_AT:O_AT + 512], yT[:, k, :], w_out[:, k, half * 512:(half + 1) * 512],
                                       start=(k == 0), stop=(k == KD - 1))
                    mm.then_inc(wo_ps, 1)

                def body(t, s, r, cur, prev, nxt):
                    if cur:
                        pe.wait_ge(qT_rdy, t * 2 + 2)
                    for u in range(NU if cur else WO_SLOTS[-1] + 1):
                        qk = scores(u, s) if cur else []
                        if cur and (u >= 2 or prev):
                            pe.wait_ge(exp_done, t * NU + u - 1)
                        tr = []
                        if cur and u in TRANSPOSE_IN:
                            def after(u=u):
                                if TRANSPOSE_IN[u] == 1 and prev:
                                    pe.wait_ge(yT_rdy, t * 2)
                                for part in range(2):
                                    if nxt and u == Q_SLOTS[part] + 1:
                                        pe.wait_ge(qT_rdy, t * 2 + 3 + part)
                            tr = transposes(t, TRANSPOSE_IN[u], after)
                        if prev and u in TRANSPOSE_LATE:
                            tr = transposes(t - 1, TRANSPOSE_LATE[u], lambda: None)
                        if prev and u == Y_SLOT:
                            tr = [lambda p=p: y_part(t - 1, 1 - s, p, cur) for p in range(2)]
                        late_back = prev and u in BACK_LATE
                        back = cur and u in BACK_IN
                        for i in range(max(len(qk), len(tr), 1)):
                            if i == (0 if len(qk) < 2 or u == Y_SLOT else 1):
                                if late_back:
                                    turn_back(t - 1, BACK_LATE[u])
                                if back:
                                    turn_back(t, BACK_IN[u])
                                late_back = back = False
                            if i < len(qk):
                                qk[i]()
                            if i < len(tr):
                                tr[i]()
                        assert not late_back and not back
                        if prev and u in VALUES_LATE:
                            values(t - 1, VALUES_LATE[u])
                        if cur and u in VALUES_IN:
                            if VALUES_IN[u] == 0 and prev:
                                pe.wait_ge(z_read, t * 2)
                            values(t, VALUES_IN[u])
                        if prev and u in WO_SLOTS:
                            project_out(t - 1, WO_SLOTS.index(u))
                        if nxt and u in Q_SLOTS:
                            part = Q_SLOTS.index(u)
                            n = max(TRANSPOSE_IN[v] for v in TRANSPOSE_IN if v <= u)
                            pe.wait_ge(t_ev, t * NCHT + (n + 1) * nch + 1)
                            q_part(t + 1, 1 - s, r + (1 if s else 0), part)

                q_part(0, 0, 0, 0)
                pe.wait_ge(qT_rdy, 1)
                q_part(0, 0, 0, 1)
                pe.wait_ge(w_out_in, 16)
                tile_bodies(pe, n_tiles, body)

            @block.scalar
            def _(act):
                act.sem_inc(t_ev, 1)
                act.wait_ge(setup, 2)
                act.activation(dle[:, :], dle[:, :], ACT.Exp).then_inc(lam_exp, 1)

                def read_q(t, s, part):
                    act.wait_ge(qT_ps, t * 2 + 1 + part)
                    w = P if part else MLA_QK
                    act.copy(qT[s][0:w, part * 4:part * 4 + 4, :],
                             ps[0:w, T_AT:T_AT + 512].rearrange("p (j n) -> p j n", j=4)).then_inc(qT_rdy, 1)

                def read_output(t, n):
                    act.wait_ge(pv_done, t * NI + n + 1)
                    act.copy(oT[:, :], ps[0:HD, O_AT:O_AT + P]).then_inc(oT_rdy, 1)

                def read_probs(t, n, may_wait):
                    for ci in range(nch):
                        if ci == 0 and may_wait:
                            act.wait_ge(pv_done, t * NI + n - 1)
                        act.wait_ge(t_ps, t * NCHT + n * nch + ci + 1)
                        w = len(chunks[ci]) * P
                        act.copy(pT[n % 2][:, ci * 512:ci * 512 + w], ps[:, T_AT:T_AT + w]).then_inc(t_ev, 1)

                def body(t, s, r, cur, prev, nxt):
                    for u in range(NU if cur else WO_SLOTS[-1] + 1):
                        if prev and u in BACK_LATE:
                            read_output(t - 1, BACK_LATE[u])
                        if cur and u in BACK_IN:
                            read_output(t, BACK_IN[u])
                        if cur and u in TRANSPOSE_IN:
                            n = TRANSPOSE_IN[u]
                            read_probs(t, n, n >= 2 or prev)
                        if prev and u in TRANSPOSE_LATE:
                            read_probs(t - 1, TRANSPOSE_LATE[u], True)
                        if prev and u == Y_SLOT:
                            for part in range(2):
                                act.wait_ge(yT_ps, t * 2 - 1 + part)
                                act.copy(yT[:, part * 4:part * 4 + 4, :],
                                         ps[:, T_AT:T_AT + 512].rearrange("p (j n) -> p j n", j=4)).then_inc(yT_rdy, 1)
                        if cur:
                            kind = ITEMS[ITEM_OF[u]][0]
                            act.wait_ge(m_rdy, t * NU + u + 1)
                            at = S_AT[u % 2]
                            act.activation(prob[u % 4][:, :], ps[:, at:at + nk], ACT.Exp, bias=nm[:, u:u + 1],
                                           scale=SCALE[kind], accum_out=rs[:, u:u + 1]).then_inc(exp_done, 1)
                        if nxt and u in Q_SLOTS:
                            read_q(t + 1, 1 - s, Q_SLOTS.index(u))

                read_q(0, 0, 0)
                read_q(0, 0, 1)
                tile_bodies(act, n_tiles, body)

            @block.vector
            def _(dve):
                dve.sem_inc(o_ev, 1)
                dve.wait_ge(w_sem, 16 * 8)
                dve.tensor_tensor(dlp[:, 0, :], dl[:, 0, :], dl[:, 1, :], ALU.mult)
                dve.tensor_tensor(dlp[:, 1, :], dl[:, 2, :], dl[:, 3, :], ALU.mult).then_inc(setup, 1)
                dve.wait_ge(setup, 1)
                dve.tensor_reduce(dle[:, :], dlp[:, :, :], AX_X, ALU.add).then_inc(setup, 1)
                dve.tensor_scalar(subln[:, :], subln[:, :], 1.0 - lam_init, None, ALU.mult)
                dve.tensor_scalar(scale2[:, :], scale2[:, :], 1.0, None, ALU.add).then_inc(lam_rdy, 1)
                dve.wait_ge(lam_exp, 1)
                dve.tensor_tensor(neg_lam[:, :], dle[:, 1:2], dle[:, 0:1], ALU.subtract).then_inc(lam_rdy, 1)
                dve.wait_ge(lam_rdy, 2)
                dve.tensor_scalar(neg_lam[:, :], neg_lam[:, :], -lam_init, None, ALU.add).then_inc(lam_rdy, 1)
                dve.wait_ge(lam_rdy, 3)
                so, sl = Steps(dve, own, OWN), Steps(dve, late, LATE)

                def maximum(t, u):
                    kind, h, us = ITEMS[ITEM_OF[u]]
                    dve.wait_ge(s_rdy, t * NU + u + 1)
                    at = S_AT[u % 2]
                    so.after(dve.tensor_reduce(mx[:, u:u + 1], ps[:, at:at + nk], AX_X, ALU.max))
                    dve.tensor_scalar(nm[:, u:u + 1], mx[:, u:u + 1], -SCALE[kind], None, ALU.mult).then_inc(m_rdy, 1)
                    if kind == "diff" and u == us[1]:
                        dve.wait_ge(exp_done, t * NU + u + 1)
                        u = us[0]
                        so.after(dve.reciprocal(ri[:, u:u + 2], rs[:, u:u + 2]))
                        so.after(dve.tensor_scalar(coef[:, h:h + 1], ri[:, u + 1:u + 2], rs[:, u:u + 1], neg_lam[:, :],
                                                   ALU.mult, ALU.mult))
                        p0, p1 = prob[u % 4], prob[(u + 1) % 4]
                        dve.scalar_tensor_tensor(p0[:, :], p1[:, :], coef[:, h:h + 1], p0[:, :], ALU.mult,
                                                 ALU.add).then_inc(comb_done, 1)

                def output(t, s, n, st):
                    kind, h, us = ITEMS[n]
                    u = us[0]
                    if kind != "diff":
                        dve.wait_ge(exp_done, t * NU + u + 1)
                        st.after(dve.reciprocal(ri[:, u:u + 1], rs[:, u:u + 1]))
                    dve.wait_ge(back_ps, t * NI + n + 1)
                    col = {"mla": 256, "diff": 512, "gqa": 768}[kind] + h * 64
                    o = O_AT + P
                    dve.tensor_scalar(y[s][:, col:col + HD], ps[:, o:o + HD], ri[:, u:u + 1], None,
                                      ALU.mult).then_inc(o_ev, 1)

                def diff_squares(t, s):
                    dve.wait_ge(o_ev, t * NI + 7 + 1)
                    so.after(dve.scalar_tensor_tensor(dsq, y[s][:, 512:768], 1.0 / HD, y[s][:, 512:768],
                                                      ALU.mult, ALU.mult))
                    so.after(dve.tensor_reduce(dss[:, :], dsq.rearrange("p (h n) -> p h n", n=HD), AX_X, ALU.add))
                    dve.tensor_scalar(dss[:, :], dss[:, :], EPS, None, ALU.add).then_inc(dvar_rdy, 1)

                def diff_norm(t, s):
                    yd = y[s][:, 512:768].rearrange("p (h n) -> p h n", n=HD)
                    dve.wait_ge(drs_rdy, t + 1)
                    sl.after(dve.tensor_tensor(yd, yd, drs[:, :].unsqueeze(2).broadcast_to([P, 4, HD]), ALU.mult))
                    sl.after(dve.tensor_tensor(yd, yd, subln[:, :].unsqueeze(1).broadcast_to([P, 4, HD]), ALU.mult))

                def read_projection(t, half):
                    dve.wait_ge(wo_ps, t * 2 + 1 + half)
                    a = half * 512
                    dve.tensor_tensor(z[:, a:a + 512], ps[:, O_AT:O_AT + 512], gate1[:, a:a + 512],
                                      ALU.mult).then_inc(z_read, 1)

                def norm_part(t, s, r, part):
                    if part == 0:
                        dve.wait_ge(x_in[s], r * 16 + 16)
                        dve.wait_ge(z_read, t * 2 + 2)
                        sl.after(dve.scalar_tensor_tensor(z[:, :], xin[s][:, :], ALPHA, z[:, :], ALU.mult, ALU.add))
                    elif part == 1:
                        layer_norm_steps(dve, sl, z, stats, mv, tick, lambda op: op.then_inc(var_rdy, 1))
                    elif part == 2:
                        dve.wait_ge(rstd_rdy, t + 1)
                        sl.after(dve.tensor_scalar(z[:, :], z[:, :], mv[:, 0:1], rstd[:, :], ALU.subtract, ALU.mult))
                    elif part == 3:
                        sl.after(dve.tensor_tensor(z[:, :], z[:, :], ln_g[:, :], ALU.mult))
                    else:
                        dve.wait_ge(x1_out[s], r * 16 + 16)
                        dve.tensor_tensor(x1[s][:, :], z[:, :], ln_b[:, :], ALU.add).then_inc(x1_rdy, 1)
                        dve.wait_ge(x1_rdy, t + 1)

                def body(t, s, r, cur, prev, nxt):
                    rp = r if s else r - 1
                    if cur:
                        so.begin(t)
                    if prev:
                        sl.begin(t - 1)
                    for u in range(NU if cur else LN_SLOTS[-1] + 1):
                        if prev and u in BACK_LATE:
                            output(t - 1, 1 - s, BACK_LATE[u], sl)
                            if u == Y_SLOT - 2:
                                diff_norm(t - 1, 1 - s)
                            if u == Y_SLOT:
                                dve.wait_ge(o_ev, t * NI + 1)
                                dve.sem_inc(y_rdy, 1)
                        if cur and u in BACK_IN:
                            output(t, s, BACK_IN[u], so)
                        if cur:
                            maximum(t, u)
                        if prev:
                            if u in WO_SLOTS:
                                read_projection(t - 1, WO_SLOTS.index(u))
                            if u in LN_SLOTS:
                                norm_part(t - 1, 1 - s, rp, LN_SLOTS.index(u))
                        if cur and u == NU - 1:
                            diff_squares(t, s)
                    if cur:
                        so.end()
                    if prev:
                        sl.end()

                tile_bodies(dve, n_tiles, body)

            @block.gpsimd
            def _(pool):
                pool.memset(neg_half[:, :], -0.5).then_inc(half_rdy, 1)
                pool.wait_ge(half_rdy, 1)
                pool.wait_ge(w_sem, 16 * 8)
                pool.wait_ge(lam_rdy, 1)

                def body(t, s, r, cur, prev, nxt):
                    if prev:
                        pool.wait_ge(dvar_rdy, t)
                        pool.tensor_tensor(drs[:, :], dss[:, :], neg_half[:, :], ALU.pow).then_inc(drs_rdy, 1)
                    if cur:
                        cv = zin[s]
                        pool.wait_ge(q_in[s], r * 64 + 64)
                        pool.tensor_tensor(cv[:, :, :], zin[s][:, :, :], conv_w[:, :, :],
                                           ALU.mult).then_inc(conv_step, 1)
                        pool.wait_ge(conv_step, t * 3 + 1)
                        pool.tensor_tensor(cv[:, 0, :], cv[:, 0, :], cv[:, 1, :], ALU.add).then_inc(conv_step, 1)
                        pool.wait_ge(conv_step, t * 3 + 2)
                        pool.tensor_tensor(cv[:, 0, :], cv[:, 0, :], cv[:, 2, :], ALU.add).then_inc(conv_step, 1)
                        pool.wait_ge(conv_step, t * 3 + 3)
                        pool.tensor_tensor(y[s][:, 0:CONV], cv[:, 0, :], qin[s][:, QB:QB + CONV],
                                           ALU.mult).then_inc(conv_rdy, 1)
                    if prev:
                        pool.wait_ge(var_rdy, t)
                        pool.tensor_tensor(rstd[:, :], mv[:, 1:2], neg_half[:, 0:1], ALU.pow).then_inc(rstd_rdy, 1)
                        pool.wait_ge(x1_rdy, t)
                        pool.wait_ge(h_out, t * 16)
                        pool.tensor_tensor(h2[:, :], x1[1 - s][:, :], scale2[:, :], ALU.mult).then_inc(h_step, 1)
                        pool.wait_ge(h_step, t)
                        pool.tensor_tensor(h2[:, :], h2[:, :], shift2[:, :], ALU.add).then_inc(h_rdy, 1)

                tile_bodies(pool, n_tiles, body)


def experts(nc, l, io, c):
    nt = NT if l < DEPTH - 1 else NT_LAT
    n_over = (2 * nt * P - 1) // P
    NBLK = NE + n_over
    HT_AT, LG_AT, RK_AT, CNT_AT, IX_AT = 0, 1024, 1536, 1536 + 384, 2048
    UP_AT, GT_AT, HM_AT, DN_AT = [0, 512], 1024, 2048, 2560
    W_RING = 3
    BIG = 3.0e38

    ctx = ExitStack()
    sb = lambda n, s, d=F32: ctx.enter_context(nc.sbuf_tensor(f"ex_{n}_{l}", s, d))
    sem = phase_semaphores(nc, ctx, lambda n: f"ex_{n}_{l}")
    with ctx:
        w13 = [sb(f"w13{j}", [P, KD, 2 * DE]) for j in range(W_RING)]
        w2 = [sb(f"w2{j}", [P, 2, D]) for j in range(W_RING)]
        w_route, b_route = sb("w_route", [P, KD, 36]), sb("b_route", [P, 36])
        before, ones = sb("before", [P, P]), sb("ones", [P, P])
        iota, token = sb("iota", [P, P]), sb("token", [P, NT])
        hx = [sb(f"hx{j}", [P, D]) for j in range(2)]
        hT = sb("hT", [P, KD, P])
        lg = sb("lg", [P, nt, 36])
        small = lambda n, w=nt: sb(n, [P, w])
        gmax, gsum, gi, m0, m1, i0, i1, e1 = [small(n) for n in ("gmax", "gsum", "gi", "m0", "m1", "i0", "i1", "e1")]
        g4, og = sb("g4", [P, nt, 4]), sb("og", [P, nt, 4])
        s84 = sb("s84", [P, nt, EPG, NG])
        s8, o8 = sb("s8", [P, nt, EPG]), sb("o8", [P, nt, EPG])
        ek, rk, blk, over, rmod = [small(n, 2 * nt) for n in ("ek", "rk", "blk", "over", "rmod")]
        rki = sb("rki", [P, 2 * nt], I32)
        member, mprod = sb("member", [P, 2 * nt, NE]), sb("mprod", [P, 2 * nt, NE])
        msum, cum, rank = sb("msum", [P, nt, NE]), sb("cum", [P, nt + 1, NE]), sb("rank", [P, nt, NE])
        cnt, ov, oe0, oe1 = small("cnt", NE), small("ov", NE), small("oe0", NE), small("oe1", NE)
        cnti = sb("cnti", [P, NE], I32)
        a_oh = [sb(f"a_oh{j}", [P, P]) for j in range(2)]
        b_oh = [sb(f"b_oh{j}", [P, NBLK]) for j in range(2)]
        idx = sb("idx", [P, NBLK], I32)
        ovc = sb("ovc", [1, n_over, NE])
        ovf = sb("ovf", [1, n_over + 1])
        ovi = sb("ovi", [1, n_over + 1], I32)
        xg = [sb(f"xg{j}", [P, D]) for j in range(2)]
        xgT = [sb(f"xgT{j}", [P, KD, P]) for j in range(2)]
        act1 = [sb(f"act1{j}", [P, DE]) for j in range(2)]
        hm = [sb(f"hm{j}", [P, DE]) for j in range(2)]
        hmT = [sb(f"hmT{j}", [P, 2, P]) for j in range(2)]
        yo = [sb(f"yo{j}", [P, D]) for j in range(2)]
        ps, ident = c["ps"], c["ident"]
        dest, wgt = c["dest"], c["wgt"]

        w_sem = sem("weights_in")
        h_in = [sem(f"h_in{j}") for j in range(2)]
        hT_ps, hT_rdy, lg_ps, lg_rdy = sem("hT_ps"), sem("hT_rdy"), sem("lg_ps"), sem("lg_rdy")
        step, exp_in, exp_out, ms_rdy, rank_ps, oh_rdy, ix_ps, idx_rdy = (
            sem("step"), sem("exp_in"), sem("exp_out"), sem("ms_rdy"), sem("rank_ps"), sem("oh_rdy"), sem("ix_ps"),
            sem("idx_rdy"))
        w_in = [sem(f"w_in{j}") for j in range(W_RING)]
        g_in = [sem(f"g_in{j}") for j in range(2)]
        gT_ps, gT_rdy, up_ps, silu_rdy, hm_rdy, hmT_ps, hmT_rdy, dn_ps, y_ev = (
            sem("gT_ps"), sem("gT_rdy"), sem("up_ps"), sem("silu_rdy"), sem("hm_rdy"), sem("hmT_ps"),
            sem("hmT_rdy"), sem("dn_ps"), sem("y_ev"))
        y_out = [sem(f"y_out{j}") for j in range(2)]
        o_w, o_g, o_gT_ps, o_gT, o_up, o_silu, o_hm, o_hmT_ps, o_hmT, o_dn, o_ev, o_out = (
            sem("o_w"), sem("o_g"), sem("o_gT_ps"), sem("o_gT"), sem("o_up"), sem("o_silu"), sem("o_hm"),
            sem("o_hmT_ps"), sem("o_hmT"), sem("o_dn"), sem("o_ev"), sem("o_out"))
        main_done, over_stored = sem("main_done"), sem("over_stored")

        def expert_steps(eng, body, before_all, after_all):
            before_all()
            with eng.Fori(0, (NE - 2) // 6) as r:
                for j in range(6):
                    e = 1 + j
                    body(r * 6 + e, e % 2, e % W_RING, r * 2 + e // W_RING)
            after_all()

        with nc.Block() as block:
            @block.sync
            def _(sp):
                def weights(e, wr):
                    if isinstance(e, int):
                        e_ = slice(e, e + 1)
                    else:
                        e_ = bass.ds(e, 1)
                    sp.dma_start(w13[wr][:, :, :], io["w13"][l, e_].rearrange("a p k n -> p (a k) n")).then_inc(
                        w_in[wr], 16)
                    sp.dma_start(w2[wr][:, :, :], io["w2"][l, e_].rearrange("a p k n -> p (a k) n")).then_inc(
                        w_in[wr], 16)

                for dst, src in ((w_route[:, :, :], io["w_route"][l]),
                                 (b_route[:, :], io["b_route"][l:l + 1, :].broadcast_to([P, 36])),
                                 (before[:, :], io["before"]), (ones[:, :], io["ones"]),
                                 (iota[:, :], io["iota"]), (token[:, :], io["token"])):
                    sp.dma_start(dst, src).then_inc(w_sem, 16)
                for s in range(2):
                    sp.dma_start(hx[s][:, :], io["h2"][s * P:(s + 1) * P, :]).then_inc(h_in[s], 16)
                with sp.Fori(0, nt // 2 - 1) as r:
                    for s in range(2):
                        sp.wait_ge(hT_ps, r * 2 + s + 1)
                        sp.dma_start(hx[s][:, :], io["h2"][bass.ds(r * 256 + (s + 2) * P, P), :]).then_inc(h_in[s], 16)
                for e in range(W_RING):
                    weights(e, e)
                with sp.Fori(0, 4) as r:
                    for j in range(6):
                        e = j + W_RING
                        sp.wait_ge(dn_ps, r * 6 + e - W_RING + 1)
                        weights(r * 6 + e, e % W_RING)
                for e in range(W_RING + 24, NE):
                    sp.wait_ge(dn_ps, e - W_RING + 1)
                    weights(e, e % W_RING)

                sp.wait_ge(main_done, 1)
                sp.sem_inc(o_out, 16)
                n_ov = sp.value_load(ovi[0:1, n_over:n_over + 1], min_val=0, max_val=n_over)
                with sp.Fori(0, n_over) as j:
                    with sp.If(n_ov > j):
                        e = sp.value_load(ovi[0:1, bass.ds(j, 1)], min_val=0, max_val=NE - 1)
                        sp.dma_start(w13[0][:, :, :], io["w13"][l, bass.ds(e, 1)].rearrange(
                            "a p k n -> p (a k) n")).then_inc(o_w, 16)
                        sp.dma_start(w2[0][:, :, :], io["w2"][l, bass.ds(e, 1)].rearrange(
                            "a p k n -> p (a k) n")).then_inc(o_w, 16)
                        sp.wait_ge(o_ev, j * 2 + 2)
                        sp.dma_start(io["ys"][bass.ds(j * P + NE * P, P), :], yo[0][:, :]).then_inc(o_out, 16)
                sp.wait_ge(o_out, n_ov * 16 + 16)
                sp.sem_inc(over_stored, 1)
                sp.wait_ge(over_stored, 1)

            @block.gpsimd
            def _(pool):
                def gather(b, slot, signal):
                    pool.indirect_dma_start(out=slot[:, :], out_offset=None, in_=io["h2"][:, :],
                                            in_offset=bass.IndirectOffsetOnAxis(ap=idx[:, b:b + 1], axis=0)
                                            ).then_inc(signal, 16)

                pool.wait_ge(idx_rdy, 1)
                for e in range(NE):
                    if e >= 2:
                        pool.wait_ge(gT_ps, e - 1)
                    gather(e, xg[e % 2], g_in[e % 2])
                pool.wait_ge(gT_ps, NE)
                n_ov = pool.value_load(ovi[0:1, n_over:n_over + 1], min_val=0, max_val=n_over)
                for j in range(n_over):
                    with pool.If(n_ov > j):
                        if j:
                            pool.wait_ge(o_gT_ps, j)
                        gather(NE + j, xg[0], o_g)

            @block.tensor
            def _(pe):
                pe.wait_ge(w_sem, 16 * 6)

                def route(t, s, r):
                    pe.wait_ge(h_in[s], r * 16 + 16)
                    for k in range(KD):
                        tr = pe.transpose(ps[:, HT_AT + k * P:HT_AT + (k + 1) * P], hx[s][:, k * P:(k + 1) * P],
                                          ident[:, :])
                    tr.then_inc(hT_ps, 1)
                    pe.wait_ge(hT_rdy, t * 2 + 2)
                    pe.wait_ge(lg_rdy, t + 1)
                    for k in range(KD):
                        mm = pe.matmul(ps[:, LG_AT:LG_AT + 36], hT[:, k, :], w_route[:, k, :], start=(k == 0),
                                       stop=(k == KD - 1))
                    mm.then_inc(lg_ps, 1)

                in_pairs(pe, nt, route)
                pe.wait_ge(ms_rdy, 1)
                rk_ps = ps[:, RK_AT:RK_AT + nt * NE]
                pe.matmul(rk_ps, before[:, :], msum[:, :, :].rearrange("p t e -> p (t e)"), start=True, stop=False)
                pe.matmul(rk_ps, ones[:, :], cum[:, 0:nt, :].rearrange("p t e -> p (t e)"), start=False, stop=True)
                pe.matmul(ps[:, CNT_AT:CNT_AT + NE], ones[:, :], cum[:, nt, :], start=True,
                          stop=True).then_inc(rank_ps, 1)
                for n in range(2 * nt):
                    pe.wait_ge(oh_rdy, n + 1)
                    pe.matmul(ps[:, IX_AT:IX_AT + NBLK], a_oh[n % 2][:, :], b_oh[n % 2][:, :], start=(n == 0),
                              stop=(n == 2 * nt - 1)).then_inc(ix_ps, 1)

                def gathered(xs, xTs, sig_in, value, sig_out):
                    pe.wait_ge(sig_in, value)
                    for k in range(KD):
                        tr = pe.transpose(ps[:, GT_AT + k * P:GT_AT + (k + 1) * P], xs[:, k * P:(k + 1) * P],
                                          ident[:, :])
                    tr.then_inc(sig_out, 1)

                def up(at, xTs, w, sig):
                    for k in range(KD):
                        mm = pe.matmul(ps[:, at:at + 512], xTs[:, k, :], w[:, k, :], start=(k == 0),
                                       stop=(k == KD - 1))
                    mm.then_inc(sig, 1)

                def hidden(h, sig):
                    for k in range(2):
                        tr = pe.transpose(ps[:, HM_AT + k * P:HM_AT + (k + 1) * P], h[:, k * P:(k + 1) * P],
                                          ident[:, :])
                    tr.then_inc(sig, 1)

                def down(hT_, w, sig):
                    for n in range(2):
                        for k in range(2):
                            mm = pe.matmul(ps[:, DN_AT + n * 512:DN_AT + (n + 1) * 512], hT_[:, k, :],
                                           w[:, k, n * 512:(n + 1) * 512], start=(k == 0), stop=(k == 1))
                    mm.then_inc(sig, 1)

                def step_up(e, s, wr, wn):
                    pe.wait_ge(w_in[wr], wn * 32 + 32)
                    pe.wait_ge(gT_rdy, e * 2 + 2)
                    pe.wait_ge(hm_rdy, e + 1)
                    up(UP_AT[s], xgT[s], w13[wr], up_ps)

                def step_down(e, s, wr):
                    pe.wait_ge(hmT_rdy, e + 1)
                    pe.wait_ge(y_ev, e * 2 + 2)
                    down(hmT[s], w2[wr], dn_ps)

                def step_hidden(e, s):
                    pe.wait_ge(hm_rdy, e + 3)
                    hidden(hm[s], hmT_ps)

                def first():
                    gathered(xg[0], xgT[0], g_in[0], 16, gT_ps)
                    step_up(0, 0, 0, 0)
                    gathered(xg[1], xgT[1], g_in[1], 16, gT_ps)
                    step_hidden(0, 0)

                def body(e, s, wr, wn):
                    step_up(e, s, wr, wn)
                    gathered(xg[1 - s], xgT[1 - s], g_in[1 - s],
                             (e - s) * 8 + (32 if s else 16), gT_ps)
                    step_down(e - 1, 1 - s, (wr - 1) % W_RING)
                    step_hidden(e, s)

                def last():
                    e = NE - 1
                    step_up(e, 1, e % W_RING, e // W_RING)
                    step_down(e - 1, 0, (e - 1) % W_RING)
                    step_hidden(e, 1)
                    step_down(e, 1, e % W_RING)

                expert_steps(pe, body, first, last)

                pe.wait_ge(main_done, 1)
                n_ov = pe.value_load(ovi[0:1, n_over:n_over + 1], min_val=0, max_val=n_over)
                with pe.Fori(0, n_over) as j:
                    with pe.If(n_ov > j):
                        gathered(xg[0], xgT[0], o_g, j * 16 + 16, o_gT_ps)
                        pe.wait_ge(o_w, j * 32 + 32)
                        pe.wait_ge(o_gT, j * 2 + 2)
                        up(UP_AT[0], xgT[0], w13[0], o_up)
                        pe.wait_ge(o_hm, j + 1)
                        hidden(hm[0], o_hmT_ps)
                        pe.wait_ge(o_hmT, j + 1)
                        down(hmT[0], w2[0], o_dn)

            @block.scalar
            def _(act):
                def route(t, s, r):
                    act.wait_ge(hT_ps, t + 1)
                    act.copy(hT[:, 0:4, :], ps[:, HT_AT:HT_AT + 512].rearrange(
                        "p (k n) -> p k n", k=4)).then_inc(hT_rdy, 1)

                in_pairs(act, nt, route)
                act.wait_ge(exp_in, 1)
                act.activation(g4[:, :, :], g4[:, :, :], ACT.Exp).then_inc(exp_out, 1)
                act.wait_ge(exp_in, 2)
                act.activation(e1[:, :], e1[:, :], ACT.Exp).then_inc(exp_out, 1)

                def rows(xTs, sig_in, value, sig_out):
                    act.wait_ge(sig_in, value)
                    act.copy(xTs[:, 0:4, :], ps[:, GT_AT:GT_AT + 512].rearrange(
                        "p (k n) -> p k n", k=4)).then_inc(sig_out, 1)

                def silu(e, s):
                    act.wait_ge(up_ps, e + 1)
                    act.activation(act1[s][:, :], ps[:, UP_AT[s]:UP_AT[s] + DE], ACT.Silu).then_inc(silu_rdy, 1)

                def output(e, s, n):
                    act.wait_ge(dn_ps, e + 1)
                    act.wait_ge(y_out[s], n * 16 + 16)
                    act.copy(yo[s][:, 0:512], ps[:, DN_AT:DN_AT + 512]).then_inc(y_ev, 1)
                    act.wait_ge(y_ev, e * 2 + 4)
                    rows_out = io["ys"][e * P:(e + 1) * P, :] if isinstance(e, int) else io["ys"][bass.ds(e * P, P), :]
                    act.dma_start(rows_out, yo[s][:, :]).then_inc(y_out[s], 16)

                def first():
                    for s in range(2):
                        act.sem_inc(y_out[s], 16)
                    rows(xgT[0], gT_ps, 1, gT_rdy)
                    silu(0, 0)
                    rows(xgT[1], gT_ps, 2, gT_rdy)

                def body(e, s, wr, wn):
                    silu(e, s)
                    rows(xgT[1 - s], gT_ps, e + 2, gT_rdy)
                    act.wait_ge(dn_ps, e)
                    p = 1 - s
                    act.wait_ge(y_out[p], (e - 1 - p) * 8 + 16)
                    act.copy(yo[p][:, 0:512], ps[:, DN_AT:DN_AT + 512]).then_inc(y_ev, 1)
                    act.wait_ge(y_ev, e * 2 + 2)
                    act.dma_start(io["ys"][bass.ds(e * P - P, P), :], yo[p][:, :]).then_inc(y_out[p], 16)

                def last():
                    e = NE - 1
                    silu(e, 1)
                    output(e - 1, 0, (e - 1) // 2)
                    output(e, 1, e // 2)
                    for s in range(2):
                        act.wait_ge(y_out[s], 16 + 16 * (NE // 2))
                    act.sem_inc(main_done, 1)

                expert_steps(act, body, first, last)
                n_ov = act.value_load(ovi[0:1, n_over:n_over + 1], min_val=0, max_val=n_over)
                with act.Fori(0, n_over) as j:
                    with act.If(n_ov > j):
                        rows(xgT[0], o_gT_ps, j + 1, o_gT)
                        act.wait_ge(o_up, j + 1)
                        act.activation(act1[0][:, :], ps[:, UP_AT[0]:UP_AT[0] + DE], ACT.Silu).then_inc(o_silu, 1)
                        act.wait_ge(o_dn, j + 1)
                        act.wait_ge(o_out, j * 16 + 16)
                        act.copy(yo[0][:, 0:512], ps[:, DN_AT:DN_AT + 512]).then_inc(o_ev, 1)

            @block.vector
            def _(dve):
                dve.sem_inc(lg_rdy, 1)
                dve.wait_ge(w_sem, 16 * 6)

                def route(t, s, r):
                    dve.wait_ge(hT_ps, t + 1)
                    dve.tensor_copy(hT[:, 4:8, :], ps[:, HT_AT + 512:HT_AT + 1024].rearrange(
                        "p (k n) -> p k n", k=4)).then_inc(hT_rdy, 1)
                    dve.wait_ge(lg_ps, t + 1)
                    dve.tensor_tensor(lg[:, bass.ds(t, 1), :], ps[:, LG_AT:LG_AT + 36].unsqueeze(1),
                                      b_route[:, :].unsqueeze(1), ALU.add).then_inc(lg_rdy, 1)

                in_pairs(dve, nt, route)
                dve.wait_ge(lg_rdy, nt + 1)
                st = Steps(dve, step, 0)
                st.begin(0)
                V = dve

                def tt(out, a, b, op):
                    st.after(V.tensor_tensor(out, a, b, op))

                def ts(out, a, x, op, x2=None, op2=None):
                    st.after(V.tensor_scalar(out, a, x, x2, op, op2) if op2 is not None
                             else V.tensor_scalar(out, a, x, None, op))

                def red(out, a, op):
                    st.after(V.tensor_reduce(out, a, AX_X, op))

                def over_last(v, shape):
                    return v.unsqueeze(len(shape) - 1).broadcast_to(shape)

                def count_up(n, w):
                    return iota[:, 0:w].unsqueeze(1).broadcast_to([P, n, w])

                def first_index(out, values, top, tmp, w):
                    tt(tmp, values, over_last(top, [P, nt, w]), ALU.is_equal)
                    st.after(V.scalar_tensor_tensor(tmp, tmp, -64.0, count_up(nt, w), ALU.mult, ALU.add))
                    red(out, tmp, ALU.min)
                    ts(out, out, 64.0, ALU.add)

                lgg = lg[:, :, 0:NG]
                red(gmax[:, :], lgg, ALU.max)
                first_index(gi[:, :], lgg, gmax[:, :], og[:, :, :], NG)
                V.tensor_tensor(g4[:, :, :], lgg, over_last(gmax[:, :], [P, nt, NG]), ALU.subtract).then_inc(exp_in, 1)
                tt(og[:, :, :], count_up(nt, NG), over_last(gi[:, :], [P, nt, NG]), ALU.is_equal)
                V.wait_ge(exp_out, 1)
                red(gsum[:, :], g4[:, :, :], ALU.add)
                st.after(V.reciprocal(gsum[:, :], gsum[:, :]))
                tt(s84[:, :, :, :], lg[:, :, NG:36].rearrange("p t (g e) -> p t e g", g=NG),
                   og[:, :, :].unsqueeze(2).broadcast_to([P, nt, EPG, NG]), ALU.mult)
                red(s8[:, :, :], s84[:, :, :, :], ALU.add)
                red(m0[:, :], s8[:, :, :], ALU.max)
                first_index(i0[:, :], s8[:, :, :], m0[:, :], o8[:, :, :], EPG)
                tt(o8[:, :, :], count_up(nt, EPG), over_last(i0[:, :], [P, nt, EPG]), ALU.is_equal)
                st.after(V.scalar_tensor_tensor(s8[:, :, :], o8[:, :, :], -BIG, s8[:, :, :], ALU.mult, ALU.add))
                red(m1[:, :], s8[:, :, :], ALU.max)
                first_index(i1[:, :], s8[:, :, :], m1[:, :], o8[:, :, :], EPG)
                V.tensor_tensor(e1[:, :], m1[:, :], m0[:, :], ALU.subtract).then_inc(exp_in, 1)
                V.wait_ge(exp_out, 2)
                ts(m0[:, :], e1[:, :], 1.0, ALU.add)
                st.after(V.reciprocal(m0[:, :], m0[:, :]))
                tt(wgt[:, 0:nt, 0], m0[:, :], gsum[:, :], ALU.mult)
                tt(wgt[:, 0:nt, 1], wgt[:, 0:nt, 0], e1[:, :], ALU.mult)
                ek2 = ek[:, :].rearrange("p (t k) -> p t k", k=2)
                for k, ik in enumerate((i0, i1)):
                    st.after(V.scalar_tensor_tensor(ek2[:, :, k], gi[:, :], float(EPG), ik[:, :], ALU.mult, ALU.add))
                tt(member[:, :, :], count_up(2 * nt, NE), over_last(ek[:, :], [P, 2 * nt, NE]), ALU.is_equal)
                mem4 = member[:, :, :].rearrange("p (t k) e -> p t k e", k=2)
                tt(msum[:, :, :], mem4[:, :, 0, :], mem4[:, :, 1, :], ALU.add)
                st.after(V.memset(cum[:, 0, :], 0.0))
                for t in range(nt):
                    tt(cum[:, t + 1, :], cum[:, t, :], msum[:, t, :], ALU.add)
                V.sem_inc(ms_rdy, 1)
                V.wait_ge(rank_ps, 1)
                st.after(V.tensor_copy(rank[:, :, :], ps[:, RK_AT:RK_AT + nt * NE].rearrange("p (t e) -> p t e", e=NE)))
                ts(cnt[:, :], ps[:, CNT_AT:CNT_AT + NE], float(P - 1), ALU.add)
                mp4 = mprod[:, :, :].rearrange("p (t k) e -> p t k e", k=2)
                tt(mp4, mem4, rank[:, :, :].unsqueeze(2).broadcast_to([P, nt, 2, NE]), ALU.mult)
                red(rk[:, :], mprod[:, :, :], ALU.add)
                st.after(V.tensor_copy(rki[:, :], rk[:, :]))
                ts(rki[:, :], rki[:, :], 7, ALU.arith_shift_right)
                st.after(V.tensor_copy(over[:, :], rki[:, :]))
                st.after(V.scalar_tensor_tensor(rmod[:, :], over[:, :], -float(P), rk[:, :], ALU.mult, ALU.add))
                st.after(V.tensor_copy(cnti[:, :], cnt[:, :]))
                ts(cnti[:, :], cnti[:, :], 7, ALU.arith_shift_right)
                st.after(V.tensor_copy(ov[:, :], cnti[:, :]))
                ts(ov[:, :], ov[:, :], -1.0, ALU.add, 0.0, ALU.max)
                src, dst = ov, oe0
                for sh in (1, 2, 4, 8, 16):
                    st.after(V.tensor_copy(dst[:, 0:sh], src[:, 0:sh]))
                    tt(dst[:, sh:NE], src[:, sh:NE], src[:, 0:NE - sh], ALU.add)
                    src, dst = dst, (oe1 if dst is oe0 else oe0)
                ovend, ovbase = src, dst
                tt(ovbase[:, :], ovend[:, :], ov[:, :], ALU.subtract)
                tt(mprod[:, :, :], member[:, :, :], ovbase[:, :].unsqueeze(1).broadcast_to([P, 2 * nt, NE]), ALU.mult)
                red(blk[:, :], mprod[:, :, :], ALU.add)
                tt(blk[:, :], blk[:, :], over[:, :], ALU.add)
                st.after(V.scalar_tensor_tensor(blk[:, :], blk[:, :], float(NE - 1), ek[:, :], ALU.add, ALU.subtract))
                ts(over[:, :], over[:, :], 1.0, ALU.min)
                tt(blk[:, :], blk[:, :], over[:, :], ALU.mult)
                tt(blk[:, :], blk[:, :], ek[:, :], ALU.add)
                st.after(V.scalar_tensor_tensor(dest[:, 0:2 * nt], blk[:, :], float(P), rmod[:, :], ALU.mult, ALU.add))
                oc = ovc[:, :, :]
                tt(oc, iota[0:1, 0:n_over].unsqueeze(2).broadcast_to([1, n_over, NE]),
                   ovend[0:1, :].unsqueeze(1).broadcast_to([1, n_over, NE]), ALU.is_ge)
                red(ovf[:, 0:n_over], oc, ALU.add)
                ts(ovf[:, 0:n_over], ovf[:, 0:n_over], float(NE - 1), ALU.min)
                st.after(V.tensor_copy(ovf[:, n_over:n_over + 1], ovend[0:1, NE - 1:NE]))
                st.after(V.tensor_copy(ovi[:, :], ovf[:, :]))
                for n in range(2 * nt):
                    if n >= 2:
                        V.wait_ge(ix_ps, n - 1)
                    V.tensor_scalar(a_oh[n % 2][:, :], iota[:, :], rmod[:, n:n + 1], None, ALU.is_equal)
                    V.tensor_scalar(b_oh[n % 2][:, :], iota[:, 0:NBLK], blk[:, n:n + 1], token[:, n // 2:n // 2 + 1],
                                    ALU.is_equal, ALU.mult).then_inc(oh_rdy, 1)
                V.wait_ge(ix_ps, 2 * nt)
                V.tensor_copy(idx[:, :], ps[:, IX_AT:IX_AT + NBLK]).then_inc(idx_rdy, 1)
                V.wait_ge(idx_rdy, 1)

                def rows(xTs, sig_in, value, sig_out):
                    dve.wait_ge(sig_in, value)
                    dve.tensor_copy(xTs[:, 4:8, :], ps[:, GT_AT + 512:GT_AT + 1024].rearrange(
                        "p (k n) -> p k n", k=4)).then_inc(sig_out, 1)

                def gated(e, s):
                    dve.wait_ge(silu_rdy, e + 1)
                    dve.tensor_tensor(hm[s][:, :], act1[s][:, :], ps[:, UP_AT[s] + DE:UP_AT[s] + 2 * DE],
                                      ALU.mult).then_inc(hm_rdy, 1)

                def hidden(e, s):
                    dve.wait_ge(hmT_ps, e + 1)
                    dve.tensor_copy(hmT[s][:, :, :], ps[:, HM_AT:HM_AT + 256].rearrange(
                        "p (k n) -> p k n", k=2)).then_inc(hmT_rdy, 1)

                def output(e, p):
                    dve.wait_ge(dn_ps, e + 1)
                    dve.wait_ge(y_out[p], (e - p) * 8 + 16)
                    dve.tensor_copy(yo[p][:, 512:1024], ps[:, DN_AT + 512:DN_AT + 1024]).then_inc(y_ev, 1)

                def first():
                    dve.sem_inc(hm_rdy, 2)
                    dve.sem_inc(y_ev, 2)
                    rows(xgT[0], gT_ps, 1, gT_rdy)
                    gated(0, 0)
                    rows(xgT[1], gT_ps, 2, gT_rdy)
                    hidden(0, 0)

                def body(e, s, wr, wn):
                    gated(e, s)
                    rows(xgT[1 - s], gT_ps, e + 2, gT_rdy)
                    output(e - 1, 1 - s)
                    hidden(e, s)

                def last():
                    e = NE - 1
                    gated(e, 1)
                    output(e - 1, 0)
                    hidden(e, 1)
                    output(e, 1)

                expert_steps(dve, body, first, last)
                dve.wait_ge(main_done, 1)
                n_ov = dve.value_load(ovi[0:1, n_over:n_over + 1], min_val=0, max_val=n_over)
                with dve.Fori(0, n_over) as j:
                    with dve.If(n_ov > j):
                        rows(xgT[0], o_gT_ps, j + 1, o_gT)
                        dve.wait_ge(o_silu, j + 1)
                        dve.tensor_tensor(hm[0][:, :], act1[0][:, :], ps[:, UP_AT[0] + DE:UP_AT[0] + 2 * DE],
                                          ALU.mult).then_inc(o_hm, 1)
                        dve.wait_ge(o_hmT_ps, j + 1)
                        dve.tensor_copy(hmT[0][:, :, :], ps[:, HM_AT:HM_AT + 256].rearrange(
                            "p (k n) -> p k n", k=2)).then_inc(o_hmT, 1)
                        dve.wait_ge(o_dn, j + 1)
                        dve.wait_ge(o_out, j * 16 + 16)
                        dve.tensor_copy(yo[0][:, 512:1024], ps[:, DN_AT + 512:DN_AT + 1024]).then_inc(o_ev, 1)


def combine(nc, l, io, c, out):
    nt = NT if l < DEPTH - 1 else NT_LAT
    STEPS = 6
    ctx = ExitStack()
    sb = lambda n, s, d=F32: ctx.enter_context(nc.sbuf_tensor(f"cb_{n}_{l}", s, d))
    sem = phase_semaphores(nc, ctx, lambda n: f"cb_{n}_{l}")
    RING = nt
    with ctx:
        yy = sb("yy", [P, RING, 2, D])
        xin = [sb(f"x{j}", [P, D]) for j in range(2)]
        gate2 = sb("gate2", [P, 2, D])
        ln_g, ln_b = sb("ln_g", [P, D]), sb("ln_b", [P, D])
        f = [sb(f"f{j}", [P, D]) for j in range(2)]
        z = sb("z", [P, D])
        xo = [sb(f"xo{j}", [P, D]) for j in range(2)]
        stats, mv, rstd, tick = sb("stats", [P, 2, 6]), sb("mv", [P, 2]), sb("rstd", [P, 1]), sb("tick", [P, 1])
        neg_half = sb("neg_half", [P, 1])
        dest, wgt = c["dest"], c["wgt"]
        w_sem, half_rdy = sem("w_in"), sem("half_rdy")
        x_in = [sem(f"x_in{j}") for j in range(2)]
        y_in = [sem(f"y_in{t}") for t in range(nt)]
        o_out = [sem(f"o_out{j}") for j in range(2)]
        first_rdy, step, var_rdy, rstd_rdy, xo_rdy, y_all = (
            sem("first"), sem("step"), sem("var_rdy"), sem("rstd_rdy"), sem("xo_rdy"), sem("y_all"))

        def store_at(t):
            return out[0, bass.ds(t * P, P), :] if l == DEPTH - 1 else io["x_mid"][bass.ds(t * P, P), :]

        with nc.Block() as block:
            @block.sync
            def _(sp):
                def load(t, s):
                    sp.dma_start(xin[s][:, :], io["x_post"][bass.ds(t * P, P), :]).then_inc(x_in[s], 16)

                def store(t, s):
                    sp.wait_ge(xo_rdy, t + 1)
                    sp.dma_start(store_at(t), xo[s][:, :]).then_inc(o_out[s], 16)

                for s in range(2):
                    sp.sem_inc(o_out[s], 16)
                    load(s, s)
                for s in range(2):
                    sp.dma_start(gate2[:, s, :], io["mod"][l, s:s + 1, 5 * D:6 * D].broadcast_to([P, D])).then_inc(w_sem, 16)
                sp.dma_start(ln_g[:, :], io["ln"][l, 2:3, :].broadcast_to([P, D])).then_inc(w_sem, 16)
                sp.dma_start(ln_b[:, :], io["ln"][l, 3:4, :].broadcast_to([P, D])).then_inc(w_sem, 16)
                with sp.Fori(0, nt // 2 - 1) as r:
                    for s in range(2):
                        store(r * 2 + s, s)
                        load(r * 2 + s + 2, s)
                for s in range(2):
                    store(nt - 2 + s, s)
                for s in range(2):
                    sp.wait_ge(o_out[s], 16 + 16 * (nt // 2))

            @block.gpsimd
            def _(pool):
                pool.memset(neg_half[:, :], -0.5).then_inc(half_rdy, 1)
                pool.wait_ge(half_rdy, 1)
                for t in range(nt):
                    for k in range(2):
                        pool.indirect_dma_start(
                            out=yy[:, t, k, :], out_offset=None, in_=io["ys"][:, :],
                            in_offset=bass.IndirectOffsetOnAxis(ap=dest[:, 2 * t + k:2 * t + k + 1], axis=0)
                        ).then_inc(y_in[t], 16)
                for t in range(nt):
                    pool.wait_ge(var_rdy, t + 1)
                    pool.tensor_tensor(rstd[:, :], mv[:, 1:2], neg_half[:, :], ALU.pow).then_inc(rstd_rdy, 1)

            @block.scalar
            def _(act):
                for t in range(nt):
                    act.wait_ge(y_in[t], 32)
                    if t >= 2:
                        act.wait_ge(step, (t - 2) * STEPS + 2)
                    act.activation(f[t % 2][:, :], yy[:, t, 0, :], ACT.Copy,
                                   scale=wgt[:, t, 0:1]).then_inc(first_rdy, 1)

            @block.vector
            def _(dve):
                dve.wait_ge(w_sem, 64)
                st = Steps(dve, step, STEPS)

                def body(t, s, stream):
                    st.begin(t)
                    dve.wait_ge(first_rdy, t + 1)
                    at = bass.ds(t, 1)
                    st.after(dve.scalar_tensor_tensor(f[s][:, :].unsqueeze(1), yy[:, at, 1, :], wgt[:, at, 1],
                                                      f[s][:, :].unsqueeze(1), ALU.mult, ALU.add))
                    st.after(dve.tensor_tensor(z[:, :], f[s][:, :], gate2[:, stream, :], ALU.mult))
                    dve.wait_ge(x_in[s], 16 * (t // 2) + 16)
                    st.after(dve.scalar_tensor_tensor(z[:, :], xin[s][:, :], ALPHA, z[:, :], ALU.mult, ALU.add))
                    for j in range(2):
                        op = dve.bn_stats(stats[:, j, :], z[:, j * 512:(j + 1) * 512])
                    st.after(op)
                    st.after(dve.bn_aggr(mv[:, :], stats[:, :, :]))
                    dve.tensor_scalar(mv[:, 1:2], mv[:, 1:2], EPS, None, ALU.add).then_inc(var_rdy, 1)
                    dve.wait_ge(rstd_rdy, t + 1)
                    st.after(dve.tensor_scalar(z[:, :], z[:, :], mv[:, 0:1], rstd[:, :], ALU.subtract, ALU.mult))
                    dve.wait_ge(o_out[s], 16 * (t // 2) + 16)
                    dve.tensor_tensor(xo[s][:, :], z[:, :], ln_g[:, :], ALU.mult).then_inc(y_all, 1)
                    dve.wait_ge(y_all, t + 1)
                    dve.tensor_tensor(xo[s][:, :], xo[s][:, :], ln_b[:, :], ALU.add).then_inc(xo_rdy, 1)
                    st.end()

                for t in range(nt):
                    body(t, t % 2, 0 if t < NT_LAT else 1)


def build(nc, io, out):
    ctx = ExitStack()
    with ctx:
        sb = lambda n, s, d=F32: ctx.enter_context(nc.sbuf_tensor(n, s, d))
        c = {"ps": ctx.enter_context(nc.psum_tensor("ps", [P, 4096], F32)),
             "ident": sb("ident", [P, P]),
             "dest": sb("dest", [P, 2 * NT], I32), "wgt": sb("wgt", [P, NT, 2])}
        keep = {"shift1": sb("shift1", [P, KD, 2]), "scale1": sb("scale1", [P, KD, 2])}
        const_in = ctx.enter_context(nc.semaphore("const_in"))
        with nc.Block() as block:
            @block.sync
            def _(sp):
                sp.dma_start(c["ident"][:, :], io["ident"]).then_inc(const_in, 16)
                sp.wait_ge(const_in, 16)
        for l in range(DEPTH):
            mod_weights(nc, l, io, c, keep)
            with ExitStack() as layer:
                kvt = lambda n, s: layer.enter_context(nc.sbuf_tensor(f"{n}_{l}", s, F32))
                kv = {"km": kvt("km", [MLA_QK, MLA_H, T]), "kd": kvt("kd", [P, 2, T]), "kg": kvt("kg", [P, T]),
                      "vm": kvt("vm", [P, NT, 256]), "vd": kvt("vd", [P, NT, 256]), "vg": kvt("vg", [P, NT, 128])}
                project(nc, l, io, c, keep, kv)
                attend(nc, l, io, c, kv, 0)
                if l < DEPTH - 1:
                    attend(nc, l, io, c, kv, 1)
            experts(nc, l, io, c)
            combine(nc, l, io, c, out)


def host_arrays(g):
    L, K = DEPTH, KD
    arr = {}
    arr["x_in"] = np.concatenate([g["x"][0], g["ctx"][0]], axis=0)
    arr["c_cols"] = np.stack([g["c"][0], g["c_ctx"]]).reshape(2, K, P).transpose(2, 1, 0)
    arr["w_ada"] = g["w_ada"].reshape(L, K, P, 12, 512).transpose(0, 3, 2, 1, 4)
    arr["b_ada"] = g["b_ada"]
    conv, mla, dif, gqa = 0, 768, 1184, 1952
    cols = [(conv + 256, 256), (conv + 512, 256), (conv, 256), (mla, 256), (dif, 512), (gqa, 384), (mla + 256, 128),
            (dif + 512, 256), (gqa + 384, 128), (mla + 384, 32)]
    order = np.concatenate([np.arange(a, a + n) for a, n in cols])
    arr["w_in"] = g["w_in"][:, :, order].reshape(L, K, P, D_IN).transpose(0, 2, 1, 3)
    uq = g["mla_w_uq"].reshape(L, 2, P, MLA_H, 64)
    qr = g["mla_w_qr"].reshape(L, 2, P, MLA_H, 32)
    arr["w_q"] = np.concatenate([uq, qr], axis=4).reshape(L, 2, P, 384).transpose(0, 2, 1, 3)
    arr["w_kv"] = np.concatenate([g["mla_w_uk"], g["mla_w_uv"]], axis=2)
    arr["lat_gain"] = np.concatenate([g["mla_q_norm"].reshape(L, 2, P), g["mla_kv_norm"].reshape(L, 1, P)],
                                     axis=1).transpose(0, 2, 1)
    arr["qk_gain"] = np.concatenate([g["gqa_q_norm"]] * 4 + [g["gqa_k_norm"]] * 2, axis=1)
    arr["w_out"] = g["w_out"].reshape(L, K, P, D).transpose(0, 2, 1, 3)
    arr["conv_w"] = g["conv_w"].reshape(L, 3 * CONV)
    arr["lambda"] = g["diff_lambda"].reshape(L, 128)
    arr["subln"] = g["diff_subln"]
    arr["ln"] = np.stack([g["ln1_g"], g["ln1_b"], g["ln2_g"], g["ln2_b"]], axis=1)
    arr["w_route"] = np.concatenate([g["moe_w_group"], g["moe_w_sub"]], axis=2).reshape(L, K, P, 36).transpose(0, 2, 1, 3)
    arr["b_route"] = np.concatenate([g["moe_b_group"], g["moe_b_sub"]], axis=1)
    w13 = np.concatenate([g["moe_w1"], g["moe_w3"]], axis=3)
    arr["w13"] = w13.reshape(L, NE, K, P, 2 * DE).transpose(0, 1, 3, 2, 4)
    arr["w2"] = g["moe_w2"].reshape(L, NE, 2, P, D).transpose(0, 1, 3, 2, 4)
    arr["ident"] = np.eye(P, dtype=np.float32)
    arr["before"] = np.triu(np.ones((P, P), np.float32), 1)
    arr["ones"] = np.ones((P, P), np.float32)
    arr["iota"] = np.broadcast_to(np.arange(P, dtype=np.float32), (P, P))
    arr["token"] = (np.arange(NT)[None, :] * P + np.arange(P)[:, None]).astype(np.float32)
    tok = np.arange(LAT)
    rope = np.zeros((T, 192), np.float32)
    rope[:, 0:32] = 1.0
    rope[:, 64:128] = 1.0
    for width, at in ((32, 0), (64, 64)):
        q = width // 4
        freqs = np.float32(THETA) ** (-np.arange(q, dtype=np.float32) / np.float32(q))
        for axis, pos in enumerate((tok // GRID_W, tok % GRID_W)):
            ang = pos.astype(np.float32)[:, None] * freqs.astype(np.float32)
            for half in range(2):
                o = at + axis * 2 * q + half * q
                rope[:LAT, o:o + q] = np.cos(ang)
                rope[:LAT, o + width:o + width + q] = np.sin(ang) * (1.0 if half else -1.0)
    arr["rope"] = rope.reshape(NT, P, 192).transpose(1, 0, 2)
    return arr


def kernel(**inputs):
    import concourse.bacc as bacc
    from concourse.bass_utils import run_bass_kernel_spmd as run

    nc = bacc.Bacc("TRN2", target_bir_lowering=False, num_devices=1)
    io, arrays = {}, {}
    for name, a in host_arrays({k: np.asarray(v) for k, v in inputs.items()}).items():
        a = np.ascontiguousarray(a)
        arrays[f"in_{name}"] = a
        io[name] = nc.dram_tensor(f"in_{name}", a.shape, mybir.dt.from_np(a.dtype), kind="ExternalInput").ap()
    for name, shape in (("mod", (DEPTH, 2, 6 * D)), ("qrow", (T, Q_W)), ("zc", (ZROWS, CONV)), ("x_mid", (T, D)),
                        ("x_post", (T, D)), ("h2", (T, D)), ("ys", (YROWS, D))):
        io[name] = nc.dram_tensor(f"{name}_scratch", shape, F32, kind="Internal").ap()
    out = nc.dram_tensor("out_x", (1, LAT, D), F32, kind="ExternalOutput").ap()
    build(nc, io, out)
    r = run(nc, [arrays], core_ids=[0])
    return r.results[0]["out_x"]
```

```python
import math
from contextlib import ExitStack

import concourse.bass as bass
import numpy as np
from concourse import mybir

F32 = mybir.dt.float32
I32 = mybir.dt.int32
U32 = mybir.dt.uint32
ALU = mybir.AluOpType
ACT = mybir.ActivationFunctionType
AX_X = mybir.AxisListType.X

DEPTH, D, LAT, CTX, GRID_W = 2, 1024, 1024, 256, 64
P = 128
KD = D // P
NT_LAT, NT_CTX = LAT // P, CTX // P
NT = NT_LAT + NT_CTX
T = NT * P
EPS, THETA = 1e-6, 10000.0
CONV = 256
MLA_H, MLA_QK, MLA_NOPE = 4, 96, 64
DIFF_H, DIFF_QK = 4, 32
GQA_KV, GQA_G, HD = 2, 2, 64
MLA_SCALE, DIFF_SCALE, GQA_SCALE = MLA_QK ** -0.5, DIFF_QK ** -0.5, HD ** -0.5
NG, EPG, NE, DE = 4, 8, 32, 256
ALPHA = (2 * DEPTH) ** 0.25

GATE_C, VAL, GATE_B, CQ, DQ, DK, GQ, GK, CKV, DV, GV, KR = (
    0, 256, 512, 768, 1024, 1280, 1536, 1792, 1920, 2048, 2304, 2432)
D_IN = 2464
U_CHUNKS = [(0, 512), (512, 1024), (1024, 1536), (1536, 2048), (2048, 2464)]
QM, QD, QG, QB, Q_W = 0, 384, 640, 896, 1152
U_CQ, U_DQ, U_GQ, U_CKV, U_KR, U_W = 512, 768, 1280, 1664, 1792, 1824
U_OF = {GATE_C: 0, DQ: U_DQ, GQ: U_GQ}
A_STEPS, VAR_STEP = 10, 3
ZROWS = 1 + LAT + 1 + CTX + 1

MAX_OVER = (2 * T - 1) // P
YROWS = (NE + MAX_OVER) * P


def conv_row(t):
    return t * P + 1 if not isinstance(t, int) or t < NT_LAT else t * P + 2


def phase_semaphores(nc, ctx, name):
    held = []

    def give_back():
        nc.clear_and_free_semaphores(held)
        nc.all_engine_barrier()

    ctx.callback(give_back)

    def sem(n):
        held.append(nc.alloc_semaphore(name(n)))
        return held[-1]

    return sem


class Modulation:
    CHUNKS, RING, COLS_AT = 12, 3, 2048

    def __init__(self, l, io, c, keep, sb, sem):
        self.l, self.io, self.c, self.keep = l, io, c, keep
        self.wa = sb("wa", [P, self.RING, KD, 512])
        self.mod = sb("mod", [2, 6 * D])
        self.ct, self.et, self.st = sb("ct", [P, KD, 2]), sb("et", [P, KD, 2]), sb("silu_c", [P, KD, 2])
        self.wa_in = [sem(f"wa_in{j}") for j in range(self.RING)]
        self.small_in, self.neg_exp, self.silu_step, self.silu_rdy = (
            sem("mod_small_in"), sem("neg_exp"), sem("silu_step"), sem("silu_rdy"))
        self.mm_done, self.mod_rdy, self.col_ps, self.stored = (
            sem("mod_mm"), sem("mod_rdy"), sem("col_ps"), sem("mod_stored"))

    def load_small(self, sp):
        sp.dma_start(self.ct[:, :, :], self.io["c_cols"]).then_inc(self.small_in, 16)
        sp.dma_start(self.mod[:, :], self.io["b_ada"][self.l:self.l + 1, :].broadcast_to([2, 6 * D])).then_inc(
            self.small_in, 16)

    def load_chunk(self, sp, i, j):
        sp.wait_ge(self.mm_done, i * self.RING + j + 1)
        sp.dma_start(self.wa[:, j, :, :], self.io["w_ada"][self.l, bass.ds(i * self.RING + j, 1), :, :, :].rearrange(
            "a p k n -> p (a k) n")).then_inc(self.wa_in[j], 16)

    def store(self, sp):
        sp.wait_ge(self.mod_rdy, self.RING + self.CHUNKS)
        sp.dma_start(self.io["mod"][self.l], self.mod[:, :]).then_inc(self.stored, 16)
        sp.wait_ge(self.stored, 16)

    def exponential(self, act):
        act.wait_ge(self.small_in, 32)
        act.activation(self.et[:, :, :], self.ct[:, :, :], ACT.Exp, scale=-1.0).then_inc(self.neg_exp, 1)

    def silu(self, dve):
        et = self.et[:, :, :]
        dve.sem_inc(self.mod_rdy, self.RING)
        dve.wait_ge(self.neg_exp, 1)
        dve.tensor_scalar(et, et, 1.0, None, ALU.add).then_inc(self.silu_step, 1)
        dve.wait_ge(self.silu_step, 1)
        dve.reciprocal(et, et).then_inc(self.silu_step, 1)
        dve.wait_ge(self.silu_step, 2)
        dve.tensor_tensor(self.st[:, :, :], et, self.ct[:, :, :], ALU.mult).then_inc(self.silu_rdy, 1)

    def read_chunk(self, dve, i, j):
        dve.wait_ge(self.mm_done, self.RING + i * self.RING + j + 1)
        at = self.mod[:, bass.ds(i * (self.RING * 512) + j * 512, 512)]
        dve.tensor_tensor(at, self.c["ps"][0:2, j * 512:(j + 1) * 512], at, ALU.add).then_inc(self.mod_rdy, 1)

    def read_columns(self, dve):
        ps, at = self.c["ps"], self.COLS_AT
        dve.wait_ge(self.col_ps, 1)
        dve.tensor_copy(self.keep["shift1"][:, :, :], ps[:, at:at + 2 * KD].rearrange("p (k s) -> p k s", s=2))
        dve.tensor_scalar(self.keep["scale1"][:, :, :],
                          ps[:, at + 2 * KD:at + 4 * KD].rearrange("p (k s) -> p k s", s=2), 1.0, None, ALU.add)

    def products(self, pe):
        ps, ident = self.c["ps"], self.c["ident"]
        pe.sem_inc(self.mm_done, self.RING)
        pe.wait_ge(self.silu_rdy, 1)
        with pe.Fori(0, self.CHUNKS // self.RING) as i:
            for j in range(self.RING):
                pe.wait_ge(self.wa_in[j], i * 16 + 16)
                pe.wait_ge(self.mod_rdy, i * self.RING + j + 1)
                for k in range(KD):
                    mm = pe.matmul(ps[0:2, j * 512:(j + 1) * 512], self.st[:, k, :], self.wa[:, j, k, :],
                                   start=(k == 0), stop=(k == KD - 1))
                mm.then_inc(self.mm_done, 1)
        pe.wait_ge(self.mod_rdy, self.RING + self.CHUNKS)
        for v in range(2):
            for k in range(KD):
                at = v * D + k * P
                o = self.COLS_AT + (v * KD + k) * 2
                mm = pe.matmul(ps[:, o:o + 2], self.mod[0:2, at:at + P], ident[0:2, 0:2], start=True, stop=True)
        mm.then_inc(self.col_ps, 1)


def first_modulation(nc, l, io, c, keep):
    ctx = ExitStack()
    with ctx:
        m = Modulation(l, io, c, keep, lambda n, s: ctx.enter_context(nc.sbuf_tensor(f"{n}_{l}", s, F32)),
                       phase_semaphores(nc, ctx, lambda n: f"{n}_{l}"))
        rounds = m.CHUNKS // m.RING
        with nc.Block() as block:
            @block.sync
            def _(sp):
                m.load_small(sp)
                with sp.Fori(0, rounds) as i:
                    for j in range(m.RING):
                        m.load_chunk(sp, i, j)
                m.store(sp)

            @block.scalar
            def _(act):
                m.exponential(act)

            @block.vector
            def _(dve):
                m.silu(dve)
                with dve.Fori(0, rounds) as i:
                    for j in range(m.RING):
                        m.read_chunk(dve, i, j)
                m.read_columns(dve)

            @block.tensor
            def _(pe):
                m.products(pe)




class Steps:

    def __init__(self, eng, sem, per_tile):
        self.eng, self.sem, self.per_tile = eng, sem, per_tile

    def begin(self, t):
        self.base, self.k = t * self.per_tile, 0

    def after(self, ins):
        self.k += 1
        ins.then_inc(self.sem, 1)
        self.eng.wait_ge(self.sem, self.base + self.k)

    def end(self):
        assert self.k == self.per_tile, (self.k, self.per_tile)


def in_pairs(eng, n, body):
    if n > 2:
        with eng.Fori(0, n // 2) as r:
            for s in range(2):
                body(r * 2 + s, s, r)
    else:
        for t in range(n):
            body(t, t % 2, t // 2)


def pipelined(eng, body):
    body(0, 0, 0, False, True, 0)
    with eng.Fori(0, NT_LAT // 2 - 1) as r:
        body(r * 2 + 1, 1, r, True, True, 0)
        body(r * 2 + 2, 0, r + 1, True, True, 0)
    for t in range(NT_LAT - 1, NT):
        body(t, t % 2, t // 2, True, t + 1 < NT, 1)


def project(nc, l, io, c, keep, kv):
    ctx = ExitStack()
    sb = lambda n, s, d=F32: ctx.enter_context(nc.sbuf_tensor(f"{n}_{l}", s, d))
    sem = phase_semaphores(nc, ctx, lambda n: f"p1_{n}_{l}")
    x_src = io["x_in"] if l == 0 else io["x_mid"]
    with ctx:
        w_in = sb("w_in", [P, KD, D_IN])
        w_q = sb("w_q", [P, 2, 4 * MLA_QK])
        w_kv = sb("w_kv", [P, 512])
        lat_gain = sb("lat_gain", [P, 3])
        qk_gain = sb("qk_gain", [P, 384])
        rope = sb("rope", [P, NT, 192])
        neg_half = sb("neg_half", [P, 8])
        xt = [sb(f"xt{j}", [P, D]) for j in range(2)]
        hT = [sb(f"hT{j}", [P, KD, P]) for j in range(2)]
        u = [sb(f"u{j}", [P, U_W]) for j in range(2)]
        qrow = [sb(f"qrow{j}", [P, Q_W]) for j in range(2)]
        zc = [sb(f"zc{j}", [P, CONV]) for j in range(2)]
        ka = [sb(f"ka{j}", [P, MLA_H, MLA_QK]) for j in range(2)]
        kdg = [sb(f"kdg{j}", [P, 384]) for j in range(2)]
        latT = sb("latT", [P, 3, P])
        t1 = sb("rt1", [P, 512])
        t2 = sb("rt2", [P, 512])
        ss = sb("ss", [P, 8])
        rs = sb("rs", [P, 8])
        junk = sb("junk", [P, 256])
        zero_row = sb("zero_row", [P, CONV])
        ps = c["ps"]
        ident = c["ident"]
        w_sem = sem("weights_in")
        w_in_in = [sem(f"w_in_in{n}") for n in range(len(U_CHUNKS))]
        x_in = [sem(f"x_in{j}") for j in range(2)]
        xT_ps, hT_rdy, u_ps, u_rdy = sem("xT_ps"), sem("hT_rdy"), sem("u_ps"), sem("u_rdy")
        sq_rdy, rs_rdy = sem("sq_rdy"), sem("rs_rdy")
        a_step, b_step, b_done = sem("a_step"), sem("b_step"), sem("b_done")
        latT_ps, latT_rdy, q_ps, kv_ps, q_rdy, kv_rdy = (
            sem("latT_ps"), sem("latT_rdy"), sem("q_ps"), sem("kv_ps"), sem("q_rdy"), sem("kv_rdy"))
        kT_ps, kT_rdy, kmT_ps, kmT_rdy = sem("kT_ps"), sem("kT_rdy"), sem("kmT_ps"), sem("kmT_rdy")
        zc_rdy, half_rdy, zero_out = sem("zc_rdy"), sem("half_rdy"), sem("zero_out")
        ys_zeroed = sem("ys_zeroed")
        q_out = [sem(f"q_out{j}") for j in range(2)]

        with nc.Block() as block:
            @block.sync
            def _(sp):
                def load(t, s):
                    sp.dma_start(xt[s][:, :], x_src[bass.ds(t * P, P), :]).then_inc(x_in[s], 16)

                for s in range(2):
                    load(s, s)
                sp.dma_start(w_in[:, :, 0:512], io["w_in"][l, :, :, 0:512]).then_inc(w_in_in[0], 16)
                sp.dma_start(w_q[:, :, :], io["w_q"][l]).then_inc(w_sem, 16)
                sp.dma_start(w_kv[:, :], io["w_kv"][l]).then_inc(w_sem, 16)
                sp.dma_start(lat_gain[:, :], io["lat_gain"][l]).then_inc(w_sem, 16)
                sp.dma_start(qk_gain[:, :], io["qk_gain"][l:l + 1, :].broadcast_to([P, 384])).then_inc(w_sem, 16)
                sp.dma_start(rope[:, :, :], io["rope"]).then_inc(w_sem, 16)

                def store(t, s):
                    sp.wait_ge(b_done, t + 3)
                    sp.dma_start(io["qrow"][bass.ds(t * P, P), :], qrow[s][:, :]).then_inc(q_out[s], 16)
                    sp.wait_ge(zc_rdy, t + 1)
                    sp.dma_start(io["zc"][bass.ds(conv_row(t), P), :], zc[s][:, :]).then_inc(q_out[s], 16)

                for n, (a, b) in list(enumerate(U_CHUNKS))[1:]:
                    sp.dma_start(w_in[:, :, a:b], io["w_in"][l, :, :, a:b]).then_inc(w_in_in[n], 16)
                sp.wait_ge(half_rdy, 2)
                for row in (0, LAT + 1, ZROWS - 1):
                    sp.dma_start(io["zc"][row:row + 1, :], zero_row[0:1, :]).then_inc(zero_out, 16)
                for s in range(2):
                    sp.sem_inc(q_out[s], 32)
                with sp.Fori(0, NT_LAT // 2) as r:
                    for s in range(2):
                        sp.wait_ge(xT_ps, r * 2 + s + 1)
                        load(r * 2 + s + 2, s)
                        store(r * 2 + s, s)
                for t in range(NT_LAT, NT):
                    store(t, t % 2)
                sp.wait_ge(zero_out, 48)
                for s in range(2):
                    sp.wait_ge(q_out[s], 32 + 32 * (NT // 2))

            @block.tensor
            def _(pe):
                def transpose_x(t, s, r):
                    pe.wait_ge(x_in[s], r * 16 + 16)
                    for k in range(KD):
                        tr = pe.transpose(ps[:, 2560 + k * P:2560 + (k + 1) * P], xt[s][:, k * P:(k + 1) * P],
                                          ident[:, :])
                    tr.then_inc(xT_ps, 1)

                def product(t, s, n, first):
                    if first:
                        pe.wait_ge(w_in_in[n], 16)
                    pe.wait_ge(u_rdy, t * 5 + n + 1)
                    a, b = U_CHUNKS[n]
                    for k in range(KD):
                        mm = pe.matmul(ps[:, n * 512:n * 512 + b - a], hT[s][:, k, :], w_in[:, k, a:b],
                                       start=(k == 0), stop=(k == KD - 1))
                    mm.then_inc(u_ps, 1)

                def rest(t, s, part):
                    if part == 1:
                        pe.wait_ge(kmT_rdy, t + 2)
                        pe.wait_ge(a_step, t * A_STEPS + A_STEPS)
                        for j, a in enumerate((U_CQ, U_CQ + P, U_CKV)):
                            tr = pe.transpose(ps[:, 3584 + j * P:3584 + (j + 1) * P], u[s][:, a:a + P], ident[:, :])
                        tr.then_inc(latT_ps, 1)
                        for j in range(3):
                            tr = pe.transpose(ps[:, 2560 + j * P:2560 + (j + 1) * P], kdg[s][:, j * P:(j + 1) * P],
                                              ident[:, :])
                        tr.then_inc(kT_ps, 1)
                    elif part == 2:
                        pe.wait_ge(latT_rdy, t + 1)
                        for j in range(2):
                            mm = pe.matmul(ps[:, 3072:3072 + 384], latT[:, j, :], w_q[:, j, :], start=(j == 0),
                                           stop=(j == 1))
                        mm.then_inc(q_ps, 1)
                        pe.matmul(ps[:, 3584:4096], latT[:, 2, :], w_kv[:, :], start=True,
                                  stop=True).then_inc(kv_ps, 1)
                    elif part == 3:
                        pe.wait_ge(kT_rdy, t + 1)
                        pe.wait_ge(kv_rdy, t + 1)
                        for h in range(MLA_H):
                            tr = pe.transpose(ps[0:MLA_QK, 2560 + h * P:2560 + (h + 1) * P], ka[s][:, h, :],
                                              ident[:, :])
                        tr.then_inc(kmT_ps, 1)

                def body(t, s, r, prev, nxt, ctxt):
                    pe.wait_ge(hT_rdy, t * 2 + 2)
                    for n in range(len(U_CHUNKS)):
                        product(t, s, n, not prev)
                        if n == 0 and nxt:
                            pe.wait_ge(kmT_rdy, t + 1)
                            transpose_x(t + 1, 1 - s, r + s)
                        if n == 1 and nxt:
                            pe.wait_ge(hT_rdy, t * 2 + 4)
                        if prev:
                            rest(t - 1, 1 - s, n)

                transpose_x(0, 0, 0)
                pe.wait_ge(w_sem, 16 * 5)
                pipelined(pe, body)
                for part in range(1, 4):
                    rest(NT - 1, (NT - 1) % 2, part)

            @block.scalar
            def _(act):
                act.sem_inc(u_rdy, 5)
                act.sem_inc(kmT_rdy, 2)

                def modulate(t, s, ctxt):
                    act.wait_ge(xT_ps, t + 1)
                    for k in range(KD // 2):
                        op = act.activation(hT[s][:, k, :], ps[:, 2560 + k * P:2560 + (k + 1) * P], ACT.Identity,
                                            bias=keep["shift1"][:, k, ctxt:ctxt + 1],
                                            scale=keep["scale1"][:, k, ctxt:ctxt + 1])
                    op.then_inc(hT_rdy, 1)

                def read_product(t, s, n):
                    a, b = U_CHUNKS[n]
                    act.wait_ge(u_ps, t * 5 + n + 1)
                    b0 = n * 512
                    if a == GATE_B:
                        act.copy(qrow[s][:, QB:QB + CONV], ps[:, b0:b0 + CONV])
                        op = act.copy(u[s][:, U_CQ:U_CQ + 256], ps[:, b0 + 256:b0 + 512])
                    elif a == DV:
                        act.copy(kv["vd"][:, bass.ds(t, 1), :], ps[:, b0:b0 + 256].unsqueeze(1))
                        act.copy(kv["vg"][:, bass.ds(t, 1), :], ps[:, b0 + 256:b0 + 384].unsqueeze(1))
                        op = act.copy(u[s][:, U_KR:U_KR + 32], ps[:, b0 + 384:b0 + 416])
                    else:
                        ua = U_OF[a]
                        op = act.copy(u[s][:, ua:ua + b - a], ps[:, b0:b0 + b - a])
                    op.then_inc(u_rdy, 1)

                def squares(t, s):
                    act.wait_ge(u_rdy, t * 5 + 10)
                    act.wait_ge(rs_rdy, t + 1)
                    act.activation(junk[:, :], u[s][:, U_CQ:U_CQ + 256], ACT.Square, scale=256 ** -0.5,
                                   accum_out=ss[:, 0:1]).then_inc(sq_rdy, 1)
                    act.wait_ge(sq_rdy, t * 2 + 1)
                    act.activation(junk[:, 0:128], u[s][:, U_CKV:U_CKV + 128], ACT.Square, scale=128 ** -0.5,
                                   accum_out=ss[:, 1:2]).then_inc(sq_rdy, 1)

                def rest(t, s, part):
                    if part == 1:
                        act.wait_ge(latT_ps, t + 1)
                        for j in range(3):
                            op = act.activation(latT[:, j, :], ps[:, 3584 + j * P:3584 + (j + 1) * P], ACT.Copy,
                                                scale=lat_gain[:, j:j + 1])
                        op.then_inc(latT_rdy, 1)
                        act.wait_ge(kT_ps, t + 1)
                        act.copy(kv["kd"][:, :, bass.ds(t * P, P)],
                                 ps[:, 2560:2560 + 2 * P].rearrange("p (j n) -> p j n", j=2))
                        act.copy(kv["kg"][:, bass.ds(t * P, P)], ps[:, 2560 + 2 * P:2560 + 3 * P]).then_inc(kT_rdy, 1)
                    elif part == 2:
                        act.wait_ge(kv_ps, t + 1)
                        act.copy(ka[s][:, :, 0:MLA_NOPE],
                                 ps[:, 3584:3584 + 256].rearrange("p (h n) -> p h n", h=MLA_H)).then_inc(kv_rdy, 1)
                        act.copy(kv["vm"][:, bass.ds(t, 1), :], ps[:, 3840:4096].unsqueeze(1))
                        act.wait_ge(q_ps, t + 1)
                        act.copy(qrow[s][:, 0:384], ps[:, 3072:3072 + 384]).then_inc(q_rdy, 1)
                    elif part == 3:
                        act.wait_ge(kmT_ps, t + 1)
                        act.copy(kv["km"][:, :, bass.ds(t * P, P)],
                                 ps[0:MLA_QK, 2560:3072].rearrange("p (h n) -> p h n", h=MLA_H)).then_inc(kmT_rdy, 1)

                def body(t, s, r, prev, nxt, ctxt):
                    act.wait_ge(b_done, t + 1)
                    act.wait_ge(q_out[s], r * 32 + 32)
                    for n in range(len(U_CHUNKS)):
                        read_product(t, s, n)
                        if n == 0 and nxt:
                            modulate(t + 1, 1 - s, ctxt)
                        if prev:
                            rest(t - 1, 1 - s, n)
                    squares(t, s)

                modulate(0, 0, 0)
                act.wait_ge(w_sem, 16 * 5)
                pipelined(act, body)
                for part in range(1, 4):
                    rest(NT - 1, (NT - 1) % 2, part)

            @block.gpsimd
            def _(pool):
                pool.memset(neg_half[:, :], -0.5).then_inc(half_rdy, 1)
                pool.memset(zero_row[:, :], 0.0).then_inc(half_rdy, 1)
                pool.wait_ge(half_rdy, 2)
                pool.sem_inc(rs_rdy, 1)
                if l == 0:
                    for b in range(MAX_OVER):
                        pool.dma_start(
                            io["ys"][(NE + b) * P:(NE + b + 1) * P, :].rearrange("p (a n) -> p a n", n=CONV),
                            zero_row[:, :].unsqueeze(1).broadcast_to([P, D // CONV, CONV])).then_inc(ys_zeroed, 16)

                def head(t, s, r):
                    pool.wait_ge(u_rdy, t * 5 + 10)
                    pool.wait_ge(q_out[s], r * 32 + 32)
                    pool.tensor_tensor(zc[s][:, :], u[s][:, 0:CONV], u[s][:, CONV:2 * CONV],
                                       ALU.mult).then_inc(zc_rdy, 1)
                    pool.wait_ge(a_step, t * A_STEPS + VAR_STEP)
                    pool.tensor_tensor(rs[:, :], ss[:, :], neg_half[:, :], ALU.pow).then_inc(rs_rdy, 1)

                in_pairs(pool, NT, head)
                if l == 0:
                    pool.wait_ge(ys_zeroed, 16 * MAX_OVER)

            @block.vector
            def _(dve):
                dve.sem_inc(b_done, 2)
                sa, sbb = Steps(dve, a_step, A_STEPS), Steps(dve, b_step, 1)

                def rotate(z, n, w, t, steps):
                    q = w // 4
                    at = 0 if w == 32 else 64
                    cos = rope[:, bass.ds(t, 1), at:at + w].broadcast_to([P, n, w])
                    sin = rope[:, bass.ds(t, 1), at + w:at + 2 * w]
                    dve.tensor_tensor(t1[:, 0:n * w].rearrange("p (h w) -> p h w", h=n), z, cos, ALU.mult)
                    sin4 = sin.rearrange("p h (a b q) -> p h a b q", a=2, b=2)
                    out5 = t2[:, 0:n * w].rearrange("p (h a b q) -> p h a b q", a=2, b=2, q=q)
                    z5 = z.rearrange("p h (a b q) -> p h a b q", a=2, b=2)
                    for b in range(2):
                        last = dve.tensor_tensor(out5[:, :, :, b, :], z5[:, :, :, 1 - b, :],
                                                 sin4[:, :, :, b, :].broadcast_to([P, n, 2, q]), ALU.mult)
                    steps.after(last)

                def modulate(t, s, ctxt):
                    dve.wait_ge(xT_ps, t + 1)
                    for k in range(KD // 2, KD):
                        op = dve.tensor_scalar(hT[s][:, k, :], ps[:, 2560 + k * P:2560 + (k + 1) * P],
                                               keep["scale1"][:, k, ctxt:ctxt + 1],
                                               keep["shift1"][:, k, ctxt:ctxt + 1], ALU.mult, ALU.add)
                    op.then_inc(hT_rdy, 1)

                def head(t, s, r):
                    sa.begin(t)
                    dve.wait_ge(b_done, t + 2)
                    dve.wait_ge(u_rdy, t * 5 + 10)
                    gqk = u[s][:, U_GQ:U_GQ + 384]
                    sa.after(dve.scalar_tensor_tensor(t1[:, 0:384], gqk, 1.0 / HD, gqk, ALU.mult, ALU.mult))
                    sa.after(dve.tensor_reduce(ss[:, 2:8], t1[:, 0:384].rearrange("p (h n) -> p h n", n=HD), AX_X,
                                               ALU.add))
                    dve.wait_ge(sq_rdy, t * 2 + 2)
                    sa.after(dve.tensor_scalar(ss[:, :], ss[:, :], EPS, None, ALU.add))
                    dve.tensor_tensor(gqk, gqk, qk_gain[:, :], ALU.mult)
                    z = u[s][:, U_DQ:U_DQ + 512].rearrange("p (h w) -> p h w", w=32)
                    rotate(z, 16, 32, t, sa)
                    dve.wait_ge(q_out[s], r * 32 + 32)
                    dve.tensor_tensor(qrow[s][:, QD:QD + 256], t1[:, 0:256], t2[:, 0:256], ALU.add)
                    sa.after(dve.tensor_tensor(kdg[s][:, 0:256], t1[:, 256:512], t2[:, 256:512], ALU.add))
                    z = u[s][:, U_KR:U_KR + 32].rearrange("p (h w) -> p h w", w=32)
                    rotate(z, 1, 32, t, sa)
                    dve.wait_ge(kmT_rdy, t + 1)
                    sa.after(dve.tensor_tensor(ka[s][:, :, MLA_NOPE:MLA_QK],
                                               t1[:, 0:32].unsqueeze(1).broadcast_to([P, MLA_H, 32]),
                                               t2[:, 0:32].unsqueeze(1).broadcast_to([P, MLA_H, 32]), ALU.add))
                    dve.wait_ge(rs_rdy, t + 2)
                    for a, b, j in ((U_CQ, U_CQ + 256, 0), (U_CKV, U_CKV + 128, 1)):
                        dve.tensor_scalar(u[s][:, a:b], u[s][:, a:b], rs[:, j:j + 1], None, ALU.mult)
                    g3 = gqk.rearrange("p (h n) -> p h n", n=HD)
                    sa.after(dve.tensor_tensor(g3, g3, rs[:, 2:8].unsqueeze(2).broadcast_to([P, 6, HD]), ALU.mult))
                    rotate(g3, 6, 64, t, sa)
                    dve.tensor_tensor(qrow[s][:, QG:QG + 256].rearrange("p (g k n) -> p k g n", g=2, k=2),
                                      t1[:, 0:256].rearrange("p (k g n) -> p k g n", g=2, k=2),
                                      t2[:, 0:256].rearrange("p (k g n) -> p k g n", g=2, k=2), ALU.add)
                    sa.after(dve.tensor_tensor(kdg[s][:, 256:384], t1[:, 256:384], t2[:, 256:384], ALU.add))
                    sa.end()

                def tail(t, s):
                    sbb.begin(t)
                    dve.wait_ge(q_rdy, t + 1)
                    z = qrow[s][:, 0:384].rearrange("p (h w) -> p h w", w=MLA_QK)[:, :, MLA_NOPE:MLA_QK]
                    rotate(z, 4, 32, t, sbb)
                    dve.tensor_tensor(z, t1[:, 0:128].rearrange("p (h w) -> p h w", w=32),
                                      t2[:, 0:128].rearrange("p (h w) -> p h w", w=32), ALU.add).then_inc(b_done, 1)
                    sbb.end()

                def body(t, s, r, prev, nxt, ctxt):
                    if prev:
                        head(t - 1, 1 - s, r - 1 + s)
                    if nxt:
                        modulate(t + 1, 1 - s, ctxt)
                    if prev:
                        tail(t - 1, 1 - s)

                modulate(0, 0, 0)
                dve.wait_ge(w_sem, 16 * 5)
                pipelined(dve, body)
                head(NT - 1, (NT - 1) % 2, NT // 2 - 1)
                tail(NT - 1, (NT - 1) % 2)


def layer_norm_steps(dve, st, z, stats, mv, tick, eps_step):
    for j in range(2):
        op = dve.bn_stats(stats[:, j, :], z[:, j * 512:(j + 1) * 512])
    st.after(op)
    dve.memset(tick[:, :], 0.0)
    st.after(dve.bn_aggr(mv[:, :], stats[:, :, :]))
    eps_step(dve.tensor_scalar(mv[:, 1:2], mv[:, 1:2], EPS, None, ALU.add))


ITEMS = []
for _h in range(4):
    ITEMS += [("diff", _h, [3 * _h, 3 * _h + 1]), ("mla", _h, [3 * _h + 2])]
ITEMS += [("gqa", _h, [12 + _h]) for _h in range(4)]
ITEM_OF = {u: n for n, (_, _, us) in enumerate(ITEMS) for u in us}
NI, NU = len(ITEMS), 16
TRANSPOSE_IN = {3: 0, 5: 1, 7: 2, 8: 3, 10: 4, 11: 5, 13: 6, 14: 7, 15: 8}
TRANSPOSE_LATE = {0: 9, 1: 10, 2: 11}
VALUES_IN = {6: 0, 7: 1, 8: 2, 9: 3, 11: 4, 12: 5, 14: 6, 15: 7}
VALUES_LATE = {0: 8, 1: 9, 2: 10, 3: 11}
BACK_IN = {u + 1: n for u, n in VALUES_IN.items() if u + 1 < NU}
BACK_LATE = {0: 7, 1: 8, 2: 9, 3: 10, 4: 11}
Y_SLOT, WO_SLOTS, Q_SLOTS = 4, (4, 5), (6, 9)
LN_SLOTS = (6, 8, 9, 11, 12)


def tile_bodies(eng, n, body):
    body(0, 0, 0, True, False, True)
    if n > 2:
        with eng.Fori(0, n // 2 - 1) as r:
            body(r * 2 + 1, 1, r, True, True, True)
            body(r * 2 + 2, 0, r + 1, True, True, True)
    body(n - 1, 1, n // 2 - 1, True, True, False)
    body(n, 0, n // 2, False, True, False)


def attend(nc, l, io, c, kv, stream):
    t0 = 0 if stream == 0 else NT_LAT
    n_tiles = NT_LAT if stream == 0 else NT_CTX
    key_tiles = list(range(NT)) if stream == 0 else list(range(NT_LAT, NT))
    k0, nk = key_tiles[0] * P, len(key_tiles) * P
    chunks = [key_tiles[a:a + 4] for a in range(0, len(key_tiles), 4)]
    nch = len(chunks)
    NCHT = NI * nch
    S_AT, T_AT, O_AT = [0, 1536], 3072, 3584
    SCALE = {"mla": MLA_SCALE, "diff": DIFF_SCALE, "gqa": GQA_SCALE}
    lam_init = 0.8 - 0.6 * math.exp(-0.3 * l)
    OWN = NU + 2 * DIFF_H + 3 + 2
    LATE = 5 + 2 + 1 + 2 + 2
    x_src = io["x_in"] if l == 0 else io["x_mid"]

    ctx = ExitStack()
    sb = lambda n, s, d=F32: ctx.enter_context(nc.sbuf_tensor(f"at_{n}_{l}{stream}", s, d))
    sem = phase_semaphores(nc, ctx, lambda n: f"at_{n}_{l}{stream}")
    with ctx:
        w_out = sb("w_out", [P, KD, D])
        gate1, scale2, shift2 = sb("gate1", [P, D]), sb("scale2", [P, D]), sb("shift2", [P, D])
        ln_g, ln_b = sb("ln_g", [P, D]), sb("ln_b", [P, D])
        conv_w = sb("conv_w", [P, 3, CONV])
        dl = sb("dl", [P, 4, 32])
        dlp = sb("dlp", [P, 2, 32])
        dle = sb("dle", [P, 2])
        neg_lam = sb("neg_lam", [P, 1])
        subln = sb("subln", [P, HD])
        neg_half = sb("neg_half", [P, 4])
        qin = [sb(f"qin{j}", [P, Q_W]) for j in range(2)]
        zin = [sb(f"zin{j}", [P, 3, CONV]) for j in range(2)]
        xin = [sb(f"xin{j}", [P, D]) for j in range(2)]
        qT = [sb(f"qT{j}", [P, 8, P]) for j in range(2)]
        prob = [sb(f"prob{j}", [P, nk]) for j in range(4)]
        pT = [sb(f"pT{j}", [P, nk]) for j in range(2)]
        y = [sb(f"y{j}", [P, D]) for j in range(2)]
        oT = sb("oT", [HD, P])
        yT = sb("yT", [P, KD, P])
        z = sb("z", [P, D])
        x1 = [sb(f"x1{j}", [P, D]) for j in range(2)]
        h2 = sb("h2", [P, D])
        mx, nm, rs, ri = sb("mx", [P, NU]), sb("nm", [P, NU]), sb("rs", [P, NU]), sb("ri", [P, NU])
        coef = sb("coef", [P, DIFF_H])
        dsq = z[:, 0:DIFF_H * HD]
        dss, drs = sb("dss", [P, 4]), sb("drs", [P, 4])
        stats, mv, rstd = sb("stats", [P, 2, 6]), sb("mv", [P, 2]), sb("rstd", [P, 1])
        tick = sb("tick", [P, 1])
        ps, ident = c["ps"], c["ident"]
        w_sem, rows_in, w_out_in = sem("weights_in"), sem("rows_in"), sem("w_out_in")
        q_in = [sem(f"q_in{j}") for j in range(2)]
        x_in = [sem(f"x_in{j}") for j in range(2)]
        x1_out = [sem(f"x1_out{j}") for j in range(2)]
        h_out = sem("h_out")
        setup, lam_exp, lam_rdy, half_rdy = sem("setup"), sem("lam_exp"), sem("lam_rdy"), sem("half_rdy")
        qT_ps, qT_rdy, s_rdy, m_rdy, exp_done, comb_done = (
            sem("qT_ps"), sem("qT_rdy"), sem("s_rdy"), sem("m_rdy"), sem("exp_done"), sem("comb_done"))
        t_ps, t_ev, pv_done, oT_rdy, back_ps, o_ev = (
            sem("t_ps"), sem("t_ev"), sem("pv_done"), sem("oT_rdy"), sem("back_ps"), sem("o_ev"))
        own, late, dvar_rdy, drs_rdy, y_rdy, conv_rdy, conv_step = (
            sem("own"), sem("late"), sem("dvar_rdy"), sem("drs_rdy"), sem("y_rdy"), sem("conv_rdy"), sem("conv_step"))
        yT_ps, yT_rdy, wo_ps, z_read, var_rdy, rstd_rdy, x1_rdy, h_step, h_rdy = (
            sem("yT_ps"), sem("yT_rdy"), sem("wo_ps"), sem("z_read"), sem("var_rdy"), sem("rstd_rdy"),
            sem("x1_rdy"), sem("h_step"), sem("h_rdy"))

        def row(t):
            return bass.ds(t * P + t0 * P, P)

        with nc.Block() as block:
            @block.sync
            def _(sp):
                def load_q(t, s):
                    z0 = t * P + (t0 * P + 1 + stream)
                    sp.dma_start(qin[s][:, :], io["qrow"][row(t), :]).then_inc(q_in[s], 16)
                    for j in range(3):
                        sp.dma_start(zin[s][:, j, :], io["zc"][bass.ds(z0 + j - 1, P), :]).then_inc(q_in[s], 16)

                def load_x(t, s):
                    sp.dma_start(xin[s][:, :], x_src[row(t), :]).then_inc(x_in[s], 16)

                def body(t, s, more_q, more_x):
                    if more_q:
                        sp.wait_ge(conv_rdy, t + 1)
                        sp.wait_ge(qT_ps, t * 2 + 2)
                        load_q(t + 2, s)
                    if not isinstance(t, int) or t > 0:
                        sp.wait_ge(x1_rdy, t)
                        sp.dma_start(io["x_post"][row(t - 1), :], x1[1 - s][:, :]).then_inc(x1_out[1 - s], 16)
                        sp.wait_ge(h_rdy, t)
                        sp.dma_start(io["h2"][row(t - 1), :], h2[:, :]).then_inc(h_out, 16)
                    if more_x:
                        load_x(t + 1, 1 - s)

                for s in range(2):
                    sp.sem_inc(x1_out[s], 16)
                sp.sem_inc(h_out, 16)
                load_q(0, 0)
                mod = lambda v: io["mod"][l, stream:stream + 1, v * D:(v + 1) * D].broadcast_to([P, D])
                sp.dma_start(dl[:, :, :].rearrange("p j n -> p (j n)"),
                             io["lambda"][l:l + 1, :].broadcast_to([P, P])).then_inc(w_sem, 16)
                for dst, src in ((subln, io["subln"][l:l + 1, :].broadcast_to([P, HD])), (scale2, mod(4))):
                    sp.dma_start(dst[:, :], src).then_inc(w_sem, 16)
                sp.dma_start(conv_w[:, :, :].rearrange("p j n -> p (j n)"),
                             io["conv_w"][l:l + 1, :].broadcast_to([P, 3 * CONV])).then_inc(rows_in, 16)
                for dst, src in ((gate1, mod(2)), (shift2, mod(3)),
                                 (ln_g, io["ln"][l, 0:1, :].broadcast_to([P, D])),
                                 (ln_b, io["ln"][l, 1:2, :].broadcast_to([P, D]))):
                    sp.dma_start(dst[:, :], src).then_inc(rows_in, 16)
                load_q(1, 1)
                load_x(0, 0)
                load_x(1, 1)
                sp.dma_start(w_out[:, :, :], io["w_out"][l]).then_inc(w_out_in, 16)
                body(0, 0, n_tiles > 2, False)
                if n_tiles > 2:
                    with sp.Fori(0, n_tiles // 2 - 2) as r:
                        body(r * 2 + 1, 1, True, True)
                        body(r * 2 + 2, 0, True, True)
                    for t in range(n_tiles - 3, n_tiles - 1):
                        body(t, t % 2, t + 2 < n_tiles, True)
                body(n_tiles - 1, 1, False, False)
                body(n_tiles, 0, False, False)
                for s in range(2):
                    sp.wait_ge(x1_out[s], 16 + 16 * (n_tiles // 2))
                sp.wait_ge(h_out, 16 + 16 * n_tiles)

            @block.tensor
            def _(pe):
                def scores(u, s):
                    kind, h, us = ITEMS[ITEM_OF[u]]
                    if kind == "mla":
                        q, kk = qT[s][0:MLA_QK, h, :], kv["km"][0:MLA_QK, h, :]
                    elif kind == "diff":
                        m = 2 * h + us.index(u)
                        b = 32 * (m % 4)
                        q, kk = qT[s][b:b + 32, 4 + m // 4, :], kv["kd"][b:b + 32, m // 4, :]
                    else:
                        b = 64 * (h // 2)
                        q, kk = qT[s][b:b + 64, 6 + h % 2, :], kv["kg"][b:b + 64, :]
                    at = S_AT[u % 2]

                    def bank(a):
                        e = min(a + 512, nk)
                        mm = pe.matmul(ps[:, at + a:at + e], q, kk[:, k0 + a:k0 + e], start=True, stop=True)
                        if e == nk:
                            mm.then_inc(s_rdy, 1)

                    return [lambda a=a: bank(a) for a in range(0, nk, 512)]

                def transposes(t, n, after):
                    kind, h, us = ITEMS[n]

                    def chunk(ci):
                        if ci == 0:
                            if kind == "diff":
                                pe.wait_ge(comb_done, t * DIFF_H + h + 1)
                            else:
                                pe.wait_ge(exp_done, t * NU + us[0] + 1)
                            after()
                        pe.wait_ge(t_ev, t * NCHT + n * nch + ci + 1)
                        for j in range(len(chunks[ci])):
                            a = (ci * 4 + j) * P
                            tr = pe.transpose(ps[:, T_AT + j * P:T_AT + (j + 1) * P], prob[us[0] % 4][:, a:a + P],
                                              ident[:, :])
                        tr.then_inc(t_ps, 1)

                    return [lambda ci=ci: chunk(ci) for ci in range(nch)]

                def values(t, n, after_projection):
                    kind, h, us = ITEMS[n]
                    vt, vc = {"mla": (kv["vm"], h * HD), "diff": (kv["vd"], h * HD),
                              "gqa": (kv["vg"], (h // 2) * HD)}[kind]

                    def chunk(ci):
                        if ci == 0:
                            if after_projection:
                                pe.wait_ge(z_read, t * 2)
                            pe.wait_ge(o_ev, t * NI + n + 1)
                        pe.wait_ge(t_ev, t * NCHT + n * nch + ci + 2)
                        for j, kt in enumerate(chunks[ci]):
                            k = ci * 4 + j
                            mm = pe.matmul(ps[0:HD, O_AT:O_AT + P], vt[:, kt, vc:vc + HD],
                                           pT[n % 2][:, k * P:(k + 1) * P], start=(k == 0),
                                           stop=(k == len(key_tiles) - 1))
                        if ci == nch - 1:
                            mm.then_inc(pv_done, 1)

                    return [lambda ci=ci: chunk(ci) for ci in range(nch)]

                def turn_back(t, n):
                    pe.wait_ge(oT_rdy, t * NI + n + 1)
                    pe.matmul(ps[:, O_AT + P:O_AT + P + HD], oT[:, :], ident[0:HD, 0:HD], start=True,
                              stop=True).then_inc(back_ps, 1)

                def y_part(t, s, part, own):
                    if part == 0:
                        pe.wait_ge(conv_rdy, t + 1)
                        pe.wait_ge(y_rdy, t + 1)
                        pe.wait_ge(t_ev, (t + 1) * NCHT + (nch if own else 0) + 1)
                    else:
                        pe.wait_ge(yT_rdy, t * 2 + 1)
                    for j in range(4):
                        k = part * 4 + j
                        tr = pe.transpose(ps[:, T_AT + j * P:T_AT + (j + 1) * P], y[s][:, k * P:(k + 1) * P],
                                          ident[:, :])
                    tr.then_inc(yT_ps, 1)

                def q_part(t, s, r, part):
                    pe.wait_ge(q_in[s], r * 64 + 64)
                    for j in range(4):
                        w = P if part else MLA_QK
                        a = QD + j * P if part else j * MLA_QK
                        tr = pe.transpose(ps[0:w, T_AT + j * P:T_AT + (j + 1) * P], qin[s][:, a:a + w], ident[:, :])
                    tr.then_inc(qT_ps, 1)

                def project_out(t, half):
                    if half == 0:
                        pe.wait_ge(w_out_in, 16)
                        pe.wait_ge(o_ev, (t + 1) * NI + 1)
                        pe.wait_ge(yT_rdy, t * 2 + 1)
                    else:
                        pe.wait_ge(z_read, t * 2 + 1)
                    for k in range(KD):
                        if half == 0 and k == KD // 2:
                            pe.wait_ge(yT_rdy, t * 2 + 2)
                        mm = pe.matmul(ps[:, O_AT:O_AT + 512], yT[:, k, :], w_out[:, k, half * 512:(half + 1) * 512],
                                       start=(k == 0), stop=(k == KD - 1))
                    mm.then_inc(wo_ps, 1)

                def body(t, s, r, cur, prev, nxt):
                    if cur:
                        pe.wait_ge(qT_rdy, t * 2 + 2)
                    for u in range(NU if cur else WO_SLOTS[-1] + 1):
                        qk = scores(u, s) if cur else []
                        if cur and (u >= 2 or prev):
                            pe.wait_ge(exp_done, t * NU + u - 1)
                        tr = []
                        if cur and u in TRANSPOSE_IN:
                            def after(u=u):
                                if TRANSPOSE_IN[u] == 1 and prev:
                                    pe.wait_ge(yT_rdy, t * 2)
                                for part in range(2):
                                    if nxt and u == Q_SLOTS[part] + 1:
                                        pe.wait_ge(qT_rdy, t * 2 + 3 + part)
                            tr = transposes(t, TRANSPOSE_IN[u], after)
                        if prev and u in TRANSPOSE_LATE:
                            tr = transposes(t - 1, TRANSPOSE_LATE[u], lambda: None)
                        if prev and u == Y_SLOT:
                            tr = [lambda p=p: y_part(t - 1, 1 - s, p, cur) for p in range(2)]
                        back, pv = [], []
                        if prev and u in BACK_LATE:
                            back.append(lambda: turn_back(t - 1, BACK_LATE[u]))
                        if cur and u in BACK_IN:
                            back.append(lambda: turn_back(t, BACK_IN[u]))
                        if prev and u in VALUES_LATE:
                            pv = values(t - 1, VALUES_LATE[u], False)
                        if cur and u in VALUES_IN:
                            pv = values(t, VALUES_IN[u], VALUES_IN[u] == 0 and prev)
                        kinds = {"q": qk, "t": tr, "b": back, "v": pv}
                        for kind in ("qbqtqt" if u == Y_SLOT else "qtqbtqvtvv"):
                            if kinds[kind]:
                                kinds[kind].pop(0)()
                        assert not any(kinds.values())
                        if prev and u in WO_SLOTS:
                            project_out(t - 1, WO_SLOTS.index(u))
                        if nxt and u in Q_SLOTS:
                            part = Q_SLOTS.index(u)
                            n = max(TRANSPOSE_IN[v] for v in TRANSPOSE_IN if v <= u)
                            pe.wait_ge(t_ev, t * NCHT + (n + 1) * nch + 1)
                            q_part(t + 1, 1 - s, r + (1 if s else 0), part)

                q_part(0, 0, 0, 0)
                pe.wait_ge(qT_rdy, 1)
                q_part(0, 0, 0, 1)
                tile_bodies(pe, n_tiles, body)

            @block.scalar
            def _(act):
                act.sem_inc(t_ev, 1)
                act.wait_ge(setup, 2)
                act.activation(dle[:, :], dle[:, :], ACT.Exp).then_inc(lam_exp, 1)

                def read_q(t, s, part):
                    act.wait_ge(qT_ps, t * 2 + 1 + part)
                    w = P if part else MLA_QK
                    act.copy(qT[s][0:w, part * 4:part * 4 + 4, :],
                             ps[0:w, T_AT:T_AT + 512].rearrange("p (j n) -> p j n", j=4)).then_inc(qT_rdy, 1)

                def read_output(t, n):
                    act.wait_ge(pv_done, t * NI + n + 1)
                    act.copy(oT[:, :], ps[0:HD, O_AT:O_AT + P]).then_inc(oT_rdy, 1)

                def read_probs(t, n, may_wait):
                    for ci in range(nch):
                        if ci == 0 and may_wait:
                            act.wait_ge(pv_done, t * NI + n - 1)
                        act.wait_ge(t_ps, t * NCHT + n * nch + ci + 1)
                        w = len(chunks[ci]) * P
                        act.copy(pT[n % 2][:, ci * 512:ci * 512 + w], ps[:, T_AT:T_AT + w]).then_inc(t_ev, 1)

                def body(t, s, r, cur, prev, nxt):
                    for u in range(NU if cur else WO_SLOTS[-1] + 1):
                        if prev and u in BACK_LATE:
                            read_output(t - 1, BACK_LATE[u])
                        if cur and u in BACK_IN:
                            read_output(t, BACK_IN[u])
                        if cur and u in TRANSPOSE_IN:
                            n = TRANSPOSE_IN[u]
                            read_probs(t, n, n >= 2 or prev)
                        if prev and u in TRANSPOSE_LATE:
                            read_probs(t - 1, TRANSPOSE_LATE[u], True)
                        if prev and u == Y_SLOT:
                            for part in range(2):
                                act.wait_ge(yT_ps, t * 2 - 1 + part)
                                act.copy(yT[:, part * 4:part * 4 + 4, :],
                                         ps[:, T_AT:T_AT + 512].rearrange("p (j n) -> p j n", j=4)).then_inc(yT_rdy, 1)
                        if cur:
                            kind = ITEMS[ITEM_OF[u]][0]
                            act.wait_ge(m_rdy, t * NU + u + 1)
                            at = S_AT[u % 2]
                            act.activation(prob[u % 4][:, :], ps[:, at:at + nk], ACT.Exp, bias=nm[:, u:u + 1],
                                           scale=SCALE[kind], accum_out=rs[:, u:u + 1]).then_inc(exp_done, 1)
                        if nxt and u in Q_SLOTS:
                            read_q(t + 1, 1 - s, Q_SLOTS.index(u))

                read_q(0, 0, 0)
                read_q(0, 0, 1)
                tile_bodies(act, n_tiles, body)

            @block.vector
            def _(dve):
                dve.sem_inc(o_ev, 1)
                dve.wait_ge(w_sem, 16 * 3)
                dve.tensor_tensor(dlp[:, 0, :], dl[:, 0, :], dl[:, 1, :], ALU.mult)
                dve.tensor_tensor(dlp[:, 1, :], dl[:, 2, :], dl[:, 3, :], ALU.mult).then_inc(setup, 1)
                dve.wait_ge(setup, 1)
                dve.tensor_reduce(dle[:, :], dlp[:, :, :], AX_X, ALU.add).then_inc(setup, 1)
                dve.tensor_scalar(subln[:, :], subln[:, :], 1.0 - lam_init, None, ALU.mult)
                dve.tensor_scalar(scale2[:, :], scale2[:, :], 1.0, None, ALU.add).then_inc(lam_rdy, 1)
                dve.wait_ge(lam_exp, 1)
                dve.tensor_tensor(neg_lam[:, :], dle[:, 1:2], dle[:, 0:1], ALU.subtract).then_inc(lam_rdy, 1)
                dve.wait_ge(lam_rdy, 2)
                dve.tensor_scalar(neg_lam[:, :], neg_lam[:, :], -lam_init, None, ALU.add).then_inc(lam_rdy, 1)
                dve.wait_ge(lam_rdy, 3)
                so, sl = Steps(dve, own, OWN), Steps(dve, late, LATE)

                def maximum(t, u):
                    kind, h, us = ITEMS[ITEM_OF[u]]
                    dve.wait_ge(s_rdy, t * NU + u + 1)
                    at = S_AT[u % 2]
                    so.after(dve.tensor_reduce(mx[:, u:u + 1], ps[:, at:at + nk], AX_X, ALU.max))
                    dve.tensor_scalar(nm[:, u:u + 1], mx[:, u:u + 1], -SCALE[kind], None, ALU.mult).then_inc(m_rdy, 1)
                    if kind == "diff" and u == us[1]:
                        dve.wait_ge(exp_done, t * NU + u + 1)
                        u = us[0]
                        so.after(dve.reciprocal(ri[:, u:u + 2], rs[:, u:u + 2]))
                        so.after(dve.tensor_scalar(coef[:, h:h + 1], ri[:, u + 1:u + 2], rs[:, u:u + 1], neg_lam[:, :],
                                                   ALU.mult, ALU.mult))
                        p0, p1 = prob[u % 4], prob[(u + 1) % 4]
                        dve.scalar_tensor_tensor(p0[:, :], p1[:, :], coef[:, h:h + 1], p0[:, :], ALU.mult,
                                                 ALU.add).then_inc(comb_done, 1)

                def output(t, s, n, st):
                    kind, h, us = ITEMS[n]
                    u = us[0]
                    if kind != "diff":
                        dve.wait_ge(exp_done, t * NU + u + 1)
                        st.after(dve.reciprocal(ri[:, u:u + 1], rs[:, u:u + 1]))
                    dve.wait_ge(back_ps, t * NI + n + 1)
                    col = {"mla": 256, "diff": 512, "gqa": 768}[kind] + h * 64
                    o = O_AT + P
                    dve.tensor_scalar(y[s][:, col:col + HD], ps[:, o:o + HD], ri[:, u:u + 1], None,
                                      ALU.mult).then_inc(o_ev, 1)

                def diff_squares(t, s):
                    dve.wait_ge(o_ev, t * NI + 7 + 1)
                    so.after(dve.scalar_tensor_tensor(dsq, y[s][:, 512:768], 1.0 / HD, y[s][:, 512:768],
                                                      ALU.mult, ALU.mult))
                    so.after(dve.tensor_reduce(dss[:, :], dsq.rearrange("p (h n) -> p h n", n=HD), AX_X, ALU.add))
                    dve.tensor_scalar(dss[:, :], dss[:, :], EPS, None, ALU.add).then_inc(dvar_rdy, 1)

                def diff_norm(t, s):
                    yd = y[s][:, 512:768].rearrange("p (h n) -> p h n", n=HD)
                    dve.wait_ge(drs_rdy, t + 1)
                    sl.after(dve.tensor_tensor(yd, yd, drs[:, :].unsqueeze(2).broadcast_to([P, 4, HD]), ALU.mult))
                    sl.after(dve.tensor_tensor(yd, yd, subln[:, :].unsqueeze(1).broadcast_to([P, 4, HD]), ALU.mult))

                def read_projection(t, half):
                    dve.wait_ge(rows_in, 16 * 5)
                    dve.wait_ge(wo_ps, t * 2 + 1 + half)
                    a = half * 512
                    dve.tensor_tensor(z[:, a:a + 512], ps[:, O_AT:O_AT + 512], gate1[:, a:a + 512],
                                      ALU.mult).then_inc(z_read, 1)

                def norm_part(t, s, r, part):
                    if part == 0:
                        dve.wait_ge(x_in[s], r * 16 + 16)
                        dve.wait_ge(z_read, t * 2 + 2)
                        sl.after(dve.scalar_tensor_tensor(z[:, :], xin[s][:, :], ALPHA, z[:, :], ALU.mult, ALU.add))
                    elif part == 1:
                        layer_norm_steps(dve, sl, z, stats, mv, tick, lambda op: op.then_inc(var_rdy, 1))
                    elif part == 2:
                        dve.wait_ge(rstd_rdy, t + 1)
                        sl.after(dve.tensor_scalar(z[:, :], z[:, :], mv[:, 0:1], rstd[:, :], ALU.subtract, ALU.mult))
                    elif part == 3:
                        sl.after(dve.tensor_tensor(z[:, :], z[:, :], ln_g[:, :], ALU.mult))
                    else:
                        dve.wait_ge(x1_out[s], r * 16 + 16)
                        dve.tensor_tensor(x1[s][:, :], z[:, :], ln_b[:, :], ALU.add).then_inc(x1_rdy, 1)
                        dve.wait_ge(x1_rdy, t + 1)

                def body(t, s, r, cur, prev, nxt):
                    rp = r if s else r - 1
                    if cur:
                        so.begin(t)
                    if prev:
                        sl.begin(t - 1)
                    for u in range(NU if cur else LN_SLOTS[-1] + 1):
                        if prev and u in BACK_LATE:
                            output(t - 1, 1 - s, BACK_LATE[u], sl)
                            if u == Y_SLOT - 2:
                                diff_norm(t - 1, 1 - s)
                            if u == Y_SLOT:
                                dve.wait_ge(o_ev, t * NI + 1)
                                dve.sem_inc(y_rdy, 1)
                        if cur and u in BACK_IN:
                            output(t, s, BACK_IN[u], so)
                        if cur:
                            maximum(t, u)
                        if prev:
                            if u in WO_SLOTS:
                                read_projection(t - 1, WO_SLOTS.index(u))
                            if u in LN_SLOTS:
                                norm_part(t - 1, 1 - s, rp, LN_SLOTS.index(u))
                        if cur and u == NU - 1:
                            diff_squares(t, s)
                    if cur:
                        so.end()
                    if prev:
                        sl.end()

                tile_bodies(dve, n_tiles, body)

            @block.gpsimd
            def _(pool):
                pool.memset(neg_half[:, :], -0.5).then_inc(half_rdy, 1)
                pool.wait_ge(half_rdy, 1)
                pool.wait_ge(rows_in, 16 * 5)
                pool.wait_ge(lam_rdy, 1)

                def body(t, s, r, cur, prev, nxt):
                    if prev:
                        pool.wait_ge(dvar_rdy, t)
                        pool.tensor_tensor(drs[:, :], dss[:, :], neg_half[:, :], ALU.pow).then_inc(drs_rdy, 1)
                    if cur:
                        cv = zin[s]
                        pool.wait_ge(q_in[s], r * 64 + 64)
                        pool.tensor_tensor(cv[:, :, :], zin[s][:, :, :], conv_w[:, :, :],
                                           ALU.mult).then_inc(conv_step, 1)
                        pool.wait_ge(conv_step, t * 3 + 1)
                        pool.tensor_tensor(cv[:, 0, :], cv[:, 0, :], cv[:, 1, :], ALU.add).then_inc(conv_step, 1)
                        pool.wait_ge(conv_step, t * 3 + 2)
                        pool.tensor_tensor(cv[:, 0, :], cv[:, 0, :], cv[:, 2, :], ALU.add).then_inc(conv_step, 1)
                        pool.wait_ge(conv_step, t * 3 + 3)
                        pool.tensor_tensor(y[s][:, 0:CONV], cv[:, 0, :], qin[s][:, QB:QB + CONV],
                                           ALU.mult).then_inc(conv_rdy, 1)
                    if prev:
                        pool.wait_ge(var_rdy, t)
                        pool.tensor_tensor(rstd[:, :], mv[:, 1:2], neg_half[:, 0:1], ALU.pow).then_inc(rstd_rdy, 1)
                        pool.wait_ge(x1_rdy, t)
                        pool.wait_ge(h_out, t * 16)
                        pool.tensor_tensor(h2[:, :], x1[1 - s][:, :], scale2[:, :], ALU.mult).then_inc(h_step, 1)
                        pool.wait_ge(h_step, t)
                        pool.tensor_tensor(h2[:, :], h2[:, :], shift2[:, :], ALU.add).then_inc(h_rdy, 1)

                tile_bodies(pool, n_tiles, body)


def experts(nc, l, io, c):
    nt = NT if l < DEPTH - 1 else NT_LAT
    n_over = (2 * nt * P - 1) // P
    NBLK = NE + n_over
    NL = NG + NE
    HT_AT, LT_AT, LG_AT, RK_AT, CNT_AT, IX_AT = (
        [0, 1024], [2048, 2560], 3072, 1536, 1536 + 384, 2048)
    UP_AT, GT_AT, HM_AT, DN_AT = [0, 512], 1024, 2048, 2560
    W_RING = 6
    OV_SLOT = 2
    PAIRS = (n_over + 1) // 2
    BIG = 3.0e38

    ctx = ExitStack()
    sb = lambda n, s, d=F32: ctx.enter_context(nc.sbuf_tensor(f"ex_{n}_{l}", s, d))
    sem = phase_semaphores(nc, ctx, lambda n: f"ex_{n}_{l}")
    with ctx:
        w13 = [sb(f"w13{j}", [P, KD, 2 * DE]) for j in range(W_RING)]
        w2 = [sb(f"w2{j}", [P, 2, D]) for j in range(W_RING)]
        w_route, b_route = sb("w_route", [P, KD, 36]), sb("b_route", [P, 36])
        before, ones = sb("before", [P, P]), sb("ones", [P, P])
        iota, token = sb("iota", [P, P]), sb("token", [P, NT])
        lgT = sb("lgT", [NL, nt * P])
        lg = sb("lg", [P, nt, 36])
        small = lambda n, w=nt: sb(n, [P, w])
        gmax, gsum, gi, m0, m1, i0, i1, e1 = [small(n) for n in ("gmax", "gsum", "gi", "m0", "m1", "i0", "i1", "e1")]
        g4, og = sb("g4", [P, nt, 4]), sb("og", [P, nt, 4])
        s84 = sb("s84", [P, nt, EPG, NG])
        s8, o8 = sb("s8", [P, nt, EPG]), sb("o8", [P, nt, EPG])
        ek, rk, blk, over, rmod = [small(n, 2 * nt) for n in ("ek", "rk", "blk", "over", "rmod")]
        rki = sb("rki", [P, 2 * nt], I32)
        member, mprod = sb("member", [P, 2 * nt, NE]), sb("mprod", [P, 2 * nt, NE])
        msum, cum, rank = sb("msum", [P, nt, NE]), sb("cum", [P, nt + 1, NE]), sb("rank", [P, nt, NE])
        cnt, ov, oe0, oe1 = small("cnt", NE), small("ov", NE), small("oe0", NE), small("oe1", NE)
        cnti = sb("cnti", [P, NE], I32)
        a_oh = [sb(f"a_oh{j}", [P, P]) for j in range(2)]
        b_oh = [sb(f"b_oh{j}", [P, NBLK]) for j in range(2)]
        idx = sb("idx", [P, NBLK], I32)
        ovc = sb("ovc", [1, n_over, NE])
        ovf = sb("ovf", [1, n_over + 1])
        ovi = sb("ovi", [1, n_over + 1], I32)
        xg = [sb(f"xg{j}", [P, D]) for j in range(2)]
        xgT = [sb(f"xgT{j}", [P, KD, P]) for j in range(2)]
        hx, hT = xg, xgT
        act1 = [sb(f"act1{j}", [P, DE]) for j in range(2)]
        hm = [sb(f"hm{j}", [P, DE]) for j in range(2)]
        hmT = [sb(f"hmT{j}", [P, 2, P]) for j in range(2)]
        yo = [sb(f"yo{j}", [P, D]) for j in range(2)]
        ps, ident = c["ps"], c["ident"]
        dest, wgt = c["dest"], c["wgt"]

        w_sem = sem("weights_in")
        h_in = [sem(f"h_in{j}") for j in range(2)]
        hT_ps, hT_act, hT_dve, lgT_ps, lgT_rdy, lg_ps, lg_rdy = (
            sem("hT_ps"), sem("hT_act"), sem("hT_dve"), sem("lgT_ps"), sem("lgT_rdy"), sem("lg_ps"), sem("lg_rdy"))
        step, exp_in, exp_out, ms_rdy, rank_ps, oh_rdy, ix_ps, idx_rdy = (
            sem("step"), sem("exp_in"), sem("exp_out"), sem("ms_rdy"), sem("rank_ps"), sem("oh_rdy"), sem("ix_ps"),
            sem("idx_rdy"))
        w_in = [sem(f"w_in{j}") for j in range(W_RING)]
        g_in = [sem(f"g_in{j}") for j in range(2)]
        gT_ps, gT_rdy, up_ps, silu_rdy, hm_rdy, hmT_ps, hmT_rdy, dn_ps, y_ev = (
            sem("gT_ps"), sem("gT_rdy"), sem("up_ps"), sem("silu_rdy"), sem("hm_rdy"), sem("hmT_ps"),
            sem("hmT_rdy"), sem("dn_ps"), sem("y_ev"))
        y_out = [sem(f"y_out{j}") for j in range(2)]
        o_w, o_g = [sem(f"o_w{j}") for j in range(2)], [sem(f"o_g{j}") for j in range(2)]
        o_gT_ps, o_gT, o_up, o_silu, o_hm, o_hmT_ps, o_hmT, o_dn, o_ev, o_out = (
            sem("o_gT_ps"), sem("o_gT"), sem("o_up"), sem("o_silu"), sem("o_hm"),
            sem("o_hmT_ps"), sem("o_hmT"), sem("o_dn"), sem("o_ev"), sem("o_out"))
        main_done, over_stored = sem("main_done"), sem("over_stored")

        def expert_steps(eng, body, before_all, after_all):
            before_all()
            with eng.Fori(0, (NE - 2) // W_RING) as r:
                for e in range(1, W_RING + 1):
                    body(r * W_RING + e, e % 2, e % W_RING, r + e // W_RING)
            after_all()

        with nc.Block() as block:
            @block.sync
            def _(sp):
                def weights(e, wr):
                    if isinstance(e, int):
                        e_ = slice(e, e + 1)
                    else:
                        e_ = bass.ds(e, 1)
                    sp.dma_start(w13[wr][:, :, :], io["w13"][l, e_].rearrange("a p k n -> p (a k) n")).then_inc(
                        w_in[wr], 16)
                    sp.dma_start(w2[wr][:, :, :], io["w2"][l, e_].rearrange("a p k n -> p (a k) n")).then_inc(
                        w_in[wr], 16)

                for dst, src in ((w_route[:, :, :], io["w_route"][l]),
                                 (b_route[:, :], io["b_route"][l:l + 1, :].broadcast_to([P, 36])),
                                 (before[:, :], io["before"]), (ones[:, :], io["ones"]),
                                 (iota[:, :], io["iota"]), (token[:, :], io["token"])):
                    sp.dma_start(dst, src).then_inc(w_sem, 16)
                for s in range(2):
                    sp.dma_start(hx[s][:, :], io["h2"][s * P:(s + 1) * P, :]).then_inc(h_in[s], 16)
                with sp.Fori(0, nt // 2 - 1) as r:
                    for s in range(2):
                        sp.wait_ge(hT_ps, r * 2 + s + 1)
                        sp.dma_start(hx[s][:, :], io["h2"][bass.ds(r * 256 + (s + 2) * P, P), :]).then_inc(h_in[s], 16)
                for e in range(W_RING):
                    weights(e, e)
                rounds = NE // W_RING - 1
                with sp.Fori(0, rounds) as r:
                    for j in range(W_RING):
                        sp.wait_ge(dn_ps, r * W_RING + j + 1)
                        weights(r * W_RING + j + W_RING, j)
                for e in range((rounds + 1) * W_RING, NE):
                    sp.wait_ge(dn_ps, e - W_RING + 1)
                    weights(e, e % W_RING)

                def extra_weights(j, s):
                    w = OV_SLOT + s
                    e = sp.value_load(ovi[0:1, bass.ds(j, 1)], min_val=0, max_val=NE - 1)
                    sp.dma_start(w13[w][:, :, :], io["w13"][l, bass.ds(e, 1)].rearrange(
                        "a p k n -> p (a k) n")).then_inc(o_w[s], 16)
                    sp.dma_start(w2[w][:, :, :], io["w2"][l, bass.ds(e, 1)].rearrange(
                        "a p k n -> p (a k) n")).then_inc(o_w[s], 16)

                sp.wait_ge(idx_rdy, 1)
                n_ov = sp.value_load(ovi[0:1, n_over:n_over + 1], min_val=0, max_val=n_over)
                for s in range(2):
                    last_use = max(e for e in range(NE) if e % W_RING == OV_SLOT + s)
                    with sp.If(n_ov > s):
                        sp.wait_ge(dn_ps, last_use + 1)
                        extra_weights(s, s)
                with sp.Fori(0, PAIRS - 1) as r:
                    for s in range(2):
                        with sp.If(n_ov > r * 2 + s + 2):
                            sp.wait_ge(o_dn, r * 2 + s + 1)
                            extra_weights(r * 2 + s + 2, s)

            @block.gpsimd
            def _(pool):
                def gather(b, slot, signal):
                    pool.indirect_dma_start(out=slot[:, :], out_offset=None, in_=io["h2"][:, :],
                                            in_offset=bass.IndirectOffsetOnAxis(ap=idx[:, b:b + 1], axis=0)
                                            ).then_inc(signal, 16)

                pool.wait_ge(idx_rdy, 1)
                for e in range(NE):
                    if e >= 2:
                        pool.wait_ge(gT_ps, e - 1)
                    gather(e, xg[e % 2], g_in[e % 2])
                pool.wait_ge(gT_ps, NE)
                n_ov = pool.value_load(ovi[0:1, n_over:n_over + 1], min_val=0, max_val=n_over)
                for j in range(n_over):
                    with pool.If(n_ov > j):
                        if j >= 2:
                            pool.wait_ge(o_gT_ps, j - 1)
                        gather(NE + j, xg[j % 2], o_g[j % 2])

            @block.tensor
            def _(pe):
                pe.wait_ge(w_sem, 16 * 6)

                def transpose_h(t, s, r):
                    pe.wait_ge(h_in[s], r * 16 + 16)
                    pe.wait_ge(hT_act, t + 1)
                    pe.wait_ge(hT_dve, t + 1)
                    for k in range(KD):
                        tr = pe.transpose(ps[:, HT_AT[s] + k * P:HT_AT[s] + (k + 1) * P],
                                          hx[s][:, k * P:(k + 1) * P], ident[:, :])
                    tr.then_inc(hT_ps, 1)

                def logits(t, s):
                    pe.wait_ge(hT_act, t + 3)
                    pe.wait_ge(hT_dve, t + 3)
                    pe.wait_ge(lgT_rdy, t + 1)
                    for k in range(KD):
                        mm = pe.matmul(ps[0:NL, LT_AT[s]:LT_AT[s] + P], w_route[:, k, :], hT[s][:, k, :],
                                       start=(k == 0), stop=(k == KD - 1))
                    mm.then_inc(lgT_ps, 1)

                transpose_h(0, 0, 0)
                with pe.Fori(0, nt // 2 - 1) as r:
                    for s in range(2):
                        transpose_h(r * 2 + s + 1, 1 - s, r + s)
                        logits(r * 2 + s, s)
                transpose_h(nt - 1, 1, nt // 2 - 1)
                logits(nt - 2, 0)
                logits(nt - 1, 1)
                pe.wait_ge(lgT_rdy, nt + 2)
                for t in range(nt):
                    mm = pe.matmul(ps[:, LG_AT + t * NL:LG_AT + (t + 1) * NL], lgT[:, t * P:(t + 1) * P],
                                   ident[0:NL, 0:NL], start=True, stop=True)
                mm.then_inc(lg_ps, 1)
                pe.wait_ge(ms_rdy, 1)
                rk_ps = ps[:, RK_AT:RK_AT + nt * NE]
                pe.matmul(rk_ps, before[:, :], msum[:, :, :].rearrange("p t e -> p (t e)"), start=True, stop=False)
                pe.matmul(rk_ps, ones[:, :], cum[:, 0:nt, :].rearrange("p t e -> p (t e)"), start=False, stop=True)
                pe.matmul(ps[:, CNT_AT:CNT_AT + NE], ones[:, :], cum[:, nt, :], start=True,
                          stop=True).then_inc(rank_ps, 1)
                for n in range(2 * nt):
                    pe.wait_ge(oh_rdy, n + 1)
                    pe.matmul(ps[:, IX_AT:IX_AT + NBLK], a_oh[n % 2][:, :], b_oh[n % 2][:, :], start=(n == 0),
                              stop=(n == 2 * nt - 1)).then_inc(ix_ps, 1)

                def gathered(xs, xTs, sig_in, value, sig_out):
                    pe.wait_ge(sig_in, value)
                    for k in range(KD):
                        tr = pe.transpose(ps[:, GT_AT + k * P:GT_AT + (k + 1) * P], xs[:, k * P:(k + 1) * P],
                                          ident[:, :])
                    tr.then_inc(sig_out, 1)

                def up(at, xTs, w, sig):
                    for k in range(KD):
                        mm = pe.matmul(ps[:, at:at + 512], xTs[:, k, :], w[:, k, :], start=(k == 0),
                                       stop=(k == KD - 1))
                    mm.then_inc(sig, 1)

                def hidden(h, sig):
                    for k in range(2):
                        tr = pe.transpose(ps[:, HM_AT + k * P:HM_AT + (k + 1) * P], h[:, k * P:(k + 1) * P],
                                          ident[:, :])
                    tr.then_inc(sig, 1)

                def down(hT_, w, sig):
                    for n in range(2):
                        for k in range(2):
                            mm = pe.matmul(ps[:, DN_AT + n * 512:DN_AT + (n + 1) * 512], hT_[:, k, :],
                                           w[:, k, n * 512:(n + 1) * 512], start=(k == 0), stop=(k == 1))
                    mm.then_inc(sig, 1)

                def step_up(e, s, wr, wn):
                    pe.wait_ge(w_in[wr], wn * 32 + 32)
                    pe.wait_ge(gT_rdy, e * 2 + 2)
                    pe.wait_ge(hm_rdy, e + 1)
                    up(UP_AT[s], xgT[s], w13[wr], up_ps)

                def step_down(e, s, wr):
                    pe.wait_ge(hmT_rdy, e + 1)
                    pe.wait_ge(y_ev, e * 2 + 2)
                    down(hmT[s], w2[wr], dn_ps)

                def step_hidden(e, s):
                    pe.wait_ge(hm_rdy, e + 3)
                    hidden(hm[s], hmT_ps)

                def first():
                    gathered(xg[0], xgT[0], g_in[0], 16, gT_ps)
                    step_up(0, 0, 0, 0)
                    gathered(xg[1], xgT[1], g_in[1], 16, gT_ps)
                    step_hidden(0, 0)

                def body(e, s, wr, wn):
                    step_up(e, s, wr, wn)
                    gathered(xg[1 - s], xgT[1 - s], g_in[1 - s],
                             (e - s) * 8 + (32 if s else 16), gT_ps)
                    step_down(e - 1, 1 - s, (wr - 1) % W_RING)
                    step_hidden(e, s)

                def last():
                    e = NE - 1
                    step_up(e, 1, e % W_RING, e // W_RING)
                    step_down(e - 1, 0, (e - 1) % W_RING)
                    step_hidden(e, 1)
                    step_down(e, 1, e % W_RING)

                expert_steps(pe, body, first, last)

                pe.wait_ge(main_done, 1)
                n_ov = pe.value_load(ovi[0:1, n_over:n_over + 1], min_val=0, max_val=n_over)
                with pe.Fori(0, PAIRS) as r:
                    for s in range(2):
                        j = r * 2 + s
                        with pe.If(n_ov > j):
                            gathered(xg[s], xgT[0], o_g[s], r * 16 + 16, o_gT_ps)
                            pe.wait_ge(o_w[s], r * 32 + 32)
                            pe.wait_ge(o_gT, j * 2 + 2)
                            up(UP_AT[0], xgT[0], w13[OV_SLOT + s], o_up)
                            pe.wait_ge(o_hm, j + 1)
                            hidden(hm[0], o_hmT_ps)
                            pe.wait_ge(o_hmT, j + 1)
                            down(hmT[0], w2[OV_SLOT + s], o_dn)

            @block.scalar
            def _(act):
                act.sem_inc(lgT_rdy, 2)
                act.sem_inc(hT_act, 2)

                def read_h(t, s):
                    act.wait_ge(hT_ps, t + 1)
                    act.copy(hT[s][:, 0:4, :], ps[:, HT_AT[s]:HT_AT[s] + 512].rearrange(
                        "p (k n) -> p k n", k=4)).then_inc(hT_act, 1)

                def read_logits(t, s):
                    act.wait_ge(lgT_ps, t + 1)
                    act.copy(lgT[:, bass.ds(t * P, P)], ps[0:NL, LT_AT[s]:LT_AT[s] + P]).then_inc(lgT_rdy, 1)

                read_h(0, 0)
                read_h(1, 1)
                with act.Fori(0, nt // 2 - 1) as r:
                    for s in range(2):
                        read_logits(r * 2 + s, s)
                        read_h(r * 2 + s + 2, s)
                for s in range(2):
                    read_logits(nt - 2 + s, s)
                act.wait_ge(exp_in, 1)
                act.activation(g4[:, :, :], g4[:, :, :], ACT.Exp).then_inc(exp_out, 1)
                act.wait_ge(exp_in, 2)
                act.activation(e1[:, :], e1[:, :], ACT.Exp).then_inc(exp_out, 1)

                def rows(xTs, sig_in, value, sig_out):
                    act.wait_ge(sig_in, value)
                    act.copy(xTs[:, 0:4, :], ps[:, GT_AT:GT_AT + 512].rearrange(
                        "p (k n) -> p k n", k=4)).then_inc(sig_out, 1)

                def silu(e, s):
                    act.wait_ge(up_ps, e + 1)
                    act.activation(act1[s][:, :], ps[:, UP_AT[s]:UP_AT[s] + DE], ACT.Silu).then_inc(silu_rdy, 1)

                def output(e, s, n):
                    act.wait_ge(dn_ps, e + 1)
                    act.wait_ge(y_out[s], n * 16 + 16)
                    act.copy(yo[s][:, 0:512], ps[:, DN_AT:DN_AT + 512]).then_inc(y_ev, 1)
                    act.wait_ge(y_ev, e * 2 + 4)
                    rows_out = io["ys"][e * P:(e + 1) * P, :] if isinstance(e, int) else io["ys"][bass.ds(e * P, P), :]
                    act.dma_start(rows_out, yo[s][:, :]).then_inc(y_out[s], 16)

                def first():
                    for s in range(2):
                        act.sem_inc(y_out[s], 16)
                    rows(xgT[0], gT_ps, 1, gT_rdy)
                    silu(0, 0)
                    rows(xgT[1], gT_ps, 2, gT_rdy)

                def body(e, s, wr, wn):
                    silu(e, s)
                    rows(xgT[1 - s], gT_ps, e + 2, gT_rdy)
                    act.wait_ge(dn_ps, e)
                    p = 1 - s
                    act.wait_ge(y_out[p], (e - 1 - p) * 8 + 16)
                    act.copy(yo[p][:, 0:512], ps[:, DN_AT:DN_AT + 512]).then_inc(y_ev, 1)
                    act.wait_ge(y_ev, e * 2 + 2)
                    act.dma_start(io["ys"][bass.ds(e * P - P, P), :], yo[p][:, :]).then_inc(y_out[p], 16)

                def last():
                    e = NE - 1
                    silu(e, 1)
                    output(e - 1, 0, (e - 1) // 2)
                    output(e, 1, e // 2)
                    for s in range(2):
                        act.wait_ge(y_out[s], 16 + 16 * (NE // 2))
                    act.sem_inc(main_done, 1)

                expert_steps(act, body, first, last)
                act.sem_inc(o_out, 16)
                n_ov = act.value_load(ovi[0:1, n_over:n_over + 1], min_val=0, max_val=n_over)
                with act.Fori(0, n_over) as j:
                    with act.If(n_ov > j):
                        rows(xgT[0], o_gT_ps, j + 1, o_gT)
                        act.wait_ge(o_up, j + 1)
                        act.activation(act1[0][:, :], ps[:, UP_AT[0]:UP_AT[0] + DE], ACT.Silu).then_inc(o_silu, 1)
                        act.wait_ge(o_dn, j + 1)
                        act.wait_ge(o_out, j * 16 + 16)
                        act.copy(yo[0][:, 0:512], ps[:, DN_AT:DN_AT + 512]).then_inc(o_ev, 1)
                        act.wait_ge(o_ev, j * 2 + 2)
                        act.dma_start(io["ys"][bass.ds(j * P + NE * P, P), :], yo[0][:, :]).then_inc(o_out, 16)
                act.wait_ge(o_out, n_ov * 16 + 16)
                act.sem_inc(over_stored, 1)
                act.wait_ge(over_stored, 1)

            @block.vector
            def _(dve):
                dve.wait_ge(w_sem, 16 * 6)

                dve.sem_inc(hT_dve, 2)

                def read_h(t, s):
                    dve.wait_ge(hT_ps, t + 1)
                    dve.tensor_copy(hT[s][:, 4:8, :], ps[:, HT_AT[s] + 512:HT_AT[s] + 1024].rearrange(
                        "p (k n) -> p k n", k=4)).then_inc(hT_dve, 1)

                read_h(0, 0)
                read_h(1, 1)
                with dve.Fori(0, nt // 2 - 1) as r:
                    for s in range(2):
                        dve.wait_ge(lgT_ps, r * 2 + s + 1)
                        read_h(r * 2 + s + 2, s)
                dve.wait_ge(lg_ps, 1)
                dve.tensor_tensor(lg[:, :, :], ps[:, LG_AT:LG_AT + nt * NL].rearrange("p (t n) -> p t n", n=NL),
                                  b_route[:, :].unsqueeze(1).broadcast_to([P, nt, NL]), ALU.add).then_inc(lg_rdy, 1)
                dve.wait_ge(lg_rdy, 1)
                st = Steps(dve, step, 0)
                st.begin(0)
                V = dve

                def tt(out, a, b, op):
                    st.after(V.tensor_tensor(out, a, b, op))

                def ts(out, a, x, op, x2=None, op2=None):
                    st.after(V.tensor_scalar(out, a, x, x2, op, op2) if op2 is not None
                             else V.tensor_scalar(out, a, x, None, op))

                def red(out, a, op):
                    st.after(V.tensor_reduce(out, a, AX_X, op))

                def over_last(v, shape):
                    return v.unsqueeze(len(shape) - 1).broadcast_to(shape)

                def count_up(n, w):
                    return iota[:, 0:w].unsqueeze(1).broadcast_to([P, n, w])

                def first_index(out, values, top, tmp, w):
                    tt(tmp, values, over_last(top, [P, nt, w]), ALU.is_equal)
                    st.after(V.scalar_tensor_tensor(tmp, tmp, -64.0, count_up(nt, w), ALU.mult, ALU.add))
                    red(out, tmp, ALU.min)
                    ts(out, out, 64.0, ALU.add)

                lgg = lg[:, :, 0:NG]
                red(gmax[:, :], lgg, ALU.max)
                first_index(gi[:, :], lgg, gmax[:, :], og[:, :, :], NG)
                V.tensor_tensor(g4[:, :, :], lgg, over_last(gmax[:, :], [P, nt, NG]), ALU.subtract).then_inc(exp_in, 1)
                tt(og[:, :, :], count_up(nt, NG), over_last(gi[:, :], [P, nt, NG]), ALU.is_equal)
                V.wait_ge(exp_out, 1)
                red(gsum[:, :], g4[:, :, :], ALU.add)
                st.after(V.reciprocal(gsum[:, :], gsum[:, :]))
                tt(s84[:, :, :, :], lg[:, :, NG:36].rearrange("p t (g e) -> p t e g", g=NG),
                   og[:, :, :].unsqueeze(2).broadcast_to([P, nt, EPG, NG]), ALU.mult)
                red(s8[:, :, :], s84[:, :, :, :], ALU.add)
                red(m0[:, :], s8[:, :, :], ALU.max)
                first_index(i0[:, :], s8[:, :, :], m0[:, :], o8[:, :, :], EPG)
                tt(o8[:, :, :], count_up(nt, EPG), over_last(i0[:, :], [P, nt, EPG]), ALU.is_equal)
                st.after(V.scalar_tensor_tensor(s8[:, :, :], o8[:, :, :], -BIG, s8[:, :, :], ALU.mult, ALU.add))
                red(m1[:, :], s8[:, :, :], ALU.max)
                first_index(i1[:, :], s8[:, :, :], m1[:, :], o8[:, :, :], EPG)
                V.tensor_tensor(e1[:, :], m1[:, :], m0[:, :], ALU.subtract).then_inc(exp_in, 1)
                V.wait_ge(exp_out, 2)
                ts(m0[:, :], e1[:, :], 1.0, ALU.add)
                st.after(V.reciprocal(m0[:, :], m0[:, :]))
                tt(wgt[:, 0:nt, 0], m0[:, :], gsum[:, :], ALU.mult)
                tt(wgt[:, 0:nt, 1], wgt[:, 0:nt, 0], e1[:, :], ALU.mult)
                ek2 = ek[:, :].rearrange("p (t k) -> p t k", k=2)
                for k, ik in enumerate((i0, i1)):
                    st.after(V.scalar_tensor_tensor(ek2[:, :, k], gi[:, :], float(EPG), ik[:, :], ALU.mult, ALU.add))
                tt(member[:, :, :], count_up(2 * nt, NE), over_last(ek[:, :], [P, 2 * nt, NE]), ALU.is_equal)
                mem4 = member[:, :, :].rearrange("p (t k) e -> p t k e", k=2)
                tt(msum[:, :, :], mem4[:, :, 0, :], mem4[:, :, 1, :], ALU.add)
                st.after(V.memset(cum[:, 0, :], 0.0))
                for t in range(nt):
                    tt(cum[:, t + 1, :], cum[:, t, :], msum[:, t, :], ALU.add)
                V.sem_inc(ms_rdy, 1)
                V.wait_ge(rank_ps, 1)
                st.after(V.tensor_copy(rank[:, :, :], ps[:, RK_AT:RK_AT + nt * NE].rearrange("p (t e) -> p t e", e=NE)))
                ts(cnt[:, :], ps[:, CNT_AT:CNT_AT + NE], float(P - 1), ALU.add)
                mp4 = mprod[:, :, :].rearrange("p (t k) e -> p t k e", k=2)
                tt(mp4, mem4, rank[:, :, :].unsqueeze(2).broadcast_to([P, nt, 2, NE]), ALU.mult)
                red(rk[:, :], mprod[:, :, :], ALU.add)
                st.after(V.tensor_copy(rki[:, :], rk[:, :]))
                ts(rki[:, :], rki[:, :], 7, ALU.arith_shift_right)
                st.after(V.tensor_copy(over[:, :], rki[:, :]))
                st.after(V.scalar_tensor_tensor(rmod[:, :], over[:, :], -float(P), rk[:, :], ALU.mult, ALU.add))
                st.after(V.tensor_copy(cnti[:, :], cnt[:, :]))
                ts(cnti[:, :], cnti[:, :], 7, ALU.arith_shift_right)
                st.after(V.tensor_copy(ov[:, :], cnti[:, :]))
                ts(ov[:, :], ov[:, :], -1.0, ALU.add, 0.0, ALU.max)
                src, dst = ov, oe0
                for sh in (1, 2, 4, 8, 16):
                    st.after(V.tensor_copy(dst[:, 0:sh], src[:, 0:sh]))
                    tt(dst[:, sh:NE], src[:, sh:NE], src[:, 0:NE - sh], ALU.add)
                    src, dst = dst, (oe1 if dst is oe0 else oe0)
                ovend, ovbase = src, dst
                tt(ovbase[:, :], ovend[:, :], ov[:, :], ALU.subtract)
                tt(mprod[:, :, :], member[:, :, :], ovbase[:, :].unsqueeze(1).broadcast_to([P, 2 * nt, NE]), ALU.mult)
                red(blk[:, :], mprod[:, :, :], ALU.add)
                tt(blk[:, :], blk[:, :], over[:, :], ALU.add)
                st.after(V.scalar_tensor_tensor(blk[:, :], blk[:, :], float(NE - 1), ek[:, :], ALU.add, ALU.subtract))
                ts(over[:, :], over[:, :], 1.0, ALU.min)
                tt(blk[:, :], blk[:, :], over[:, :], ALU.mult)
                tt(blk[:, :], blk[:, :], ek[:, :], ALU.add)
                st.after(V.scalar_tensor_tensor(dest[:, 0:2 * nt], blk[:, :], float(P), rmod[:, :], ALU.mult, ALU.add))
                oc = ovc[:, :, :]
                tt(oc, iota[0:1, 0:n_over].unsqueeze(2).broadcast_to([1, n_over, NE]),
                   ovend[0:1, :].unsqueeze(1).broadcast_to([1, n_over, NE]), ALU.is_ge)
                red(ovf[:, 0:n_over], oc, ALU.add)
                ts(ovf[:, 0:n_over], ovf[:, 0:n_over], float(NE - 1), ALU.min)
                st.after(V.tensor_copy(ovf[:, n_over:n_over + 1], ovend[0:1, NE - 1:NE]))
                st.after(V.tensor_copy(ovi[:, :], ovf[:, :]))
                for n in range(2 * nt):
                    if n >= 2:
                        V.wait_ge(ix_ps, n - 1)
                    V.tensor_scalar(a_oh[n % 2][:, :], iota[:, :], rmod[:, n:n + 1], None, ALU.is_equal)
                    V.tensor_scalar(b_oh[n % 2][:, :], iota[:, 0:NBLK], blk[:, n:n + 1], token[:, n // 2:n // 2 + 1],
                                    ALU.is_equal, ALU.mult).then_inc(oh_rdy, 1)
                V.wait_ge(ix_ps, 2 * nt)
                V.tensor_copy(idx[:, :], ps[:, IX_AT:IX_AT + NBLK]).then_inc(idx_rdy, 1)
                V.wait_ge(idx_rdy, 1)

                def rows(xTs, sig_in, value, sig_out):
                    dve.wait_ge(sig_in, value)
                    dve.tensor_copy(xTs[:, 4:8, :], ps[:, GT_AT + 512:GT_AT + 1024].rearrange(
                        "p (k n) -> p k n", k=4)).then_inc(sig_out, 1)

                def gated(e, s):
                    dve.wait_ge(silu_rdy, e + 1)
                    dve.tensor_tensor(hm[s][:, :], act1[s][:, :], ps[:, UP_AT[s] + DE:UP_AT[s] + 2 * DE],
                                      ALU.mult).then_inc(hm_rdy, 1)

                def hidden(e, s):
                    dve.wait_ge(hmT_ps, e + 1)
                    dve.tensor_copy(hmT[s][:, :, :], ps[:, HM_AT:HM_AT + 256].rearrange(
                        "p (k n) -> p k n", k=2)).then_inc(hmT_rdy, 1)

                def output(e, p):
                    dve.wait_ge(dn_ps, e + 1)
                    dve.wait_ge(y_out[p], (e - p) * 8 + 16)
                    dve.tensor_copy(yo[p][:, 512:1024], ps[:, DN_AT + 512:DN_AT + 1024]).then_inc(y_ev, 1)

                def first():
                    dve.sem_inc(hm_rdy, 2)
                    dve.sem_inc(y_ev, 2)
                    rows(xgT[0], gT_ps, 1, gT_rdy)
                    gated(0, 0)
                    rows(xgT[1], gT_ps, 2, gT_rdy)
                    hidden(0, 0)

                def body(e, s, wr, wn):
                    gated(e, s)
                    rows(xgT[1 - s], gT_ps, e + 2, gT_rdy)
                    output(e - 1, 1 - s)
                    hidden(e, s)

                def last():
                    e = NE - 1
                    gated(e, 1)
                    output(e - 1, 0)
                    hidden(e, 1)
                    output(e, 1)

                expert_steps(dve, body, first, last)
                dve.wait_ge(main_done, 1)
                n_ov = dve.value_load(ovi[0:1, n_over:n_over + 1], min_val=0, max_val=n_over)
                with dve.Fori(0, n_over) as j:
                    with dve.If(n_ov > j):
                        rows(xgT[0], o_gT_ps, j + 1, o_gT)
                        dve.wait_ge(o_silu, j + 1)
                        dve.tensor_tensor(hm[0][:, :], act1[0][:, :], ps[:, UP_AT[0] + DE:UP_AT[0] + 2 * DE],
                                          ALU.mult).then_inc(o_hm, 1)
                        dve.wait_ge(o_hmT_ps, j + 1)
                        dve.tensor_copy(hmT[0][:, :, :], ps[:, HM_AT:HM_AT + 256].rearrange(
                            "p (k n) -> p k n", k=2)).then_inc(o_hmT, 1)
                        dve.wait_ge(o_dn, j + 1)
                        dve.wait_ge(o_out, j * 16 + 16)
                        dve.tensor_copy(yo[0][:, 512:1024], ps[:, DN_AT + 512:DN_AT + 1024]).then_inc(o_ev, 1)


def combine(nc, l, io, c, keep, out):
    nt = NT if l < DEPTH - 1 else NT_LAT
    STEPS = 5
    ctx = ExitStack()
    sb = lambda n, s, d=F32: ctx.enter_context(nc.sbuf_tensor(f"cb_{n}_{l}", s, d))
    sem = phase_semaphores(nc, ctx, lambda n: f"cb_{n}_{l}")
    RING = nt
    with ctx:
        m = Modulation(l + 1, io, c, keep, sb, sem) if l < DEPTH - 1 else None
        yy = sb("yy", [P, RING, 2, D])
        xin = [sb(f"x{j}", [P, D]) for j in range(2)]
        gate2 = sb("gate2", [P, 2, D])
        ln_g, ln_b = sb("ln_g", [P, D]), sb("ln_b", [P, D])
        f = [sb(f"f{j}", [P, D]) for j in range(2)]
        z = sb("z", [P, D])
        xo = [sb(f"xo{j}", [P, D]) for j in range(2)]
        stats, mv, rstd, tick = sb("stats", [P, 2, 6]), sb("mv", [P, 2]), sb("rstd", [P, 1]), sb("tick", [P, 1])
        neg_half = sb("neg_half", [P, 1])
        dest, wgt = c["dest"], c["wgt"]
        w_sem, half_rdy = sem("w_in"), sem("half_rdy")
        x_in = [sem(f"x_in{j}") for j in range(2)]
        y_in = [sem(f"y_in{t}") for t in range(nt)]
        o_out = [sem(f"o_out{j}") for j in range(2)]
        first_rdy, step, var_rdy, rstd_rdy, xo_rdy, gained, normed = (
            sem("first"), sem("step"), sem("var_rdy"), sem("rstd_rdy"), sem("xo_rdy"), sem("gained"), sem("normed"))

        def store_at(t):
            return out[0, bass.ds(t * P, P), :] if l == DEPTH - 1 else io["x_mid"][bass.ds(t * P, P), :]

        with nc.Block() as block:
            @block.sync
            def _(sp):
                def load(t, s):
                    sp.dma_start(xin[s][:, :], io["x_post"][bass.ds(t * P, P), :]).then_inc(x_in[s], 16)

                def store(t, s):
                    sp.wait_ge(xo_rdy, t + 1)
                    sp.dma_start(store_at(t), xo[s][:, :]).then_inc(o_out[s], 16)

                for s in range(2):
                    sp.sem_inc(o_out[s], 16)
                    load(s, s)
                for s in range(2):
                    sp.dma_start(gate2[:, s, :], io["mod"][l, s:s + 1, 5 * D:6 * D].broadcast_to([P, D])).then_inc(w_sem, 16)
                sp.dma_start(ln_g[:, :], io["ln"][l, 2:3, :].broadcast_to([P, D])).then_inc(w_sem, 16)
                sp.dma_start(ln_b[:, :], io["ln"][l, 3:4, :].broadcast_to([P, D])).then_inc(w_sem, 16)
                if m:
                    m.load_small(sp)
                    for t in range(m.RING):
                        m.load_chunk(sp, 0, t)
                for t in range(nt):
                    store(t, t % 2)
                    if t + 2 < nt:
                        load(t + 2, t % 2)
                    if m and t + m.RING < m.CHUNKS:
                        m.load_chunk(sp, (t + m.RING) // m.RING, t % m.RING)
                if m:
                    m.store(sp)
                for s in range(2):
                    sp.wait_ge(o_out[s], 16 + 16 * (nt // 2))

            @block.gpsimd
            def _(pool):
                pool.memset(neg_half[:, :], -0.5).then_inc(half_rdy, 1)
                pool.wait_ge(half_rdy, 1)
                for t in range(nt):
                    for k in range(2):
                        pool.indirect_dma_start(
                            out=yy[:, t, k, :], out_offset=None, in_=io["ys"][:, :],
                            in_offset=bass.IndirectOffsetOnAxis(ap=dest[:, 2 * t + k:2 * t + k + 1], axis=0)
                        ).then_inc(y_in[t], 16)
                pool.wait_ge(w_sem, 64)
                for t in range(nt):
                    pool.wait_ge(var_rdy, t + 1)
                    pool.tensor_tensor(rstd[:, :], mv[:, 1:2], neg_half[:, :], ALU.pow).then_inc(rstd_rdy, 1)
                    pool.wait_ge(normed, t + 1)
                    xs = xo[t % 2][:, :]
                    pool.tensor_tensor(xs, xs, ln_g[:, :], ALU.mult).then_inc(gained, 1)
                    pool.wait_ge(gained, t + 1)
                    pool.tensor_tensor(xs, xs, ln_b[:, :], ALU.add).then_inc(xo_rdy, 1)

            @block.scalar
            def _(act):
                if m:
                    m.exponential(act)
                for t in range(nt):
                    act.wait_ge(y_in[t], 32)
                    if t >= 2:
                        act.wait_ge(step, (t - 2) * STEPS + 2)
                    act.activation(f[t % 2][:, :], yy[:, t, 0, :], ACT.Copy,
                                   scale=wgt[:, t, 0:1]).then_inc(first_rdy, 1)

            @block.vector
            def _(dve):
                if m:
                    m.silu(dve)
                dve.wait_ge(w_sem, 64)
                st = Steps(dve, step, STEPS)

                def body(t, s, stream):
                    st.begin(t)
                    dve.wait_ge(first_rdy, t + 1)
                    at = bass.ds(t, 1)
                    st.after(dve.scalar_tensor_tensor(f[s][:, :].unsqueeze(1), yy[:, at, 1, :], wgt[:, at, 1],
                                                      f[s][:, :].unsqueeze(1), ALU.mult, ALU.add))
                    st.after(dve.tensor_tensor(z[:, :], f[s][:, :], gate2[:, stream, :], ALU.mult))
                    dve.wait_ge(x_in[s], 16 * (t // 2) + 16)
                    st.after(dve.scalar_tensor_tensor(z[:, :], xin[s][:, :], ALPHA, z[:, :], ALU.mult, ALU.add))
                    for j in range(2):
                        op = dve.bn_stats(stats[:, j, :], z[:, j * 512:(j + 1) * 512])
                    st.after(op)
                    st.after(dve.bn_aggr(mv[:, :], stats[:, :, :]))
                    dve.tensor_scalar(mv[:, 1:2], mv[:, 1:2], EPS, None, ALU.add).then_inc(var_rdy, 1)
                    dve.wait_ge(rstd_rdy, t + 1)
                    dve.wait_ge(o_out[s], 16 * (t // 2) + 16)
                    dve.tensor_scalar(xo[s][:, :], z[:, :], mv[:, 0:1], rstd[:, :], ALU.subtract,
                                      ALU.mult).then_inc(normed, 1)
                    dve.wait_ge(normed, t + 1)
                    st.end()

                for t in range(nt):
                    body(t, t % 2, 0 if t < NT_LAT else 1)
                    if m:
                        m.read_chunk(dve, t // m.RING, t % m.RING)
                if m:
                    for n in range(nt, m.CHUNKS):
                        m.read_chunk(dve, n // m.RING, n % m.RING)
                    m.read_columns(dve)

            if m:
                @block.tensor
                def _(pe):
                    m.products(pe)


def build(nc, io, out):
    ctx = ExitStack()
    with ctx:
        sb = lambda n, s, d=F32: ctx.enter_context(nc.sbuf_tensor(n, s, d))
        c = {"ps": ctx.enter_context(nc.psum_tensor("ps", [P, 4096], F32)),
             "ident": sb("ident", [P, P]),
             "dest": sb("dest", [P, 2 * NT], I32), "wgt": sb("wgt", [P, NT, 2])}
        keep = {"shift1": sb("shift1", [P, KD, 2]), "scale1": sb("scale1", [P, KD, 2])}
        const_in = ctx.enter_context(nc.semaphore("const_in"))
        with nc.Block() as block:
            @block.sync
            def _(sp):
                sp.dma_start(c["ident"][:, :], io["ident"]).then_inc(const_in, 16)
                sp.wait_ge(const_in, 16)
        first_modulation(nc, 0, io, c, keep)
        for l in range(DEPTH):
            with ExitStack() as layer:
                kvt = lambda n, s: layer.enter_context(nc.sbuf_tensor(f"{n}_{l}", s, F32))
                kv = {"km": kvt("km", [MLA_QK, MLA_H, T]), "kd": kvt("kd", [P, 2, T]), "kg": kvt("kg", [P, T]),
                      "vm": kvt("vm", [P, NT, 256]), "vd": kvt("vd", [P, NT, 256]), "vg": kvt("vg", [P, NT, 128])}
                project(nc, l, io, c, keep, kv)
                attend(nc, l, io, c, kv, 0)
                if l < DEPTH - 1:
                    attend(nc, l, io, c, kv, 1)
            experts(nc, l, io, c)
            combine(nc, l, io, c, keep, out)


def host_arrays(g):
    L, K = DEPTH, KD
    arr = {}
    arr["x_in"] = np.concatenate([g["x"][0], g["ctx"][0]], axis=0)
    arr["c_cols"] = np.stack([g["c"][0], g["c_ctx"]]).reshape(2, K, P).transpose(2, 1, 0)
    arr["w_ada"] = g["w_ada"].reshape(L, K, P, 12, 512).transpose(0, 3, 2, 1, 4)
    arr["b_ada"] = g["b_ada"]
    conv, mla, dif, gqa = 0, 768, 1184, 1952
    cols = [(conv + 256, 256), (conv + 512, 256), (conv, 256), (mla, 256), (dif, 512), (gqa, 384), (mla + 256, 128),
            (dif + 512, 256), (gqa + 384, 128), (mla + 384, 32)]
    order = np.concatenate([np.arange(a, a + n) for a, n in cols])
    arr["w_in"] = g["w_in"][:, :, order].reshape(L, K, P, D_IN).transpose(0, 2, 1, 3)
    uq = g["mla_w_uq"].reshape(L, 2, P, MLA_H, 64)
    qr = g["mla_w_qr"].reshape(L, 2, P, MLA_H, 32)
    arr["w_q"] = np.concatenate([uq, qr], axis=4).reshape(L, 2, P, 384).transpose(0, 2, 1, 3)
    arr["w_kv"] = np.concatenate([g["mla_w_uk"], g["mla_w_uv"]], axis=2)
    arr["lat_gain"] = np.concatenate([g["mla_q_norm"].reshape(L, 2, P), g["mla_kv_norm"].reshape(L, 1, P)],
                                     axis=1).transpose(0, 2, 1)
    arr["qk_gain"] = np.concatenate([g["gqa_q_norm"]] * 4 + [g["gqa_k_norm"]] * 2, axis=1)
    arr["w_out"] = g["w_out"].reshape(L, K, P, D).transpose(0, 2, 1, 3)
    arr["conv_w"] = g["conv_w"].reshape(L, 3 * CONV)
    arr["lambda"] = g["diff_lambda"].reshape(L, 128)
    arr["subln"] = g["diff_subln"]
    arr["ln"] = np.stack([g["ln1_g"], g["ln1_b"], g["ln2_g"], g["ln2_b"]], axis=1)
    arr["w_route"] = np.concatenate([g["moe_w_group"], g["moe_w_sub"]], axis=2).reshape(L, K, P, 36).transpose(0, 2, 1, 3)
    arr["b_route"] = np.concatenate([g["moe_b_group"], g["moe_b_sub"]], axis=1)
    w13 = np.concatenate([g["moe_w1"], g["moe_w3"]], axis=3)
    arr["w13"] = w13.reshape(L, NE, K, P, 2 * DE).transpose(0, 1, 3, 2, 4)
    arr["w2"] = g["moe_w2"].reshape(L, NE, 2, P, D).transpose(0, 1, 3, 2, 4)
    arr["ident"] = np.eye(P, dtype=np.float32)
    arr["before"] = np.triu(np.ones((P, P), np.float32), 1)
    arr["ones"] = np.ones((P, P), np.float32)
    arr["iota"] = np.broadcast_to(np.arange(P, dtype=np.float32), (P, P))
    arr["token"] = (np.arange(NT)[None, :] * P + np.arange(P)[:, None]).astype(np.float32)
    tok = np.arange(LAT)
    rope = np.zeros((T, 192), np.float32)
    rope[:, 0:32] = 1.0
    rope[:, 64:128] = 1.0
    for width, at in ((32, 0), (64, 64)):
        q = width // 4
        freqs = np.float32(THETA) ** (-np.arange(q, dtype=np.float32) / np.float32(q))
        for axis, pos in enumerate((tok // GRID_W, tok % GRID_W)):
            ang = pos.astype(np.float32)[:, None] * freqs.astype(np.float32)
            for half in range(2):
                o = at + axis * 2 * q + half * q
                rope[:LAT, o:o + q] = np.cos(ang)
                rope[:LAT, o + width:o + width + q] = np.sin(ang) * (1.0 if half else -1.0)
    arr["rope"] = rope.reshape(NT, P, 192).transpose(1, 0, 2)
    return arr


def kernel(**inputs):
    import concourse.bacc as bacc
    from concourse.bass_utils import run_bass_kernel_spmd as run

    nc = bacc.Bacc("TRN2", target_bir_lowering=False, num_devices=1)
    io, arrays = {}, {}
    for name, a in host_arrays({k: np.asarray(v) for k, v in inputs.items()}).items():
        a = np.ascontiguousarray(a)
        arrays[f"in_{name}"] = a
        io[name] = nc.dram_tensor(f"in_{name}", a.shape, mybir.dt.from_np(a.dtype), kind="ExternalInput").ap()
    for name, shape in (("mod", (DEPTH, 2, 6 * D)), ("qrow", (T, Q_W)), ("zc", (ZROWS, CONV)), ("x_mid", (T, D)),
                        ("x_post", (T, D)), ("h2", (T, D)), ("ys", (YROWS, D))):
        io[name] = nc.dram_tensor(f"{name}_scratch", shape, F32, kind="Internal").ap()
    out = nc.dram_tensor("out_x", (1, LAT, D), F32, kind="ExternalOutput").ap()
    build(nc, io, out)
    r = run(nc, [arrays], core_ids=[0])
    return r.results[0]["out_x"]
```
